# Optimizing a Trainium2 kernel written in Bass

```python
import math
import jax, jax.numpy as jnp
from jax import lax
import numpy as np

D_MODEL = 1024
BATCH = 1
SEQ = 1024
DEPTH = 1

HEAD_DIM = 64
D_ATTN = D_MODEL // 2
N_HEADS = D_ATTN // HEAD_DIM
DILATED_GROUPS = ((128, 1), (512, 4), (2048, 16))
N_GROUPS = len(DILATED_GROUPS)
N_QKV = 3 * N_GROUPS * N_HEADS * HEAD_DIM
D_HYENA = D_MODEL // 2
HYENA_ORDER = 2
FILTER_EMB = 33
FILTER_WIDTH = 64
DECAY_TARGET = 1e-2
FAST_DECAY_PCT = 0.3
SLOW_DECAY_PCT = 1.5
N_IN = N_QKV + D_ATTN + 3 * D_HYENA + D_HYENA + 2 * D_MODEL
DEEPNORM_ALPHA = (2 * DEPTH) ** 0.25
DEEPNORM_BETA = (8 * DEPTH) ** -0.25
LN_EPS = 1e-5


def _layer_norm(x):
    xf = x.astype(jnp.float32)
    mu = jnp.mean(xf, axis=-1, keepdims=True)
    var = jnp.mean(jnp.square(xf - mu), axis=-1, keepdims=True)
    return (xf - mu) * lax.rsqrt(var + LN_EPS)

def _alibi_slopes(n_heads):
    return jnp.asarray(2.0 ** (-8.0 * (np.arange(n_heads) + 1) / n_heads), dtype=jnp.float32)

def dilated_window_attention(q, k, v, slopes, dilation, radius):
    B, S, H, E = q.shape
    L = S // dilation
    nb = -(-L // radius)
    Lp = nb * radius

    def by_residue(a):
        return a.reshape(B, L, dilation, H, E).transpose(0, 2, 1, 3, 4)

    qs, ks, vs = by_residue(q), by_residue(k), by_residue(v)
    qb = jnp.pad(qs, ((0, 0), (0, 0), (0, Lp - L), (0, 0), (0, 0))).reshape(B, dilation, nb, radius, H, E)

    def windows(a):
        ap = jnp.pad(a, ((0, 0), (0, 0), (radius, Lp - L + radius), (0, 0), (0, 0)))
        ap = ap.reshape(B, dilation, nb + 2, radius, H, E)
        return jnp.concatenate([ap[:, :, :-2], ap[:, :, 1:-1], ap[:, :, 2:]], axis=3)

    kw, vw = windows(ks), windows(vs)
    qi = jnp.arange(nb)[:, None] * radius + jnp.arange(radius)[None, :]
    ki = jnp.arange(nb)[:, None] * radius - radius + jnp.arange(3 * radius)[None, :]
    rel = ki[:, None, :] - qi[:, :, None]
    valid = (jnp.abs(rel) <= radius) & (ki[:, None, :] >= 0) & (ki[:, None, :] < L)
    dist = (jnp.abs(rel) * dilation).astype(jnp.float32)

    s = jnp.einsum('bdnqhe,bdnkhe->bdnhqk', qb, kw).astype(jnp.float32) * (E ** -0.5)
    s = s - slopes[:, None, None] * dist[:, None]
    s = jnp.where(valid[:, None], s, -jnp.inf)
    lse = jax.nn.logsumexp(s, axis=-1)
    p = jnp.exp(s - lse[..., None]).astype(v.dtype)
    o = jnp.einsum('bdnhqk,bdnkhe->bdnqhe', p, vw)

    o = o.reshape(B, dilation, Lp, H, E)[:, :, :L].transpose(0, 2, 1, 3, 4).reshape(B, S, H, E)
    lse = lse.transpose(0, 1, 2, 4, 3).reshape(B, dilation, Lp, H)[:, :, :L]
    lse = lse.transpose(0, 2, 1, 3).reshape(B, S, H)
    return o, lse

def _hyena_pos_features(L):
    t = jnp.linspace(0.0, 1.0, L, dtype=jnp.float32)[:, None]
    bands = (FILTER_EMB - 1) // 2
    w = 2.0 * math.pi * jnp.arange(L, dtype=jnp.float32)[:, None] / L
    f = jnp.linspace(1e-4, bands - 1, bands, dtype=jnp.float32)[None, :]
    return jnp.concatenate([t, jnp.cos(f * w), -jnp.sin(f * w)], axis=-1)

def implicit_filters(L, w1, b1, w2, b2, w3, b3, w4, freq):
    f32 = jnp.float32
    freq = freq.astype(f32)
    h = jnp.sin(freq * (_hyena_pos_features(L) @ w1.astype(f32) + b1.astype(f32)))
    h = jnp.sin(freq * (h @ w2.astype(f32) + b2.astype(f32)))
    h = jnp.sin(freq * (h @ w3.astype(f32) + b3.astype(f32)))
    h = h @ w4.astype(f32)
    t = jnp.linspace(0.0, 1.0, L, dtype=f32)[:, None]
    deltas = jnp.linspace(math.log(DECAY_TARGET) / SLOW_DECAY_PCT,
                          math.log(DECAY_TARGET) / FAST_DECAY_PCT, D_HYENA, dtype=f32)
    decay = jnp.exp(-t * jnp.abs(deltas)[None, :])
    return h.reshape(L, HYENA_ORDER, 2, D_HYENA) * decay[:, None, None, :]

def bidirectional_long_conv(z, h_fwd, h_bwd):
    L, C = h_fwd.shape
    circ = jnp.concatenate([h_fwd, jnp.zeros((1, C), jnp.float32), h_bwd[:0:-1]], axis=0)
    hf = jnp.fft.rfft(circ, axis=0)
    zf = jnp.fft.rfft(z.astype(jnp.float32), n=2 * L, axis=1)
    y = jnp.fft.irfft(zf * hf[None], n=2 * L, axis=1)[:, :L]
    return y.astype(z.dtype)

def centred_conv3(u, w, b):
    up = jnp.pad(u, ((0, 0), (1, 1), (0, 0)))
    return w[0] * up[:, :-2] + w[1] * up[:, 1:-1] + w[2] * up[:, 2:] + b

def hybrid_layer(x, c, w_ada, b_ada, w_in, b_in, conv_w, conv_b,
                 filt_w1, filt_b1, filt_w2, filt_b2, filt_w3, filt_b3, filt_w4, filt_freq, filt_bias,
                 w_proj_attn, w_proj_hyena, w_out, b_out, ln_g, ln_b):
    B, S, _ = x.shape
    mod = (c @ w_ada + b_ada)[:, None, :]
    shift, scale, gate = jnp.split(mod, 3, axis=-1)
    h = (_layer_norm(x) * (1.0 + scale) + shift).astype(x.dtype)

    p = h @ w_in + b_in
    i1 = N_QKV
    i2 = i1 + D_ATTN
    i3 = i2 + 3 * D_HYENA
    i4 = i3 + D_HYENA
    p_qkv, g_attn, p_hy, g_hy, r_merge = jnp.split(p, [i1, i2, i3, i4], axis=-1)
    r_attn, r_hy = jnp.split(r_merge, 2, axis=-1)

    qkv = p_qkv.reshape(B, S, 3, N_GROUPS, N_HEADS, HEAD_DIM)
    slopes = _alibi_slopes(N_HEADS)
    outs, lses = [], []
    for g, (window, dilation) in enumerate(DILATED_GROUPS):
        radius = window // (2 * dilation)
        o_g, lse_g = dilated_window_attention(qkv[:, :, 0, g], qkv[:, :, 1, g], qkv[:, :, 2, g],
                                              slopes, dilation, radius)
        outs.append(o_g)
        lses.append(lse_g)
    wts = jax.nn.softmax(jnp.stack(lses, axis=0), axis=0)
    o_attn = jnp.einsum('gbsh,gbshe->bshe', wts.astype(x.dtype), jnp.stack(outs, axis=0))
    y_attn = o_attn.reshape(B, S, D_ATTN) * jax.nn.silu(g_attn)

    u = centred_conv3(p_hy, conv_w, conv_b)
    v, x1, x2 = jnp.split(u, 3, axis=-1)
    filters = implicit_filters(S, filt_w1, filt_b1, filt_w2, filt_b2, filt_w3, filt_b3, filt_w4, filt_freq)
    z = v
    for o, gate_o in enumerate((x1, x2)):
        z = gate_o * (bidirectional_long_conv(z, filters[:, o, 0], filters[:, o, 1]) + filt_bias[o] * z)
    y_hy = z * jax.nn.silu(g_hy)

    merged = jax.nn.sigmoid(r_attn) * (y_attn @ w_proj_attn) + jax.nn.sigmoid(r_hy) * (y_hy @ w_proj_hyena)
    out = merged @ w_out + b_out

    res = DEEPNORM_ALPHA * x.astype(jnp.float32) + (gate * out).astype(jnp.float32)
    return (_layer_norm(res) * ln_g + ln_b).astype(x.dtype)

def first_inputs(seed: int = 0) -> dict:
    key = jax.random.key(seed)
    ks = jax.random.split(key, 24)
    f32 = jnp.float32

    def nrm(k, shape, scale):
        return jax.random.normal(k, shape, f32) * scale

    return {
        "x": nrm(ks[0], (BATCH, SEQ, D_MODEL), 1.0),
        "c": nrm(ks[1], (BATCH, D_MODEL), 1.0),
        "w_ada": nrm(ks[2], (DEPTH, D_MODEL, 3 * D_MODEL), 0.5 * D_MODEL ** -0.5),
        "b_ada": nrm(ks[3], (DEPTH, 3 * D_MODEL), 0.01),
        "w_in": nrm(ks[4], (DEPTH, D_MODEL, N_IN), D_MODEL ** -0.5),
        "b_in": nrm(ks[5], (DEPTH, N_IN), 0.01),
        "conv_w": nrm(ks[6], (DEPTH, 3, 3 * D_HYENA), 3 ** -0.5),
        "conv_b": nrm(ks[7], (DEPTH, 3 * D_HYENA), 0.01),
        "filt_w1": nrm(ks[8], (DEPTH, FILTER_EMB, FILTER_WIDTH), FILTER_EMB ** -0.5),
        "filt_b1": nrm(ks[9], (DEPTH, FILTER_WIDTH), 0.1),
        "filt_w2": nrm(ks[10], (DEPTH, FILTER_WIDTH, FILTER_WIDTH), FILTER_WIDTH ** -0.5),
        "filt_b2": nrm(ks[11], (DEPTH, FILTER_WIDTH), 0.1),
        "filt_w3": nrm(ks[12], (DEPTH, FILTER_WIDTH, FILTER_WIDTH), FILTER_WIDTH ** -0.5),
        "filt_b3": nrm(ks[13], (DEPTH, FILTER_WIDTH), 0.1),
        "filt_w4": nrm(ks[14], (DEPTH, FILTER_WIDTH, HYENA_ORDER * 2 * D_HYENA), 0.1 * FILTER_WIDTH ** -0.5),
        "filt_freq": 1.0 + nrm(ks[15], (DEPTH, FILTER_WIDTH), 0.05),
        "filt_bias": nrm(ks[16], (DEPTH, HYENA_ORDER, D_HYENA), 0.1),
        "w_proj_attn": nrm(ks[17], (DEPTH, D_ATTN, D_MODEL), DEEPNORM_BETA * D_ATTN ** -0.5),
        "w_proj_hyena": nrm(ks[18], (DEPTH, D_HYENA, D_MODEL), DEEPNORM_BETA * D_HYENA ** -0.5),
        "w_out": nrm(ks[19], (DEPTH, D_MODEL, D_MODEL), DEEPNORM_BETA * D_MODEL ** -0.5),
        "b_out": nrm(ks[20], (DEPTH, D_MODEL), 0.01),
        "ln_g": 1.0 + nrm(ks[21], (DEPTH, D_MODEL), 0.05),
        "ln_b": nrm(ks[22], (DEPTH, D_MODEL), 0.01),
    }

def first_block(x, c, w_ada, b_ada, w_in, b_in, conv_w, conv_b,
              filt_w1, filt_b1, filt_w2, filt_b2, filt_w3, filt_b3, filt_w4, filt_freq, filt_bias,
              w_proj_attn, w_proj_hyena, w_out, b_out, ln_g, ln_b):
    for l in range(DEPTH):
        x = hybrid_layer(x, c, w_ada[l], b_ada[l], w_in[l], b_in[l], conv_w[l], conv_b[l],
                         filt_w1[l], filt_b1[l], filt_w2[l], filt_b2[l], filt_w3[l], filt_b3[l],
                         filt_w4[l], filt_freq[l], filt_bias[l],
                         w_proj_attn[l], w_proj_hyena[l], w_out[l], b_out[l], ln_g[l], ln_b[l])
    return x


D_MIX = D_MODEL
SSM_WIDTH = D_MIX // 2
SSM_GROUP = 16
SSM_GROUPS = SSM_WIDTH // SSM_GROUP
SSM_STATE = 64
MLA_HEADS = 4
QK_NOPE = 128
QK_ROPE = 64
QK_DIM = QK_NOPE + QK_ROPE
V_HEAD = 128
MLA_WIDTH = MLA_HEADS * V_HEAD
Q_LORA = 256
KV_LORA = 128
PLE_DIM = 256
ROPE_THETA = 10000.0
Q_BLOCK = 128
RMS_EPS = 1e-6
DT_MIN = 1e-3
DT_MAX = 1e-1
MAX_POS_OFFSET = 4096
DEEPNORM_ALPHA_2 = (2 * DEPTH) ** 0.25
DEEPNORM_BETA_2 = (8 * DEPTH) ** -0.25

IN_SPLITS = (SSM_WIDTH, SSM_WIDTH, Q_LORA, KV_LORA, QK_ROPE, MLA_WIDTH)
D_IN = sum(IN_SPLITS)
IN_SPLIT_POINTS = tuple(int(v) for v in np.cumsum(IN_SPLITS)[:-1])


def layer_norm(x, g, b):
    xf = x.astype(jnp.float32)
    mu = jnp.mean(xf, axis=-1, keepdims=True)
    var = jnp.mean(jnp.square(xf - mu), axis=-1, keepdims=True)
    return ((xf - mu) * lax.rsqrt(var + LN_EPS)).astype(x.dtype) * g + b

def rms_norm(x, g):
    xf = x.astype(jnp.float32)
    return (xf * lax.rsqrt(jnp.mean(xf * xf, axis=-1, keepdims=True) + RMS_EPS)).astype(x.dtype) * g

def rope_tables(positions):
    inv_freq = 1.0 / (ROPE_THETA ** (jnp.arange(0, QK_ROPE, 2, dtype=jnp.float32) / QK_ROPE))
    ang = positions.astype(jnp.float32)[..., None] * inv_freq
    return jnp.cos(ang), jnp.sin(ang)

def rotary(x, cos, sin):
    xf = x.astype(jnp.float32)
    x1, x2 = jnp.split(xf, 2, axis=-1)
    return jnp.concatenate([x1 * cos - x2 * sin, x2 * cos + x1 * sin], axis=-1).astype(x.dtype)

def s5_branch(u, a_re, a_im, log_dt, b_re, b_im, c_re, c_im, d_skip, w_glu, b_glu):
    bsz, seqlen, _ = u.shape
    f32 = jnp.float32
    uf = u.astype(f32)
    ug = uf.reshape(bsz, seqlen, SSM_GROUPS, SSM_GROUP)
    a_re = a_re.astype(f32)
    a_im = a_im.astype(f32)
    dt = jnp.exp(log_dt.astype(f32))[:, None]
    mag = jnp.exp(dt * a_re)
    ab_re = mag * jnp.cos(dt * a_im)
    ab_im = mag * jnp.sin(dt * a_im)
    den = a_re * a_re + a_im * a_im
    nr = ab_re - 1.0
    k_re = (nr * a_re + ab_im * a_im) / den
    k_im = (ab_im * a_re - nr * a_im) / den
    bu_re = jnp.einsum('gpc,blgc->lbgp', b_re.astype(f32), ug)
    bu_im = jnp.einsum('gpc,blgc->lbgp', b_im.astype(f32), ug)
    x_re = k_re * bu_re - k_im * bu_im
    x_im = k_re * bu_im + k_im * bu_re
    a_seq_re = jnp.broadcast_to(ab_re, (seqlen, 1, SSM_GROUPS, SSM_STATE))
    a_seq_im = jnp.broadcast_to(ab_im, (seqlen, 1, SSM_GROUPS, SSM_STATE))

    def combine(left, right):
        al_re, al_im, bl_re, bl_im = left
        ar_re, ar_im, br_re, br_im = right
        return (al_re * ar_re - al_im * ar_im,
                al_re * ar_im + al_im * ar_re,
                ar_re * bl_re - ar_im * bl_im + br_re,
                ar_re * bl_im + ar_im * bl_re + br_im)

    _, _, h_re, h_im = lax.associative_scan(combine, (a_seq_re, a_seq_im, x_re, x_im), axis=0)
    y = (jnp.einsum('gcp,lbgp->blgc', c_re.astype(f32), h_re)
         - jnp.einsum('gcp,lbgp->blgc', c_im.astype(f32), h_im))
    y = y.reshape(bsz, seqlen, SSM_WIDTH) + d_skip.astype(f32) * uf
    y = jax.nn.gelu(y)
    y = y * jax.nn.sigmoid(y @ w_glu.astype(f32) + b_glu.astype(f32))
    return y.astype(u.dtype)

def mla_branch(cq, ckv, kr, cos, sin, q_norm_g, w_uq, kv_norm_g, w_ukv):
    bsz, seqlen, _ = cq.shape
    q = (rms_norm(cq, q_norm_g) @ w_uq).reshape(bsz, seqlen, MLA_HEADS, QK_DIM)
    q = jnp.concatenate([q[..., :QK_NOPE],
                         rotary(q[..., QK_NOPE:], cos[:, :, None, :], sin[:, :, None, :])], axis=-1)
    kv = (rms_norm(ckv, kv_norm_g) @ w_ukv).reshape(bsz, seqlen, MLA_HEADS, QK_NOPE + V_HEAD)
    k_nope, v = kv[..., :QK_NOPE], kv[..., QK_NOPE:]
    k_rope = rotary(kr, cos, sin)
    k = jnp.concatenate([k_nope, jnp.broadcast_to(k_rope[:, :, None, :],
                                                  (bsz, seqlen, MLA_HEADS, QK_ROPE))], axis=-1)
    scale = QK_DIM ** -0.5
    n_blocks = seqlen // Q_BLOCK
    q_blocks = q.reshape(bsz, n_blocks, Q_BLOCK, MLA_HEADS, QK_DIM).transpose(1, 0, 2, 3, 4)
    key_pos = jnp.arange(seqlen)

    def attend(args):
        qb, start = args
        s = jnp.einsum('bqhd,bkhd->bhqk', qb, k, preferred_element_type=jnp.float32) * scale
        q_pos = start + jnp.arange(Q_BLOCK)
        causal = key_pos[None, :] <= q_pos[:, None]
        s = jnp.where(causal, s, -jnp.inf)
        pr = jax.nn.softmax(s, axis=-1).astype(v.dtype)
        return jnp.einsum('bhqk,bkhd->bqhd', pr, v)

    out = lax.map(attend, (q_blocks, jnp.arange(n_blocks) * Q_BLOCK))
    return out.transpose(1, 0, 2, 3, 4).reshape(bsz, seqlen, MLA_WIDTH)

def second_inputs(seed: int = 0) -> dict:
    key = jax.random.key(seed)
    ks = jax.random.split(key, 26)
    f32 = jnp.float32
    nrm = lambda k, shape, s: jax.random.normal(k, shape, f32) * s
    x = jax.random.normal(ks[0], (BATCH, SEQ, D_MODEL), f32)
    p = jax.random.normal(ks[1], (DEPTH, BATCH, SEQ, PLE_DIM), f32)
    offsets = jax.random.randint(ks[2], (BATCH, 1), 0, MAX_POS_OFFSET, dtype=jnp.int32)
    positions = (jnp.arange(SEQ, dtype=jnp.int32)[None, :] + offsets).astype(jnp.int32)
    ln_emb_g = 1.0 + nrm(ks[3], (D_MODEL,), 0.05)
    ln_emb_b = nrm(ks[4], (D_MODEL,), 0.02)
    w_in = nrm(ks[5], (DEPTH, D_MODEL, D_IN), D_MODEL ** -0.5)
    a_re = -0.5 * jnp.exp(nrm(ks[6], (DEPTH, SSM_GROUPS, SSM_STATE), 0.05))
    a_im = math.pi * jnp.arange(SSM_STATE, dtype=f32) + nrm(ks[7], (DEPTH, SSM_GROUPS, SSM_STATE), 0.05)
    log_dt = jax.random.uniform(ks[8], (DEPTH, SSM_GROUPS), f32, math.log(DT_MIN), math.log(DT_MAX))
    b_re = nrm(ks[9], (DEPTH, SSM_GROUPS, SSM_STATE, SSM_GROUP), (2 * SSM_GROUP) ** -0.5)
    b_im = nrm(ks[10], (DEPTH, SSM_GROUPS, SSM_STATE, SSM_GROUP), (2 * SSM_GROUP) ** -0.5)
    c_re = nrm(ks[11], (DEPTH, SSM_GROUPS, SSM_GROUP, SSM_STATE), SSM_STATE ** -0.5)
    c_im = nrm(ks[12], (DEPTH, SSM_GROUPS, SSM_GROUP, SSM_STATE), SSM_STATE ** -0.5)
    d_skip = nrm(ks[13], (DEPTH, SSM_WIDTH), 1.0)
    w_glu = nrm(ks[14], (DEPTH, SSM_WIDTH, SSM_WIDTH), SSM_WIDTH ** -0.5)
    b_glu = nrm(ks[15], (DEPTH, SSM_WIDTH), 0.02)
    q_norm_g = 1.0 + nrm(ks[16], (DEPTH, Q_LORA), 0.05)
    w_uq = nrm(ks[17], (DEPTH, Q_LORA, MLA_HEADS * QK_DIM), Q_LORA ** -0.5)
    kv_norm_g = 1.0 + nrm(ks[18], (DEPTH, KV_LORA), 0.05)
    w_ukv = nrm(ks[19], (DEPTH, KV_LORA, MLA_HEADS * (QK_NOPE + V_HEAD)), KV_LORA ** -0.5)
    w_out = nrm(ks[20], (DEPTH, D_MIX, D_MODEL), D_MIX ** -0.5 * DEEPNORM_BETA_2)
    w_pg = nrm(ks[21], (DEPTH, D_MODEL, D_MODEL), D_MODEL ** -0.5)
    w_pp = nrm(ks[22], (DEPTH, PLE_DIM, D_MODEL), PLE_DIM ** -0.5 * DEEPNORM_BETA_2)
    ln_g = 1.0 + nrm(ks[23], (DEPTH, D_MODEL), 0.05)
    ln_b = nrm(ks[24], (DEPTH, D_MODEL), 0.02)
    return {"x": x, "p": p, "positions": positions, "ln_emb_g": ln_emb_g, "ln_emb_b": ln_emb_b,
            "w_in": w_in, "a_re": a_re, "a_im": a_im, "log_dt": log_dt,
            "b_re": b_re, "b_im": b_im, "c_re": c_re, "c_im": c_im, "d_skip": d_skip,
            "w_glu": w_glu, "b_glu": b_glu, "q_norm_g": q_norm_g, "w_uq": w_uq,
            "kv_norm_g": kv_norm_g, "w_ukv": w_ukv, "w_out": w_out, "w_pg": w_pg,
            "w_pp": w_pp, "ln_g": ln_g, "ln_b": ln_b}

def second_block(x, p, positions, ln_emb_g, ln_emb_b, w_in, a_re, a_im, log_dt,
              b_re, b_im, c_re, c_im, d_skip, w_glu, b_glu, q_norm_g, w_uq,
              kv_norm_g, w_ukv, w_out, w_pg, w_pp, ln_g, ln_b):
    x = layer_norm(x, ln_emb_g, ln_emb_b)
    cos, sin = rope_tables(positions)
    for i in range(DEPTH):
        z = x @ w_in[i]
        xs, gs, cq, ckv, kr, gm = jnp.split(z, IN_SPLIT_POINTS, axis=-1)
        ys = s5_branch(xs, a_re[i], a_im[i], log_dt[i], b_re[i], b_im[i], c_re[i], c_im[i],
                       d_skip[i], w_glu[i], b_glu[i]) * jax.nn.silu(gs)
        ym = mla_branch(cq, ckv, kr, cos, sin, q_norm_g[i], w_uq[i], kv_norm_g[i],
                        w_ukv[i]) * jax.nn.silu(gm)
        mix = jnp.concatenate([ys, ym], axis=-1) @ w_out[i]
        u = DEEPNORM_ALPHA_2 * x + mix
        ple = jax.nn.sigmoid(u @ w_pg[i]) * (p[i] @ w_pp[i])
        x = layer_norm(u + ple, ln_g[i], ln_b[i])
    return x


def setup_inputs(seed=0):
    out = dict(first_inputs(seed))
    for name, value in second_inputs(seed + 1).items():
        if name != "x":
            out[name + "_2"] = value
    return out


def reference(
    x, c, w_ada, b_ada, w_in, b_in, conv_w, conv_b, filt_w1, filt_b1, filt_w2, filt_b2, filt_w3,
    filt_b3, filt_w4, filt_freq, filt_bias, w_proj_attn, w_proj_hyena, w_out, b_out, ln_g, ln_b,
    p_2, positions_2, ln_emb_g_2, ln_emb_b_2, w_in_2, a_re_2, a_im_2, log_dt_2, b_re_2, b_im_2,
    c_re_2, c_im_2, d_skip_2, w_glu_2, b_glu_2, q_norm_g_2, w_uq_2, kv_norm_g_2, w_ukv_2,
    w_out_2, w_pg_2, w_pp_2, ln_g_2, ln_b_2,
):
    x = first_block(
        x, c, w_ada, b_ada, w_in, b_in, conv_w, conv_b, filt_w1, filt_b1, filt_w2, filt_b2,
        filt_w3, filt_b3, filt_w4, filt_freq, filt_bias, w_proj_attn, w_proj_hyena, w_out,
        b_out, ln_g, ln_b,
    )
    return second_block(
        x, p_2, positions_2, ln_emb_g_2, ln_emb_b_2, w_in_2, a_re_2, a_im_2, log_dt_2, b_re_2,
        b_im_2, c_re_2, c_im_2, d_skip_2, w_glu_2, b_glu_2, q_norm_g_2, w_uq_2, kv_norm_g_2,
        w_ukv_2, w_out_2, w_pg_2, w_pp_2, ln_g_2, ln_b_2,
    )


_drawn_inputs = setup_inputs


def setup_inputs(seed=0):
    import zlib

    import numpy as np

    out = dict(_drawn_inputs(seed))
    spreads = {}
    factors = {'b_ada': 4.304,
     'b_in': 5.459,
     'conv_b': 4.704,
     'filt_bias': 3.695,
     'b_out': 8.0,
     'ln_b': 5.656,
     'ln_emb_b_2': 2.901,
     'a_re_2': 64.0,
     'a_im_2': 64.0,
     'log_dt_2': 64.0,
     'b_re_2': 64.0,
     'b_im_2': 64.0,
     'c_re_2': 64.0,
     'c_im_2': 64.0,
     'w_glu_2': 7.655,
     'b_glu_2': 64.0,
     'q_norm_g_2': 8.0,
     'kv_norm_g_2': 8.0,
     'ln_b_2': 2.841}
    for name, (base, spread) in spreads.items():
        noise = np.random.default_rng([zlib.crc32(name.encode()), seed]).standard_normal(out[name].shape)
        drawn = base * np.exp(spread * noise) if base else spread * noise
        out[name] = __import__('jax').numpy.asarray(drawn.astype(out[name].dtype))
    for name, factor in factors.items():
        out[name] = (out[name] * factor).astype(out[name].dtype)
    return out
```

```python
import math
from contextlib import ExitStack

import numpy as np

import concourse.bass as bass
from concourse import mybir

fp32 = mybir.dt.float32
i32 = mybir.dt.int32
ALU = mybir.AluOpType
ACT = mybir.ActivationFunctionType
AX = mybir.AxisListType

P = 128
S = 1024
D = 1024
KT = D // P
NT = S // P
HD = 64
CH = 512
N_QKV = 4608
COL_GATTN = N_QKV
COL_HY = COL_GATTN + CH
COL_R = COL_HY + 4 * CH
ALPHA = 2 ** 0.25
TWO_PI = 2 * math.pi
ROUND = 1.5 * 2 ** 23
R2 = math.sqrt(0.5)
FAR = 1e32

PI_A = float(np.float32(6.28125))
PI_B = float(np.float32(np.round((TWO_PI - PI_A) * 2 ** 22) / 2 ** 22))
PI_C = float(np.float32(TWO_PI - PI_A - PI_B))
PI_CLIP = float(np.nextafter(np.float32(math.pi), np.float32(0)))


def leaf_tables():
    fwd, inv = {}, {}
    t = np.arange(256)[None, :]
    for name, phase in (("P", math.pi / 4), ("M", 5 * math.pi / 4)):
        k = np.arange(256)[:, None]
        a = (phase + 2 * math.pi * k) / 256 * t
        c, s = np.cos(a), np.sin(a)
        fwd[name] = np.block([[c.T, s.T], [-s.T, c.T]])
        inv[name] = np.block([[c, -s], [s, c]]) / 256 / 4
    for name, n, k, roots, scale in (("B", 512, 256, math.pi * (2 * np.arange(256) + 1) / 512, 2 / 512 / 4),
                                     ("N", 256, 128, math.pi * (2 * np.arange(128) + 1) / 256, 2 / 256 / 8),
                                     ("C", 256, 256, 2 * math.pi * np.arange(256) / 256, 1 / 256 / 8)):
        a = roots[:, None] * np.arange(n)[None, :]
        c, s = np.cos(a), np.sin(a)
        fwd[name] = np.hstack([c.T, s.T])
        inv[name] = np.vstack([c, s]) * scale
    order = "PMBNC"
    return {f"fwd_{n}": fwd[n].astype(np.float32) for n in order} | {f"inv_{n}": inv[n].astype(np.float32) for n in order}


def shape_constants():
    f32 = np.float32
    out = {"ident": np.eye(P, dtype=f32)}
    L = S
    pos = np.concatenate([np.arange(L), (L - np.arange(L)) % L])
    t = np.linspace(0.0, 1.0, L, dtype=f32)[:, None]
    bands = 16
    w = (2.0 * math.pi * np.arange(L, dtype=f32)[:, None] / L).astype(f32)
    f = np.linspace(1e-4, bands - 1, bands, dtype=f32)[None, :]
    feat = np.concatenate([t, np.cos(f * w), -np.sin(f * w)], axis=-1).astype(f32)
    out["posT"] = np.ascontiguousarray(feat[pos].T)
    deltas = np.linspace(math.log(1e-2) / 1.5, math.log(1e-2) / 0.3, CH, dtype=f32)
    decay = np.exp(-t * np.abs(deltas)[None, :]).astype(f32)[pos]
    decay[L] = 0.0
    out["decay"] = decay
    out.update(leaf_tables())
    q, key = np.arange(P)[:, None], np.arange(256)[None, :]
    tables = []
    for shift in (0, 64, 128):
        rel = np.abs(key - shift - q)
        tables.append(np.where(rel <= 64, rel, FAR))
    for a in range(2):
        rel = np.abs(key - (2 * q + a))
        same = np.abs(key[:, :P] - q)
        tables += [np.where(rel <= 64, 4 * rel, FAR), np.where(same % 2 == 0, 8 * same, FAR)]
    out["dist"] = np.concatenate(tables, axis=1).astype(f32)
    out["causal"] = np.concatenate([np.zeros((P, 7 * P)), np.where(np.arange(P)[None, :] <= q, 0.0, -1e30)], axis=1).astype(f32)
    out["inv_freq"] = (np.float32(1.0) / np.power(np.float32(10000.0), np.arange(0, 64, 2, dtype=f32) / np.float32(64))).astype(f32)
    return out


class Count:

    def __init__(self, sem):
        self.sem, self.n = sem, 0

    def by(self, ins):
        self.n += 1
        return ins.then_inc(self.sem, 1)


class Kernel:
    def __init__(self, nc, io):
        self.nc, self.io = nc, io
        self.ctx = ExitStack()
        self.A = self.ctx.enter_context(nc.sbuf_tensor("arena", [P, 52400], fp32))
        self.PS = self.ctx.enter_context(nc.psum_tensor("banks", [P, 8, 512], fp32))
        self.phase_sems = []
        self.out_done = self.ctx.enter_context(nc.semaphore("out_done"))

    def at(self, off, *dims):
        n = int(np.prod(dims))
        assert off + n <= 52400, (off, n)
        v = self.A[:, off:off + n]
        if len(dims) == 2:
            v = v.rearrange("p (a b) -> p a b", a=dims[0])
        if len(dims) == 3:
            v = v.rearrange("p (a b c) -> p a b c", a=dims[0], b=dims[1])
        if len(dims) == 4:
            v = v.rearrange("p (a b c d) -> p a b c d", a=dims[0], b=dims[1], c=dims[2])
        return v

    def sem(self, ctx, name):
        self.phase_sems.append(self.nc.alloc_semaphore(name))
        return self.phase_sems[-1]

    def end_phase(self):
        self.nc.clear_and_free_semaphores(self.phase_sems)
        self.nc.all_engine_barrier()
        self.phase_sems = []


def bcast_rows(ap1d, n=P):
    return ap1d.partition_broadcast(n)


IDENT = 0
COLS1 = 128
COLS2 = COLS1 + 128
MODT = COLS2 + 64
GATE = MODT + 16
MLPC = GATE + 1024
HT = 1408
assert MLPC + 8 <= HT
H3 = HT + 8192
FREE1 = H3 + 2048
N_COLS1 = 120


def reduced_sine_argument(nc, link, out, x, k, quarter=0.0):
    link(nc.vector.tensor_scalar(k, x, 1 / TWO_PI, ROUND + quarter if not quarter else quarter, ALU.mult, ALU.add))
    if quarter:
        link(nc.vector.tensor_scalar(k, k, ROUND, None, ALU.add))
    link(nc.vector.tensor_scalar(k, k, ROUND, None, ALU.subtract))
    link(nc.vector.scalar_tensor_tensor(out, k, -PI_A, x, ALU.mult, ALU.add))
    link(nc.vector.scalar_tensor_tensor(out, k, -PI_B, out, ALU.mult, ALU.add))
    link(nc.vector.scalar_tensor_tensor(out, k, -PI_C, out, ALU.mult, ALU.add))
    if quarter:
        link(nc.vector.tensor_scalar(out, out, quarter * TWO_PI, PI_CLIP, ALU.add, ALU.min))
        link(nc.vector.tensor_scalar(out, out, -PI_CLIP, None, ALU.max))
    else:
        link(nc.vector.tensor_scalar(out, out, PI_CLIP, -PI_CLIP, ALU.min, ALU.max))


def prepare(K):
    nc, io = K.nc, K.io
    o = FREE1
    xr = K.at(o, NT, D); o += NT * D
    wada = K.at(o, 2, KT, 512); o += 2 * KT * 512
    bada = K.at(o, 3 * D); o += 3 * D
    mod = K.at(o, 6, 512); o += 3 * D
    cbc = K.at(o, KT, P); o += KT * P
    stats = K.at(o, NT, 12); o += NT * 12
    mv = K.at(o, NT, 2); o += NT * 2
    std = K.at(o, NT); o += NT
    rows = K.at(o, 2, P); o += 2 * P
    posT = K.at(o, 2048); o += 2048
    hA = K.at(o, 2048); o += 2048
    kk = K.at(o, 2048); o += 2048
    wf = K.at(o, 3, HD); o += 3 * HD
    one = K.at(o, 1); o += 1
    ident, hT, modT, gate = K.at(IDENT, P), K.at(HT, KT, S), K.at(MODT, 16), K.at(GATE, D)
    cols1, cols2, mlpc, h3 = K.at(COLS1, N_COLS1), K.at(COLS2, 64), K.at(MLPC, 8), K.at(H3, 2048)
    PS = K.PS
    with ExitStack() as ctx:
        s = lambda n: K.sem(ctx, "prep_" + n)
        x_in, c_in, small_in, row_in = [s(f"x_in{i}") for i in range(4)], s("c_in"), s("small_in"), s("row_in")
        wada_in = [s("wada_in0"), s("wada_in1")]
        order, cbc_ready, mod_done, mod_ready, col_done, modT_ready = s("order"), s("cbc"), s("mod_done"), s("mod_ready"), s("col_done"), s("modT")
        var_ready, std_ready, norm_ready, tr_done, hT_ready = s("var"), s("std"), s("norm"), s("tr"), s("hT")
        rows_tr, rows_ready, mlp_mm, mlp_arg, mlp_sin = s("rows_tr"), s("rows_ready"), s("mlp_mm"), s("mlp_arg"), s("mlp_sin")
        zero_ready = s("zero")
        block = ctx.enter_context(nc.Block())

        @block.sync
        def _(sp):
            sp.dma_start(ident, io["ident"]).then_inc(row_in, 16)
            sp.wait_ge(zero_ready, 1)
            sp.dma_start(rows[0:72, 0, :], io["b_in"].rearrange("o (n p) -> (o n) p", p=P)).then_inc(row_in, 16)
            sp.dma_start(rows[72:108, 0, :], io["conv_w"].rearrange("o t (n p) -> (o t n) p", p=P)).then_inc(row_in, 16)
            sp.dma_start(rows[108:120, 0, :], io["conv_b"].rearrange("o (n p) -> (o n) p", p=P)).then_inc(row_in, 16)
            sp.dma_start(rows[0:16, 1, :], io["a_re_2"].rearrange("o (j g) p -> (o j) (g p)", g=2)).then_inc(row_in, 16)
            sp.dma_start(rows[16:32, 1, :], io["a_im_2"].rearrange("o (j g) p -> (o j) (g p)", g=2)).then_inc(row_in, 16)
            sp.dma_start(rows[32:36, 1, :], io["b_glu_2"].rearrange("o (n p) -> (o n) p", p=P)).then_inc(row_in, 16)
            sp.dma_start(rows[36:38, 1, :], io["q_norm_g_2"].rearrange("o (n p) -> (o n) p", p=P)).then_inc(row_in, 16)
            sp.dma_start(rows[38:39, 1, :], io["kv_norm_g_2"]).then_inc(row_in, 16)
            sp.dma_start(rows[39:47, 1, :], io["c"].rearrange("o (k p) -> (o k) p", p=P)).then_inc(row_in, 16)
            for i in range(4):
                sp.dma_start(xr[:, 2 * i:2 * i + 2, :], io["x"][0, 2 * i * P:(2 * i + 2) * P, :].rearrange("(a p) n -> p a n", p=P)).then_inc(x_in[i], 16)
            sp.dma_start(bada, bcast_rows(io["b_ada"][0])).then_inc(c_in, 16)

        @block.gpsimd
        def _(pool):
            nc.gpsimd.memset(rows[:, :, :], 0.0).then_inc(zero_ready, 1)
            for n, name in enumerate(("filt_b1", "filt_b2", "filt_b3", "filt_freq")):
                pool.dma_start(mlpc[0:HD, n:n + 1], io[name].rearrange("o (p a) -> p (o a)", a=1)).then_inc(small_in, 16)
            pool.dma_start(posT[0:33, :], io["posT"]).then_inc(small_in, 16)
            pool.dma_start(wf[0:33, 0, :], io["filt_w1"][0]).then_inc(small_in, 16)
            pool.dma_start(wf[0:HD, 1, :], io["filt_w2"][0]).then_inc(small_in, 16)
            pool.dma_start(wf[0:HD, 2, :], io["filt_w3"][0]).then_inc(small_in, 16)
            w = io["w_ada"][0].rearrange("(k p) n -> p k n", p=P)
            for c in range(6):
                if c >= 2:
                    pool.wait_ge(mod_done, c - 1)
                pool.dma_start(wada[:, c % 2, :, :], w[:, :, c * 512:(c + 1) * 512]).then_inc(wada_in[c % 2], 16)

        @block.scalar
        def _(act):
            act.wait_ge(var_ready, 1)
            nc.scalar.activation(std, mv[:, :, 1], ACT.Sqrt).then_inc(std_ready, 1)
            for layer in range(3):
                act.wait_ge(mlp_arg, layer + 1)
                dst = h3 if layer == 2 else hA
                nc.scalar.activation(dst[0:HD, :], kk[0:HD, :], ACT.Sin).then_inc(mlp_sin, 1)
            act.wait_ge(modT_ready, 1)
            for n in range(16):
                k, h = n // 2, n % 2
                act.wait_ge(tr_done, n + 1)
                nc.scalar.activation(hT[:, k, h * 512:(h + 1) * 512], PS[:, n % 4, :], ACT.Identity,
                                     bias=modT[:, k:k + 1], scale=modT[:, 8 + k:9 + k]).then_inc(hT_ready, 1)

        @block.vector
        def _(dve):
            chain = Count(order)

            def link(ins, signal=chain):
                signal.by(ins)
                dve.wait_ge(signal.sem, signal.n)

            nc.vector.memset(one, 1.0)
            dve.wait_ge(rows_tr, 1)
            nc.vector.tensor_copy(cols1, PS[:, 7, 0:N_COLS1])
            nc.vector.tensor_copy(cols2, PS[:, 7, 128:192]).then_inc(rows_ready, 1)
            dve.wait_ge(rows_ready, 1)
            nc.vector.tensor_copy(cbc, cols2[:, 39:39 + KT].unsqueeze(2).to_broadcast([P, KT, P])).then_inc(cbc_ready, 1)
            for i in range(NT):
                dve.wait_ge(x_in[i // 2], 16)
                nc.vector.bn_stats(stats[:, i, 0:6], xr[:, i, 0:512])
                link(nc.vector.bn_stats(stats[:, i, 6:12], xr[:, i, 512:1024]))
            for i in range(NT):
                link(nc.vector.bn_aggr(mv[:, i, :], stats[:, i, :]))
            link(nc.vector.tensor_scalar(mv[:, :, 1], mv[:, :, 1], 1e-5, None, ALU.add), Count(var_ready))
            for layer in range(3):
                dve.wait_ge(small_in, 16 * 8)
                dve.wait_ge(mlp_mm, layer + 1)
                for n in range(4):
                    link(nc.vector.tensor_scalar(hA[0:HD, n * 512:(n + 1) * 512], PS[0:HD, n, :],
                                                 mlpc[0:HD, layer:layer + 1], mlpc[0:HD, 3:4], ALU.add, ALU.mult))
                reduced_sine_argument(nc, link, kk[0:HD, :], hA[0:HD, :], posT[0:HD, :])
                nc.vector.memset(posT[0:1, 0:1], 0.0).then_inc(mlp_arg, 1)
            dve.wait_ge(std_ready, 1)
            link(nc.vector.reciprocal(std, std))
            for i in range(NT):
                nc.vector.tensor_scalar(xr[:, i, :], xr[:, i, :], mv[:, i, 0:1], std[:, i:i + 1],
                                        ALU.subtract, ALU.mult).then_inc(norm_ready, 1)
            dve.wait_ge(c_in, 16)
            for c in range(6):
                dve.wait_ge(mod_done, c + 1)
                nc.vector.tensor_tensor(mod[:, c, :], PS[:, 4 + c % 2, :], bada[:, c * 512:(c + 1) * 512],
                                        ALU.add).then_inc(mod_ready, 1)
            dve.wait_ge(mod_ready, 6)
            nc.vector.tensor_copy(gate, mod[:, 4:6, :].rearrange("p a b -> p (a b)"))
            dve.wait_ge(col_done, 1)
            link(nc.vector.tensor_copy(modT, PS[:, 6, 0:16]))
            nc.vector.tensor_scalar(modT[:, 8:16], modT[:, 8:16], 1.0, None, ALU.add).then_inc(modT_ready, 1)

        @block.tensor
        def _(pe):
            def mlp(layer):
                if layer == 0:
                    pe.wait_ge(small_in, 16 * 8)
                else:
                    pe.wait_ge(mlp_sin, layer)
                rows_in = 33 if layer == 0 else HD
                src = posT if layer == 0 else hA
                for n in range(4):
                    last = nc.tensor.matmul(PS[0:HD, n, :], wf[0:rows_in, layer, :], src[0:rows_in, n * 512:(n + 1) * 512],
                                            start=True, stop=True)
                last.then_inc(mlp_mm, 1)

            pe.wait_ge(row_in, 16 * 10)
            nc.tensor.transpose(PS[:, 7, 0:128], rows[:, 0, :], ident)
            nc.tensor.transpose(PS[:, 7, 128:256], rows[:, 1, :], ident).then_inc(rows_tr, 1)
            mlp(0)
            pe.wait_ge(cbc_ready, 1)
            for c in range(6):
                pe.wait_ge(wada_in[c % 2], 16 * (c // 2 + 1))
                if c >= 2:
                    pe.wait_ge(mod_ready, c - 1)
                for k in range(KT):
                    last = nc.tensor.matmul(PS[:, 4 + c % 2, :], cbc[:, k, :], wada[:, c % 2, k, :],
                                            start=(k == 0), stop=(k == KT - 1))
                last.then_inc(mod_done, 1)
                if c == 0:
                    mlp(1)
                if c == 1:
                    mlp(2)
            pe.wait_ge(mod_ready, 4)
            for k in range(16):
                last = nc.tensor.matmul(PS[:, 6, k:k + 1], mod[0:1, k // 4, (k % 4) * P:(k % 4 + 1) * P],
                                        one[0:1, 0:1], start=True, stop=True)
            last.then_inc(col_done, 1)
            pe.wait_ge(norm_ready, NT)
            pe.wait_ge(mlp_sin, 3)
            for n in range(16):
                k, h = n // 2, n % 2
                if n >= 4:
                    pe.wait_ge(hT_ready, n - 3)
                for i in range(4):
                    last = nc.tensor.transpose(PS[:, n % 4, i * P:(i + 1) * P], xr[:, 4 * h + i, k * P:(k + 1) * P], ident)
                last.then_inc(tr_done, 1)


ZV, X1T = FREE1, FREE1 + 4096
LF = X1T + 4096
HS = LF + 8192
FWORK = HS + 18 * 512


def project_hyena(K, first, last, scratch, x2=None, ghy=None):
    nc, io, PS = K.nc, K.io, K.PS
    o = scratch
    wt = K.at(o, 4, KT, P); o += 4096
    pb = K.at(o, 2, S + 2); o += 2 * (S + 2)
    ub = K.at(o, 2, S); o += 2 * S
    hT, cols1, ident = K.at(HT, KT, S), K.at(COLS1, N_COLS1), K.at(IDENT, P)
    rows_of = [K.at(ZV, 8, CH), K.at(X1T, 8, CH)]
    tiles = list(range(first, last))
    w = io["w_in"][0].rearrange("(k p) n -> p k n", p=P)
    with ExitStack() as ctx:
        s = lambda n: K.sem(ctx, f"hy{first}_" + n)
        w_in, order = [s(f"w_in{b}") for b in range(4)], s("order")
        proj_done, p_ready, conv_done, tr_done, z_ready, border = s("proj"), s("p_ready"), s("conv"), s("tr"), s("z"), s("border")
        block = ctx.enter_context(nc.Block())

        @block.sync
        def _(sp):
            for n, t in enumerate(tiles):
                if n >= 4:
                    sp.wait_ge(proj_done, n - 3)
                c0 = COL_HY + t * P
                sp.dma_start(wt[:, n % 4, :, :], w[:, :, c0:c0 + P]).then_inc(w_in[n % 4], 16)

        @block.tensor
        def _(pe):
            def project(n):
                pe.wait_ge(w_in[n % 4], 16 * (n // 4 + 1))
                if n >= 3:
                    pe.wait_ge(p_ready, n - 2)
                for h in range(2):
                    for k in range(KT):
                        last = nc.tensor.matmul(PS[:, 2 * (n % 3) + h, :], wt[:, n % 4, k, :], hT[:, k, h * 512:(h + 1) * 512],
                                                start=(k == 0), stop=(k == KT - 1))
                last.then_inc(proj_done, 1)

            def to_rows(n):
                pe.wait_ge(conv_done, n + 1)
                if n >= 1:
                    pe.wait_ge(z_ready, n)
                for i in range(NT):
                    last = nc.tensor.transpose(PS[:, 6 + i // 4, (i % 4) * P:(i % 4 + 1) * P], ub[:, n % 2, i * P:(i + 1) * P], ident)
                last.then_inc(tr_done, 1)

            for n, t in enumerate(tiles):
                project(n)
                if n >= 2 and tiles[n - 2] < 8:
                    to_rows(n - 2)
            for n in range(len(tiles) - 2, len(tiles)):
                if tiles[n] < 8:
                    to_rows(n)

        @block.scalar
        def _(act):
            def take_rows(n):
                act.wait_ge(tr_done, n + 1)
                dst = rows_of[tiles[n] // 4][:, :, (tiles[n] % 4) * P:(tiles[n] % 4 + 1) * P]
                for h in range(2):
                    last = nc.scalar.copy(dst[:, 4 * h:4 * h + 4, :], PS[:, 6 + h, :].rearrange("p (i c) -> p i c", c=P))
                last.then_inc(z_ready, 1)

            act.wait_ge(border, 1)
            for n, t in enumerate(tiles):
                act.wait_ge(proj_done, n + 1)
                if n >= 2 and t < 12:
                    act.wait_ge(conv_done, n - 1)
                bias = cols1[:, COL_HY // P + t:COL_HY // P + t + 1]
                for h in range(2):
                    src = PS[:, 2 * (n % 3) + h, :]
                    if t < 12:
                        last = nc.scalar.activation(pb[:, n % 2, 1 + h * 512:1 + (h + 1) * 512], src, ACT.Identity, bias=bias)
                    else:
                        last = nc.scalar.activation(ghy[:, t - 12, h * 512:(h + 1) * 512], src, ACT.Silu, bias=bias)
                last.then_inc(p_ready, 1)
                if n >= 2 and tiles[n - 2] < 8:
                    take_rows(n - 2)
            for n in range(len(tiles) - 2, len(tiles)):
                if tiles[n] < 8:
                    take_rows(n)

        @block.vector
        def _(dve):
            chain = Count(order)

            def link(ins, signal=chain):
                signal.by(ins)
                dve.wait_ge(signal.sem, signal.n)

            nc.vector.memset(pb[:, :, 0:1], 0.0)
            nc.vector.memset(pb[:, :, S + 1:S + 2], 0.0).then_inc(border, 1)
            for n, t in enumerate(tiles):
                if t >= 12:
                    continue
                dve.wait_ge(p_ready, n + 1)
                if n >= 2 and t < 8:
                    dve.wait_ge(tr_done, n - 1)
                u = ub[:, n % 2, :] if t < 8 else x2[:, t - 8, :]
                tap = lambda j: cols1[:, 72 + 12 * j + t:73 + 12 * j + t]
                link(nc.vector.tensor_scalar(u, pb[:, n % 2, 1:S + 1], tap(1), cols1[:, 108 + t:109 + t], ALU.mult, ALU.add))
                link(nc.vector.scalar_tensor_tensor(u, pb[:, n % 2, 0:S], tap(0), u, ALU.mult, ALU.add))
                nc.vector.scalar_tensor_tensor(u, pb[:, n % 2, 2:S + 2], tap(2), u, ALU.mult, ALU.add).then_inc(conv_done, 1)


LEAVES = {"P": (4, 0, 2), "M": (4, 4, 2), "B": (4, 8, 2), "N": (2, 12, 1), "C": (2, 14, 2)}


def leaf_inputs(name, neg, cyc):
    return {"P": [neg[0], neg[1], neg[4], neg[5]], "M": [neg[2], neg[3], neg[6], neg[7]],
            "B": cyc[0:4], "N": cyc[4:6], "C": cyc[6:8]}[name]


def long_convolution(K, order_no, scratch, x2=None, ghy=None, yT=None):
    nc, io, PS = K.nc, K.io, K.PS
    o = scratch
    w4 = K.at(o, 2, CH); o += 1024
    dec = K.at(o, 4, CH); o += 4 * CH
    mat = K.at(o, 2, 2048); o += 4096
    tmp = K.at(o, 4, CH); o += 4 * CH
    bias_row = K.at(o, CH); o += CH
    z, x1t, h3 = K.at(ZV, 8, CH), K.at(X1T, 8, CH), K.at(H3, 2048)
    neg, cyc, H = K.at(LF, 8, CH), K.at(LF + 4096, 8, CH), K.at(HS, 18, CH)
    names = "PMBNC"
    rec = {"P": K.at(LF, 4, CH), "M": K.at(LF + 2048, 4, CH), "A": K.at(LF + 4096, 4, CH), "B": K.at(LF + 6144, 4, CH)}
    rec_of = {"P": rec["P"], "M": rec["M"], "B": rec["B"], "N": rec["A"][:, 0:2, :], "C": rec["A"][:, 2:4, :]}
    with ExitStack() as ctx:
        s = lambda n: K.sem(ctx, f"lc{order_no}_" + n)
        w_in, dec_in, mat_in = s("w_in"), [s(f"dec_in{b}") for b in range(4)], [s("mat_in0"), s("mat_in1")]
        order, f_mm, f_ready, lf_ready = s("order"), s("f_mm"), s("f_ready"), s("lf_ready")
        hs_mm, hs_ready, zl_ready, zs_mm, zs_ready = s("hs_mm"), s("hs_ready"), s("zl"), s("zs_mm"), s("zs_ready")
        iv_mm, iv_ready, y_done = s("iv_mm"), s("iv_ready"), s("y_done")
        block = ctx.enter_context(nc.Block())

        @block.sync
        def _(sp):
            for d in range(2):
                c0 = order_no * 1024 + d * CH
                sp.dma_start(w4[0:HD, d, :], io["filt_w4"][0, :, c0:c0 + CH]).then_inc(w_in, 16)
            sp.dma_start(bias_row[0:1, :], io["filt_bias"][0, order_no:order_no + 1, :]).then_inc(w_in, 16)
            for t in range(16):
                if t >= 4:
                    sp.wait_ge(f_ready, t - 3)
                sp.dma_start(dec[:, t % 4, :], io["decay"][t * P:(t + 1) * P, :]).then_inc(dec_in[t % 4], 16)

        matrices = [("fwd_" + n) for n in names] * 2 + [("inv_" + n) for n in names]

        def matrix(n):
            rows, cols = io[matrices[n]].shape
            return mat[:, n % 2, 0:rows // P * cols].rearrange("p (k c) -> p k c", c=cols)

        def used_after(stage, name):
            kt, first, pairs = LEAVES[name]
            if stage < 2:
                return first + 2 * pairs
            upto = names[:names.index(name) + 1]
            return 4 * len(upto) if order_no else sum(io["inv_" + m].shape[1] // P for m in upto)

        @block.gpsimd
        def _(pool):
            for n, name in enumerate(matrices):
                if n >= 2:
                    pool.wait_ge((hs_mm, zs_mm, iv_mm)[(n - 2) // 5], used_after((n - 2) // 5, names[(n - 2) % 5]))
                pool.dma_start(matrix(n), io[name].rearrange("(k p) c -> p k c", p=P)).then_inc(mat_in[n % 2], 16)

        def forward(pe, n, name, neg_in, mm_sem, before):
            kt, first, pairs = LEAVES[name]
            ins, m = leaf_inputs(name, [neg_in[:, i, :] for i in range(8)], [cyc[:, i, :] for i in range(8)]), matrix(n)
            pe.wait_ge(mat_in[n % 2], 16 * (n // 2 + 1))
            f = m.shape[2] // 2
            for q in range(pairs):
                for part in range(2):
                    b = (first + 2 * q + part) % 8
                    before(first + 2 * q + part)
                    for k in range(kt):
                        last = nc.tensor.matmul(PS[:, b, :], m[:, k, part * f + q * P:part * f + (q + 1) * P], ins[k],
                                                start=(k == 0), stop=(k == kt - 1))
                    last.then_inc(mm_sem, 1)

        @block.tensor
        def _(pe):
            pe.wait_ge(w_in, 48)
            for t in range(16):
                if t >= 8:
                    pe.wait_ge(f_ready, t - 7)
                nc.tensor.matmul(PS[:, t % 8, :], h3[0:HD, t * P:(t + 1) * P], w4[0:HD, t // 8, :],
                                 start=True, stop=True).then_inc(f_mm, 1)
            pe.wait_ge(lf_ready, 1)

            def bank_free_h(t):
                if t >= 8:
                    pe.wait_ge(hs_ready, t - 7)

            def bank_free_z(t):
                if t < 8:
                    pe.wait_ge(hs_ready, 18)
                elif t % 2 == 0:
                    pe.wait_ge(zs_ready, t // 2 - 3)

            for n, name in enumerate(names):
                forward(pe, n, name, neg, hs_mm, bank_free_h)
            pe.wait_ge(zl_ready, 1)
            for n, name in enumerate(names):
                forward(pe, 5 + n, name, z, zs_mm, bank_free_z)
            job = 0
            for n, name in enumerate(names):
                kt, first, pairs = LEAVES[name]
                m = matrix(10 + n)
                freq = 2 * pairs
                out_tiles = m.shape[2] // P
                pe.wait_ge(mat_in[(10 + n) % 2], 16 * ((10 + n) // 2 + 1))
                pe.wait_ge(zs_ready, 9)
                if order_no == 0:
                    for i in range(out_tiles):
                        if job >= 8:
                            pe.wait_ge(iv_ready, job - 7)
                        for k in range(freq):
                            last = nc.tensor.matmul(PS[:, job % 8, :], m[:, k, i * P:(i + 1) * P], H[:, first + k, :],
                                                    start=(k == 0), stop=(k == freq - 1))
                        last.then_inc(iv_mm, 1)
                        job += 1
                else:
                    for c in range(4):
                        if job >= 8:
                            pe.wait_ge(iv_ready, job - 7)
                        for k in range(freq):
                            last = nc.tensor.matmul(PS[:, job % 8, 0:out_tiles * P], H[:, first + k, c * P:(c + 1) * P], m[:, k, :],
                                                    start=(k == 0), stop=(k == freq - 1))
                        last.then_inc(iv_mm, 1)
                        job += 1

        @block.scalar
        def _(act):
            t = 0
            for n, name in enumerate(names):
                for q in range(LEAVES[name][2]):
                    for dst in spectrum_pair(H, name, q):
                        act.wait_ge(hs_mm, t + 1)
                        nc.scalar.copy(dst, PS[:, t % 8, :]).then_inc(hs_ready, 1)
                        t += 1
            job = 0
            for n, name in enumerate(names):
                out_tiles = io["inv_" + name].shape[1] // P
                act.wait_ge(zs_ready, 9)
                for i in range(out_tiles if order_no == 0 else 4):
                    act.wait_ge(iv_mm, job + 1)
                    if order_no == 0:
                        nc.scalar.copy(rec_of[name][:, i, :], PS[:, job % 8, :]).then_inc(iv_ready, 1)
                    else:
                        dst = rec_of[name][:, :, i * P:(i + 1) * P]
                        nc.scalar.copy(dst, PS[:, job % 8, 0:out_tiles * P].rearrange("p (a b) -> p a b", b=P)).then_inc(iv_ready, 1)
                    job += 1

        @block.vector
        def _(dve):
            chain = Count(order)

            def link(ins, signal=chain):
                signal.by(ins)
                dve.wait_ge(signal.sem, signal.n)

            def total_and_difference(a, b):
                link(nc.vector.tensor_tensor(b, a, b, ALU.add))
                link(nc.vector.scalar_tensor_tensor(a, a, 2.0, b, ALU.mult, ALU.subtract))

            def split_negacyclic(v):
                total_and_difference(v[:, 2:4, :], v[:, 6:8, :])
                for lo, hi in ((0, 2), (4, 6)):
                    link(nc.vector.scalar_tensor_tensor(v[:, hi:hi + 2, :], v[:, hi:hi + 2, :], -R2, v[:, lo:lo + 2, :], ALU.mult, ALU.add))
                    link(nc.vector.scalar_tensor_tensor(v[:, lo:lo + 2, :], v[:, lo:lo + 2, :], 2.0, v[:, hi:hi + 2, :], ALU.mult, ALU.subtract))

            for t in range(16):
                dve.wait_ge(f_mm, t + 1)
                dve.wait_ge(dec_in[t % 4], 16 * (t // 4 + 1))
                dst = (neg if t < 8 else cyc)[:, t % 8, :]
                nc.vector.tensor_tensor(dst, PS[:, t % 8, :], dec[:, t % 4, :], ALU.mult).then_inc(f_ready, 1)
            dve.wait_ge(f_ready, 16)
            link(nc.vector.tensor_tensor(neg[0:1, 0, :], neg[0:1, 0, :], bias_row[0:1, :], ALU.add))
            total_and_difference(neg[:, :, :], cyc[:, :, :])
            total_and_difference(cyc[:, 0:4, :], cyc[:, 4:8, :])
            total_and_difference(cyc[:, 4:6, :], cyc[:, 6:8, :])
            split_negacyclic(neg)
            nc.vector.memset(tmp[:, 0, 0:1], 0.0).then_inc(lf_ready, 1)
            dve.wait_ge(hs_mm, 18)
            link(nc.vector.tensor_tensor(cyc[:, 0:4, :], z[:, 0:4, :], z[:, 4:8, :], ALU.subtract))
            link(nc.vector.tensor_tensor(cyc[:, 4:8, :], z[:, 0:4, :], z[:, 4:8, :], ALU.add))
            total_and_difference(cyc[:, 4:6, :], cyc[:, 6:8, :])
            split_negacyclic(z)
            nc.vector.memset(tmp[:, 0, 0:1], 0.0).then_inc(zl_ready, 1)
            dve.wait_ge(hs_ready, 18)
            pair = 0
            for name in names:
                kt, first, pairs = LEAVES[name]
                for q in range(pairs):
                    dve.wait_ge(zs_mm, first + 2 * q + 2)
                    if pair:
                        dve.wait_ge(zs_ready, pair)
                    pair += 1
                    t = first + 2 * q
                    hr, hi = spectrum_pair(H, name, q)
                    zr, zi = PS[:, t % 8, :], PS[:, (t + 1) % 8, :]
                    for dst, a, b in ((0, zr, hr), (1, zi, hi), (2, zr, hi)):
                        chain.by(nc.vector.tensor_tensor(tmp[:, dst, :], a, b, ALU.mult))
                    chain.by(nc.vector.tensor_tensor(tmp[:, 3, :], zi, hr, ALU.mult))
                    dve.wait_ge(order, chain.n)
                    chain.by(nc.vector.tensor_tensor(hr, tmp[:, 0, :], tmp[:, 1, :], ALU.subtract))
                    nc.vector.tensor_tensor(hi, tmp[:, 2, :], tmp[:, 3, :], ALU.add).then_inc(zs_ready, 1)
            Pm, Mm, Am, Bm = rec["P"], rec["M"], rec["A"], rec["B"]
            total_jobs = 16 if order_no == 0 else 20
            dve.wait_ge(iv_ready, total_jobs)
            total_and_difference(Pm, Mm)
            total_and_difference(Pm[:, 0:2, :], Pm[:, 2:4, :])
            link(nc.vector.tensor_tensor(Am[:, 0:2, :], Am[:, 0:2, :], Am[:, 2:4, :], ALU.add))
            link(nc.vector.scalar_tensor_tensor(Am[:, 2:4, :], Am[:, 2:4, :], 2.0, Am[:, 0:2, :], ALU.mult, ALU.subtract))
            total_and_difference(Am, Bm)
            y = z
            link(nc.vector.tensor_tensor(y[:, 0:2, :], Mm[:, 0:2, :], Bm[:, 0:2, :], ALU.add))
            link(nc.vector.scalar_tensor_tensor(y[:, 2:4, :], Pm[:, 2:4, :], R2, Bm[:, 2:4, :], ALU.mult, ALU.add))
            link(nc.vector.tensor_tensor(y[:, 4:6, :], Mm[:, 2:4, :], Am[:, 0:2, :], ALU.add))
            link(nc.vector.scalar_tensor_tensor(y[:, 6:8, :], Pm[:, 0:2, :], -R2, Am[:, 2:4, :], ALU.mult, ALU.add))
            if order_no == 0:
                link(nc.vector.tensor_tensor(z[:, :, :], z[:, :, :], x1t[:, :, :], ALU.mult))
            else:
                for c in range(4):
                    yc = y[:, :, c * P:(c + 1) * P]
                    dst = yT[:, c, :].rearrange("p (a b) -> p a b", b=P)
                    link(nc.vector.tensor_tensor(dst, yc, x2[:, c, :].rearrange("p (a b) -> p a b", b=P), ALU.mult))
                    link(nc.vector.tensor_tensor(yT[:, c, :], yT[:, c, :], ghy[:, c, :], ALU.mult))


def spectrum_pair(H, name, q):
    kt, first, pairs = LEAVES[name]
    return H[:, first + q, :], H[:, first + pairs + q, :]


YATT, YHY = ZV, X1T
SLOPES = [2.0 ** (-(h + 1)) for h in range(8)]
TILES = 10
UNITS = 32


def unit_kind(u):
    return u < 16, (u % 16) // 2, u % 2


def first_key(i):
    return min(max(P * i - 64, 0), S - 256)


V_TILES = ([(0, 0, 1), (0, 128, 1)] + [(0, 64 + P * m, 1) for m in range(7)] + [(0, 768, 1), (0, 896, 1)]
           + [(1, c + 512 * half, 4) for c in range(4) for half in range(2)] + [(2, r, 8) for r in range(8)])
V_GROUPS = [list(range(g, min(g + 4, len(V_TILES)))) for g in range(0, len(V_TILES), 4)]


def unit_blocks(u):
    strided, i, _ = unit_kind(u)
    if strided:
        return [V_TILES.index((1, i % 4, 4)), V_TILES.index((1, i % 4 + 512, 4)), V_TILES.index((2, i, 8))]
    return [V_TILES.index((0, first_key(i), 1)), V_TILES.index((0, first_key(i) + P, 1))]


def dilated_attention(K):
    nc, io, PS = K.nc, K.io, K.PS
    o = LF
    wt = K.at(o, 2, KT, P); o += 2 * 1024
    qk = K.at(o, 2, 6, S); o += 12 * S
    vT = K.at(o, 3, S); o += 3 * S
    gat = K.at(o, 2, S); o += 2 * S
    vrows = K.at(o, 27, P); o += 27 * P
    dist = K.at(o, 1536); o += 1536
    bias = K.at(o, 2, 1536); o += 3072
    sb = K.at(o, 3, 384); o += 3 * 384
    st_b = K.at(o, 8, 2, 66); o += 1056
    outs = K.at(o, NT, P); o += NT * P
    back = K.at(o, 8, 2, 66); o += 1056
    o = H3
    pt = K.at(o, 2, 384); o += 768
    st_a = K.at(o, 8, 2, 66); o += 1056
    nm = K.at(o, 4); o += 4
    mx = K.at(o, 16); o += 16
    ex = K.at(o, 2, 16); o += 32
    den = K.at(o, 16); o += 16
    assert o <= FREE1
    yT, hT, cols1, ident = K.at(YATT, 4, S), K.at(HT, KT, S), K.at(COLS1, N_COLS1), K.at(IDENT, P)
    w = io["w_in"][0].rearrange("(k p) n -> p k n", p=P)
    scratch = nc.dram_tensor("strided_sums", (S, 132), fp32, kind="Internal").ap()
    pairs = 4
    halves = 2 * TILES

    def tile_column(T):
        j, t = T // TILES, T % TILES
        return (36 + j) if t == 9 else (t // 3) * 12 + (t % 3) * 4 + j

    def dest(T):
        j, t = T // TILES, T % TILES
        return gat[:, j % 2, :] if t == 9 else (vT[:, t - 6, :] if t >= 6 else qk[:, j % 2, t, :])

    def projections(j):
        after = [[] for _ in range(UNITS + 1)]
        if j + 1 < pairs:
            for n in range(halves):
                after[min(2 * n, UNITS) if n < 16 else UNITS].append((j + 1) * halves + n)
        return after

    def bank_of_t(j, n):
        g = j * 41 + n
        return g, 2 + g % 2

    with ExitStack() as ctx:
        s = lambda n: K.sem(ctx, "da_" + n)
        w_in, dist_in = [s(f"w_in{b}") for b in range(2)], s("dist_in")
        proj_mm, proj_ready, order = s("proj_mm"), s("proj_ready"), s("order")
        t_done, t_taken, bias_ready = s("t_done"), s("t_taken"), s("bias")
        s_done, s_taken, nm_ready, exp_done, pv_done, o_ready = s("s_done"), s("s_taken"), s("nm"), s("exp"), s("pv"), s("o")
        sums_out, sums_in, comb_d, comb_e, comb_done, y_ready = s("sums_out"), s("sums_in"), s("comb_d"), s("comb_e"), s("comb"), s("y")
        block = ctx.enter_context(nc.Block())

        @block.sync
        def _(sp):
            sp.dma_start(dist, io["dist"]).then_inc(dist_in, 16)

            def load(T):
                if T >= 2:
                    sp.wait_ge(proj_mm, 2 * (T - 1))
                c0 = tile_column(T) * P
                sp.dma_start(wt[:, T % 2, :, :], w[:, :, c0:c0 + P]).then_inc(w_in[T % 2], 16)

            for T in range(TILES * pairs):
                load(T)

        @block.gpsimd
        def _(pool):
            for j in range(pairs):
                pool.wait_ge(o_ready, UNITS * j + 16)
                pool.dma_start(scratch.rearrange("(n r) c -> n r c", r=8), st_b.rearrange("p r h c -> p r (h c)")).then_inc(sums_out, 16)
                pool.wait_ge(sums_out, 16 * (j + 1))
                if j >= 1:
                    pool.wait_ge(comb_done, j)
                pool.dma_start(back.rearrange("p r h c -> p r (h c)"), scratch.rearrange("(i p) c -> p i c", p=P)).then_inc(sums_in, 16)

        @block.tensor
        def _(pe):
            def project(n):
                T, h = n // 2, n % 2
                pe.wait_ge(w_in[T % 2], 16 * (T // 2 + 1))
                if n >= 2:
                    pe.wait_ge(proj_ready, n - 1)
                for k in range(KT):
                    last = nc.tensor.matmul(PS[:, 6 + h, :], wt[:, T % 2, k, :], hT[:, k, h * 512:(h + 1) * 512],
                                            start=(k == 0), stop=(k == KT - 1))
                last.then_inc(proj_mm, 1)

            def transposes(j, n, sources):
                g, b = bank_of_t(j, n)
                if g >= 2:
                    pe.wait_ge(t_taken, g - 1)
                for i, src in enumerate(sources):
                    last = nc.tensor.transpose(PS[:, b, i * P:(i + 1) * P], src, ident)
                last.then_inc(t_done, 1)

            def scores(j, u):
                U = UNITS * j + u
                strided, i, h = unit_kind(u)
                if U >= 2:
                    pe.wait_ge(s_taken, U - 1)
                head = slice(64 * h, 64 * h + 64)
                q = lambda g: qk[head, j % 2, g, :]
                k = lambda g: qk[head, j % 2, 3 + g, :]
                b = PS[:, U % 2, :]
                if strided:
                    nc.tensor.matmul(b[:, 0:256], q(1)[:, i:S:8], k(1)[:, i % 4:S:4], start=True, stop=True)
                    last = nc.tensor.matmul(b[:, 256:384], q(2)[:, i:S:8], k(2)[:, i:S:8], start=True, stop=True)
                else:
                    k0 = first_key(i)
                    last = nc.tensor.matmul(b[:, 0:256], q(0)[:, i * P:(i + 1) * P], k(0)[:, k0:k0 + 256], start=True, stop=True)
                last.then_inc(s_done, 1)

            def prob_transposes(j, u):
                U = UNITS * j + u
                pe.wait_ge(exp_done, U + 1)
                transposes(j, 7 + u, [sb[:, U % 3, b * P:(b + 1) * P] for b in range(len(unit_blocks(u)))])

            def values(j, u):
                U = UNITS * j + u
                _, _, h = unit_kind(u)
                pe.wait_ge(t_taken, bank_of_t(j, 7 + u)[0] + 1)
                if U >= 2:
                    pe.wait_ge(o_ready, U - 1)
                blocks = unit_blocks(u)
                for b, v in enumerate(blocks):
                    last = nc.tensor.matmul(PS[:, 4 + U % 2, 0:HD], pt[:, U % 2, b * P:(b + 1) * P], vrows[:, v, h * HD:(h + 1) * HD],
                                            start=(b == 0), stop=(b == len(blocks) - 1))
                last.then_inc(pv_done, 1)

            for n in range(halves):
                project(n)
            for j in range(pairs):
                pe.wait_ge(proj_ready, halves * (j + 1))
                for g, tiles in enumerate(V_GROUPS):
                    transposes(j, g, [vT[:, V_TILES[v][0], V_TILES[v][1]:V_TILES[v][1] + P * V_TILES[v][2] - V_TILES[v][2] + 1:V_TILES[v][2]] for v in tiles])
                extra = projections(j)
                for u in range(UNITS + 2):
                    if u < UNITS:
                        scores(j, u)
                        for n in extra[u]:
                            project(n)
                    if 1 <= u <= UNITS:
                        prob_transposes(j, u - 1)
                    if u >= 2:
                        values(j, u - 2)
                for n in extra[UNITS]:
                    project(n)
                pe.wait_ge(comb_done, j + 1)
                for g in range(2):
                    transposes(j, 39 + g, [outs[:, i, :] for i in range(4 * g, 4 * g + 4)])

        @block.scalar
        def _(act):
            def take_projection(n):
                T, h = n // 2, n % 2
                t = T % TILES
                act.wait_ge(proj_mm, n + 1)
                if t == 9 and T // TILES >= 2:
                    act.wait_ge(y_ready, T // TILES - 1)
                c = tile_column(T)
                nc.scalar.activation(dest(T)[:, h * 512:(h + 1) * 512], PS[:, 6 + h, :], ACT.Silu if t == 9 else ACT.Identity,
                                     bias=cols1[:, c:c + 1]).then_inc(proj_ready, 1)

            def stats_of(u):
                strided, i, h = unit_kind(u)
                return (st_b if strided else st_a)[:, i, h, :]

            def exponentials(j, u):
                U = UNITS * j + u
                n = 384 if unit_kind(u)[0] else 256
                act.wait_ge(nm_ready, U + 1)
                nc.scalar.activation(sb[:, U % 3, 0:n], sb[:, U % 3, 0:n], ACT.Exp, bias=nm[:, U % 4:U % 4 + 1], scale=0.125,
                                     accum_out=stats_of(u)[:, 64:65]).then_inc(exp_done, 1)

            def take_output(j, u):
                U = UNITS * j + u
                act.wait_ge(pv_done, U + 1)
                nc.scalar.copy(stats_of(u)[:, 0:HD], PS[:, 4 + U % 2, 0:HD]).then_inc(o_ready, 1)

            for n in range(halves):
                take_projection(n)
            for j in range(pairs):
                if j >= 1:
                    act.wait_ge(sums_out, 16 * j)
                    act.wait_ge(comb_done, j)
                extra = projections(j)
                for u in range(UNITS + 2):
                    if u < UNITS:
                        exponentials(j, u)
                        for n in extra[u]:
                            take_projection(n)
                    if u >= 2:
                        take_output(j, u - 2)
                act.wait_ge(comb_d, j + 1)
                nc.scalar.activation(ex, ex, ACT.Exp, scale=0.125).then_inc(comb_e, 1)
                for n in extra[UNITS]:
                    take_projection(n)

        @block.vector
        def _(dve):
            chain = Count(order)
            done = Count(comb_done)
            diff = Count(comb_d)

            def link(ins, signal=chain):
                signal.by(ins)
                dve.wait_ge(signal.sem, signal.n)

            def take_scores(j, u):
                U = UNITS * j + u
                strided, i, h = unit_kind(u)
                n = 384 if strided else 256
                col = 768 + 384 * (i // 4) if strided else 256 * (0 if i == 0 else 2 if i == NT - 1 else 1)
                st = (st_b if strided else st_a)[:, i, h, :]
                dve.wait_ge(s_done, U + 1)
                if U >= 3:
                    dve.wait_ge(t_done, bank_of_t((U - 3) // UNITS, 7 + (U - 3) % UNITS)[0] + 1)
                nc.vector.tensor_tensor_reduce(out=sb[:, U % 3, 0:n], in0=PS[:, U % 2, 0:n], in1=bias[:, h, col:col + n],
                                               scale=1.0, scalar=-3e38, op0=ALU.add, op1=ALU.max, accum_out=st[:, 65:66]).then_inc(s_taken, 1)
                dve.wait_ge(s_taken, U + 1)
                nc.vector.tensor_scalar(nm[:, U % 4:U % 4 + 1], st[:, 65:66], -0.125, None, ALU.mult).then_inc(nm_ready, 1)

            def take_transposes(j, n, dst, wait=None):
                g, b = bank_of_t(j, n)
                dve.wait_ge(t_done, g + 1)
                cols = dst.shape[1] * (dst.shape[2] if len(dst.shape) == 3 else 1)
                src = PS[:, b, 0:cols]
                if len(dst.shape) == 3:
                    src = src.rearrange("p (a b) -> p a b", a=dst.shape[1])
                return src

            for j in range(pairs):
                if j == 0:
                    dve.wait_ge(dist_in, 16)
                else:
                    dve.wait_ge(s_taken, UNITS * j)
                for h in range(2):
                    link(nc.vector.tensor_scalar(bias[:, h, :], dist, -8.0 * SLOPES[2 * j + h], None, ALU.mult))
                for g, tiles in enumerate(V_GROUPS):
                    dst = vrows[:, tiles[0]:tiles[-1] + 1, :]
                    nc.vector.tensor_copy(dst, take_transposes(j, g, dst)).then_inc(t_taken, 1)
                if j >= 1:
                    dve.wait_ge(sums_out, 16 * j)
                for u in range(UNITS + 1):
                    if u < UNITS:
                        take_scores(j, u)
                    if u >= 1:
                        U = UNITS * j + u - 1
                        if U >= 2:
                            dve.wait_ge(pv_done, U - 1)
                        n = 384 if unit_kind(u - 1)[0] else 256
                        dst = pt[:, U % 2, 0:n]
                        nc.vector.tensor_copy(dst, take_transposes(j, 6 + u, dst)).then_inc(t_taken, 1)
                dve.wait_ge(o_ready, UNITS * (j + 1))
                dve.wait_ge(sums_in, 16 * (j + 1))
                pick = lambda st, c: st[:, :, :, c:c + 1].rearrange("p r h c -> p (r h) c")[:, :, 0]
                link(nc.vector.tensor_tensor(mx, pick(st_a, 65), pick(back, 65), ALU.max))
                link(nc.vector.tensor_tensor(ex[:, 0, :], pick(st_a, 65), mx, ALU.subtract))
                link(nc.vector.tensor_tensor(ex[:, 1, :], pick(back, 65), mx, ALU.subtract), diff)
                dve.wait_ge(comb_e, j + 1)
                link(nc.vector.tensor_tensor(mx, pick(st_a, 64), ex[:, 0, :], ALU.mult))
                link(nc.vector.tensor_tensor(den, pick(back, 64), ex[:, 1, :], ALU.mult))
                link(nc.vector.tensor_tensor(den, den, mx, ALU.add))
                link(nc.vector.reciprocal(den, den))
                for n in range(2):
                    link(nc.vector.tensor_tensor(ex[:, n, :], ex[:, n, :], den, ALU.mult))
                for n, st in enumerate((st_a, back)):
                    v = st[:, :, :, 0:HD].rearrange("p r h c -> p (r h) c")
                    link(nc.vector.tensor_tensor(v, v, ex[:, n, :].unsqueeze(2).to_broadcast([P, 16, HD]), ALU.mult))
                    if n == 1:
                        link(nc.vector.tensor_tensor(outs.rearrange("p r (h c) -> p (r h) c", h=2), v,
                                                     st_a[:, :, :, 0:HD].rearrange("p r h c -> p (r h) c"), ALU.add), done)
                for g in range(2):
                    dst = yT[:, j, g * 512:(g + 1) * 512]
                    ins = nc.vector.tensor_tensor(dst, take_transposes(j, 39 + g, dst), gat[:, j % 2, g * 512:(g + 1) * 512], ALU.mult)
                    ins.then_inc(t_taken, 1)
                dve.wait_ge(t_taken, bank_of_t(j, 40)[0] + 1)
                nc.vector.memset(mx[:, 0:1], 0.0).then_inc(y_ready, 1)


WPROJ = LF
MERGED = 34176
WOUT = MERGED + 8192


def merge_branches(K):
    nc, io, PS = K.nc, K.io, K.PS
    wp = K.at(WPROJ, 2, 4, D)
    wr = K.at(WPROJ + 8192, 2, 2, KT, P)
    tmp = K.at(WPROJ + 8192 + 4096, 2, 2, 512)
    sg = K.at(H3, 2, 2, 512)
    hT, cols1, merged, wout = K.at(HT, KT, S), K.at(COLS1, N_COLS1), K.at(MERGED, KT, S), K.at(WOUT, KT, D)
    branch = [K.at(YATT, 4, S), K.at(YHY, 4, S)]
    w = io["w_in"][0].rearrange("(k p) n -> p k n", p=P)
    with ExitStack() as ctx:
        s = lambda n: K.sem(ctx, "mg_" + n)
        w_in, wp_in, wout_in = [s("w_in0"), s("w_in1")], s("wp_in"), s("wout_in")
        r_mm, y_mm, sig_ready, merged_ready, order = s("r_mm"), s("y_mm"), s("sig"), s("merged"), s("order")
        block = ctx.enter_context(nc.Block())

        @block.sync
        def _(sp):
            def load(k):
                if k >= 2:
                    sp.wait_ge(r_mm, 2 * (k - 1))
                for a in range(2):
                    c0 = COL_R + a * D + k * P
                    sp.dma_start(wr[:, k % 2, a, :, :], w[:, :, c0:c0 + P]).then_inc(w_in[k % 2], 16)

            load(0)
            for a, name in enumerate(("w_proj_attn", "w_proj_hyena")):
                sp.dma_start(wp[:, a, :, :], io[name][0].rearrange("(k p) n -> p k n", p=P)).then_inc(wp_in, 16)
            load(1)
            sp.dma_start(wout, io["w_out"][0].rearrange("(k p) n -> p k n", p=P)).then_inc(wout_in, 16)
            for k in range(2, KT):
                load(k)
            sp.wait_ge(wout_in, 16)

        @block.tensor
        def _(pe):
            for k in range(KT):
                pe.wait_ge(w_in[k % 2], 32 * (k // 2 + 1))
                for h in range(2):
                    n = 2 * k + h
                    b = 4 * (n % 2)
                    if n >= 2:
                        pe.wait_ge(sig_ready, n - 1)
                    for a in range(2):
                        for c in range(KT):
                            last = nc.tensor.matmul(PS[:, b + a, :], wr[:, k % 2, a, c, :], hT[:, c, h * 512:(h + 1) * 512],
                                                    start=(c == 0), stop=(c == KT - 1))
                    last.then_inc(r_mm, 1)
                    if n == 0:
                        pe.wait_ge(wp_in, 32)
                    if n >= 2:
                        pe.wait_ge(merged_ready, n - 1)
                    for a in range(2):
                        for c in range(4):
                            last = nc.tensor.matmul(PS[:, b + 2 + a, :], wp[:, a, c, k * P:(k + 1) * P], branch[a][:, c, h * 512:(h + 1) * 512],
                                                    start=(c == 0), stop=(c == 3))
                    last.then_inc(y_mm, 1)

        @block.scalar
        def _(act):
            for n in range(2 * KT):
                k = n // 2
                act.wait_ge(r_mm, n + 1)
                if n >= 2:
                    act.wait_ge(merged_ready, n - 1)
                for a in range(2):
                    col = COL_R // P + 8 * a + k
                    last = nc.scalar.activation(sg[:, n % 2, a, :], PS[:, 4 * (n % 2) + a, :], ACT.Sigmoid, bias=cols1[:, col:col + 1])
                last.then_inc(sig_ready, 1)

        @block.vector
        def _(dve):
            chain = Count(order)

            def link(ins, signal=chain):
                signal.by(ins)
                dve.wait_ge(signal.sem, signal.n)

            for n in range(2 * KT):
                k, h, b = n // 2, n % 2, 4 * (n % 2)
                dve.wait_ge(sig_ready, n + 1)
                dve.wait_ge(y_mm, n + 1)
                for a in range(2):
                    last = nc.vector.tensor_tensor(tmp[:, n % 2, a, :], PS[:, b + 2 + a, :], sg[:, n % 2, a, :], ALU.mult)
                link(last)
                nc.vector.tensor_tensor(merged[:, k, h * 512:(h + 1) * 512], tmp[:, n % 2, 0, :], tmp[:, n % 2, 1, :], ALU.add).then_inc(merged_ready, 1)


VECS = 1408 + 64
X2T = 11648
X2R = X2T + 8192


class RowNorm:

    def __init__(self, nc, dve, link, stat, var_signal, std_sem):
        self.nc, self.dve, self.link, self.stat, self.var, self.std = nc, dve, link, stat, var_signal, std_sem

    def __call__(self, row, gamma, beta, final=None):
        nc, st = self.nc, self.stat
        self.link(nc.vector.bn_stats(st[:, 0:6], row[:, 0:512]))
        self.link(nc.vector.bn_stats(st[:, 6:12], row[:, 512:1024]))
        self.link(nc.vector.bn_aggr(st[:, 12:14], st[:, 0:12]))
        self.link(nc.vector.tensor_scalar(st[:, 14:15], st[:, 13:14], 1e-5, None, ALU.add), self.var)
        self.dve.wait_ge(self.std, self.var.n)
        self.link(nc.vector.reciprocal(st[:, 15:16], st[:, 15:16]))
        self.link(nc.vector.tensor_scalar(row, row, st[:, 12:13], st[:, 15:16], ALU.subtract, ALU.mult))
        self.link(nc.vector.tensor_tensor(row, row, gamma, ALU.mult))
        self.link(nc.vector.tensor_tensor(row, row, beta, ALU.add), *([final] if final else []))


def first_output(K):
    nc, io, PS = K.nc, K.io, K.PS
    vec = K.at(VECS, 5, D)
    xin = K.at(VECS + 5 * D, 2, D)
    work = K.at(VECS + 7 * D, 2, D)
    stat = K.at(28032, 16)
    gate, merged, wout, ident = K.at(GATE, D), K.at(MERGED, KT, S), K.at(WOUT, KT, D), K.at(IDENT, P)
    x2r, x2T = K.at(X2R, NT, D), K.at(X2T, KT, S)
    x_class = io["x"][0].rearrange("(n r) d -> n r d", r=8)
    with ExitStack() as ctx:
        s = lambda n: K.sem(ctx, "fo_" + n)
        x_in, vec_in, mm, t_read, x_used, order = [s("x_in0"), s("x_in1")], s("vec_in"), s("mm"), s("t_read"), s("x_used"), s("order")
        var, std, row_ready, tr, tr_taken, gated = s("var"), s("std"), s("row"), s("tr"), s("tr_taken"), s("gated")
        block = ctx.enter_context(nc.Block())

        @block.sync
        def _(sp):
            for n, v in enumerate((io["b_out"][0], io["ln_g"][0], io["ln_b"][0], io["ln_emb_g_2"], io["ln_emb_b_2"])):
                sp.dma_start(vec[:, n, :], bcast_rows(v)).then_inc(vec_in, 16)
            for r in range(NT):
                if r >= 2:
                    sp.wait_ge(x_used, r - 1)
                sp.dma_start(xin[:, r % 2, :], x_class[:, r, :]).then_inc(x_in[r % 2], 16)

        @block.tensor
        def _(pe):
            def out_rows(r):
                if r >= 2:
                    pe.wait_ge(t_read, r - 1)
                for h in range(2):
                    for k in range(KT):
                        last = nc.tensor.matmul(PS[:, 2 * (r % 2) + h, :], merged[:, k, r:S:8], wout[:, k, h * 512:(h + 1) * 512],
                                                start=(k == 0), stop=(k == KT - 1))
                last.then_inc(mm, 1)

            def to_columns(r):
                pe.wait_ge(row_ready, r + 1)
                for g in range(2):
                    n = 2 * r + g
                    if n >= 4:
                        pe.wait_ge(tr_taken, n - 3)
                    for i in range(4):
                        k = 4 * g + i
                        last = nc.tensor.transpose(PS[:, 4 + n % 4, i * P:(i + 1) * P], x2r[:, r, k * P:(k + 1) * P], ident)
                    last.then_inc(tr, 1)

            for r in range(NT):
                out_rows(r)
                if r >= 1:
                    to_columns(r - 1)
            to_columns(NT - 1)

        @block.scalar
        def _(act):
            def take_columns(r):
                for g in range(2):
                    n = 2 * r + g
                    act.wait_ge(tr, n + 1)
                    nc.scalar.copy(x2T[:, 4 * g:4 * g + 4, r:S:8], PS[:, 4 + n % 4, :].rearrange("p (a b) -> p a b", b=P)).then_inc(tr_taken, 1)

            for r in range(NT):
                for n in range(2 * r, 2 * r + 2):
                    act.wait_ge(var, n + 1)
                    nc.scalar.activation(stat[:, 15:16], stat[:, 14:15], ACT.Sqrt).then_inc(std, 1)
                if r >= 1:
                    take_columns(r - 1)
            take_columns(NT - 1)

        @block.gpsimd
        def _(pool):
            for r in range(NT):
                pool.wait_ge(t_read, r + 1)
                nc.gpsimd.tensor_tensor(work[:, r % 2, :], work[:, r % 2, :], gate, ALU.mult).then_inc(gated, 1)

        @block.vector
        def _(dve):
            chain = Count(order)

            def link(ins, signal=chain):
                signal.by(ins)
                dve.wait_ge(signal.sem, signal.n)

            norm = RowNorm(nc, dve, link, stat, Count(var), std)
            rows, used, read = Count(row_ready), Count(x_used), Count(t_read)
            dve.wait_ge(vec_in, 80)
            for r in range(NT):
                dve.wait_ge(mm, r + 1)
                src = PS[:, 2 * (r % 2):2 * (r % 2) + 2, :].rearrange("p a b -> p (a b)")
                link(nc.vector.tensor_tensor(work[:, r % 2, :], src, vec[:, 0, :], ALU.add), read)
                dve.wait_ge(gated, r + 1)
                dve.wait_ge(x_in[r % 2], 16 * (r // 2 + 1))
                row = x2r[:, r, :]
                link(nc.vector.scalar_tensor_tensor(row, xin[:, r % 2, :], ALPHA, work[:, r % 2, :], ALU.mult, ALU.add), used)
                norm(row, vec[:, 1, :], vec[:, 2, :])
                norm(row, vec[:, 3, :], vec[:, 4, :], rows)


XS = VECS
QTAP = XS + 4096
S5S = QTAP + 4608
S5T = 28032
S5W, S5M, S5U, S5G, S5TMP = S5T + 4096, S5T + 8192, S5T + 12288, S5T + 16384, S5T + 20480
S5B = S5TMP + 2048
TC = 8
NCH = S // TC


def s5_states(K):
    nc, io, PS = K.nc, K.io, K.PS
    ident, cols2, x2T = K.at(IDENT, P), K.at(COLS2, 64), K.at(X2T, KT, S)
    xs = K.at(XS, 32, TC, 16)
    yg = K.at(S5T, TC, CH)
    QR, QN = K.at(QTAP, 16, 9, 16), K.at(QTAP + 2304, 16, 9, 16)
    Tc, Ts = K.at(S5T, 16, NCH), K.at(S5T + 2048, 16, NCH)
    W = K.at(S5W, 16, 2, P)
    M, U = K.at(S5M, 2, 16, P), K.at(S5U, 2, 16, P)
    WTr, WTi = K.at(S5M, 16, 8, 16), K.at(S5M + 2048, 16, 8, 16)
    wxs, Ksb = K.at(S5G, KT, CH), K.at(S5G, 2, 16, P)
    G = [K.at(S5G, 16, NCH), K.at(S5G + 2048, 16, NCH)]
    tmp = K.at(S5TMP, 4, 4, NCH)
    braw = K.at(S5TMP, 2, 16, 16)
    craw = K.at(S5W, 2, 4, P)
    kB, C = K.at(S5B, 2, 16, 16), K.at(S5B + 512, 2, 16, 16)
    pw, rev = K.at(S5B + 1024, 2, 9, 16), K.at(S5B + 1312, 2, 8, 16)
    o = S5S
    dskip = K.at(o, CH); o += CH
    ldt = K.at(o, 32); o += 32
    names = ("dt", "arg", "magarg", "kk", "sn", "cs", "mag", "rho", "den", "nr", "kre", "kim", "ta", "tb", "abre", "abim", "s8", "c8", "arg2", "argc")
    v = {}
    for n in names:
        v[n] = K.at(o, 16); o += 16
    args = K.at(o, 4, 16); o += 64
    trig = K.at(o, 4, 16); o += 64
    assert o <= X2T
    are, aim = cols2[:, 0:16], cols2[:, 16:32]
    over_c = lambda a: a.unsqueeze(2).to_broadcast([P, 16, 16])
    with ExitStack() as ctx:
        s = lambda n: K.sem(ctx, "s5_" + n)
        wxs_in, dt_in, b_in, c_in, ds_in = s("wxs_in"), s("dt_in"), s("b_in"), s("c_in"), s("ds_in")
        order, aorder = s("order"), s("aorder")
        c_tr, c_ready, xs_mm, xs_ready, u_tr, u_ready = s("c_tr"), s("c_ready"), s("xs_mm"), s("xs_ready"), s("u_tr"), s("u_ready")
        dt_ready, arg_ready, trig_ready = s("dt"), s("arg"), s("trig")
        wt_ready, w_tr, w_ready, kb_ready, k_mm, k_ready, m_clear, toeplitz = s("wt"), s("w_tr"), s("w"), s("kb"), s("k_mm"), s("k"), s("m_clear"), s("toeplitz")
        v_mm, v_read, h_ready, y_mm, y_ready, gelu_done = s("v_mm"), s("v_read"), s("h"), s("y_mm"), s("y"), s("gelu")
        block = ctx.enter_context(nc.Block())

        @block.sync
        def _(sp):
            sp.dma_start(ldt, bcast_rows(io["log_dt_2"][0])).then_inc(dt_in, 16)
            for n, name in enumerate(("b_re_2", "b_im_2")):
                sp.dma_start(braw[:, n, :, :], io[name][0].rearrange("(j g) p c -> (g p) j c", g=2)).then_inc(b_in, 16)
            for n, name in enumerate(("c_re_2", "c_im_2")):
                rows = io[name][0].rearrange("(q g) c p -> (g c) q p", q=4)
                for dup in range(2):
                    sp.dma_start(craw[:, n, :, dup * 64:dup * 64 + 64], rows).then_inc(c_in, 16)
            sp.dma_start(wxs, io["w_in_2"][0, :, 0:CH].rearrange("(k p) n -> p k n", p=P)).then_inc(wxs_in, 16)
            sp.dma_start(dskip, bcast_rows(io["d_skip_2"][0])).then_inc(ds_in, 16)
            sp.wait_ge(k_ready, 8)
            sp.wait_ge(m_clear, 1)
            for t in range(TC):
                sp.dma_start(M[16 * t:16 * t + 16, :, :, 16 * t:P], Ksb[0:16, :, :, 0:P - 16 * t]).then_inc(toeplitz, 16)

        @block.gpsimd
        def _(pool):
            pool.wait_ge(w_tr, 8)
            nc.gpsimd.memset(K.at(S5M, 4096), 0.0).then_inc(m_clear, 1)

        @block.tensor
        def _(pe):
            pe.wait_ge(c_in, 64)
            for n in range(2):
                for q in range(4):
                    last = nc.tensor.transpose(PS[:, 6 + n, q * P:(q + 1) * P], craw[:, n, q, :], ident)
            last.then_inc(c_tr, 1)
            pe.wait_ge(wxs_in, 16)
            for t in range(TC):
                if t >= 6:
                    pe.wait_ge(xs_ready, t - 5)
                for k in range(KT):
                    last = nc.tensor.matmul(PS[:, t % 6, :], x2T[:, k, t:S:TC], wxs[:, k, :], start=(k == 0), stop=(k == KT - 1))
                last.then_inc(xs_mm, 1)
            pe.wait_ge(xs_ready, TC)
            pe.wait_ge(c_ready, 1)
            for n in range(8):
                q, g2 = n // 2, n % 2
                for i in range(4):
                    g = 2 * (4 * q + i) + g2
                    last = nc.tensor.transpose(PS[:, n, i * P:(i + 1) * P], xs[:, g, :, :], ident)
                last.then_inc(u_tr, 1)
            pe.wait_ge(wt_ready, 1)
            for n in range(8):
                pe.wait_ge(u_ready, n + 1)
                q, ri = n // 2, n % 2
                for i in range(4):
                    last = nc.tensor.transpose(PS[:, n, i * P:(i + 1) * P], (WTr, WTi)[ri][:, 4 * q + i, :, :], ident)
                last.then_inc(w_tr, 1)
            pe.wait_ge(kb_ready, 1)
            for n in range(8):
                pe.wait_ge(w_ready, n + 1)
                q, g2 = n // 2, n % 2
                half = slice(64 * g2, 64 * g2 + 64)
                for i in range(4):
                    j = 4 * q + i
                    nc.tensor.matmul(PS[0:16, n, i * P:(i + 1) * P], kB[half, 0, j, :], QR[half, j, 0:8, :], start=True, stop=False)
                    last = nc.tensor.matmul(PS[0:16, n, i * P:(i + 1) * P], kB[half, 1, j, :], QN[half, j, 0:8, :], start=False, stop=True)
                last.then_inc(k_mm, 1)
            for n in range(8):
                pe.wait_ge(k_ready, n + 1)
                q, ri = n // 2, n % 2
                for i in range(4):
                    j = 4 * q + i
                    for g2 in range(2):
                        half = slice(64 * g2, 64 * g2 + 64)
                        last = nc.tensor.matmul(PS[half, n, i * P:(i + 1) * P], W[:, j, ri, half], U[:, g2, j, :], start=True, stop=True)
                last.then_inc(v_mm, 1)
            pe.wait_ge(toeplitz, 16 * TC)
            for n in range(8):
                q, g2 = n // 2, n % 2
                pe.wait_ge(v_read, 4)
                pe.wait_ge(h_ready, q + 1)
                half = slice(64 * g2, 64 * g2 + 64)
                for i in range(4):
                    j = 4 * q + i
                    out = PS[:, n, i * P:(i + 1) * P]
                    nc.tensor.matmul(out, U[:, g2, j, :], M[:, g2, j, :], start=True, stop=False)
                    nc.tensor.matmul(out, G[0][half, j, :], QR[half, j, 1:9, :], start=False, stop=False)
                    last = nc.tensor.matmul(out, G[1][half, j, :], QN[half, j, 1:9, :], start=False, stop=True)
                last.then_inc(y_mm, 1)

        @block.scalar
        def _(act):
            act.wait_ge(dt_ready, 1)
            nc.scalar.activation(v["dt"], v["dt"], ACT.Exp).then_inc(aorder, 1)
            act.wait_ge(arg_ready, 1)
            nc.scalar.activation(v["mag"], v["magarg"], ACT.Exp)
            nc.scalar.activation(v["rho"], v["magarg"], ACT.Exp, scale=float(TC))
            nc.scalar.activation(trig, args, ACT.Sin).then_inc(trig_ready, 1)
            for t in range(TC):
                act.wait_ge(xs_mm, t + 1)
                nc.scalar.copy(xs[:, :, t, :], PS[:, t % 6, :].rearrange("p (g c) -> p g c", c=16)).then_inc(xs_ready, 1)
            act.wait_ge(c_tr, 1)
            for n in range(8):
                act.wait_ge(u_tr, n + 1)
                nc.scalar.copy(U[:, n % 2, 4 * (n // 2):4 * (n // 2) + 4, :], PS[:, n, :].rearrange("p (a b) -> p a b", b=P)).then_inc(u_ready, 1)
            for n in range(8):
                act.wait_ge(w_tr, n + 1)
                nc.scalar.copy(W[:, 4 * (n // 2):4 * (n // 2) + 4, n % 2, :], PS[:, n, :].rearrange("p (a b) -> p a b", b=P)).then_inc(w_ready, 1)
            for n in range(8):
                act.wait_ge(k_mm, n + 1)
                nc.scalar.copy(Ksb[0:16, n % 2, 4 * (n // 2):4 * (n // 2) + 4, :], PS[0:16, n, :].rearrange("p (a b) -> p a b", b=P)).then_inc(k_ready, 1)
            for q in range(4):
                act.wait_ge(y_ready, 2 * q + 2)
                nc.scalar.activation(yg[:, :, q * P:(q + 1) * P].rearrange("p t (g c) -> p g t c", c=16), xs[:, 8 * q:8 * q + 8, :, :],
                                     ACT.Gelu_apprx_tanh).then_inc(gelu_done, 1)

        @block.vector
        def _(dve):
            chain = Count(order)

            def link(ins, signal=chain):
                signal.by(ins)
                dve.wait_ge(signal.sem, signal.n)

            def tt(out, a, b, op, signal=chain):
                link(nc.vector.tensor_tensor(out, a, b, op), signal)

            dve.wait_ge(dt_in, 16)
            nc.vector.tensor_copy(v["dt"][0:64, :], ldt[0:64, 0:32:2])
            link(nc.vector.tensor_copy(v["dt"][64:128, :], ldt[64:128, 1:32:2]), Count(dt_ready))
            dve.wait_ge(aorder, 1)
            tt(v["magarg"], v["dt"], are, ALU.mult)
            tt(v["arg"], v["dt"], aim, ALU.mult)
            link(nc.vector.tensor_scalar(v["arg2"], v["arg"], float(TC), None, ALU.mult))
            for n, (src, quarter) in enumerate(((v["arg"], 0.0), (v["arg"], 0.25), (v["arg2"], 0.0), (v["arg2"], 0.25))):
                reduced_sine_argument(nc, link, args[:, n, :], src, v["kk"], quarter)
            link(nc.vector.memset(v["ta"], 0.0), Count(arg_ready))
            dve.wait_ge(trig_ready, 1)
            sn, cs = trig[:, 0, :], trig[:, 1, :]
            tt(v["abre"], v["mag"], cs, ALU.mult)
            tt(v["abim"], v["mag"], sn, ALU.mult)
            tt(v["den"], are, are, ALU.mult)
            tt(v["ta"], aim, aim, ALU.mult)
            tt(v["den"], v["den"], v["ta"], ALU.add)
            link(nc.vector.reciprocal(v["den"], v["den"]))
            link(nc.vector.tensor_scalar(v["nr"], v["abre"], 1.0, None, ALU.subtract))
            tt(v["ta"], v["nr"], are, ALU.mult)
            tt(v["tb"], v["abim"], aim, ALU.mult)
            tt(v["kre"], v["ta"], v["tb"], ALU.add)
            tt(v["kre"], v["kre"], v["den"], ALU.mult)
            tt(v["ta"], v["abim"], are, ALU.mult)
            tt(v["tb"], v["nr"], aim, ALU.mult)
            tt(v["kim"], v["ta"], v["tb"], ALU.subtract)
            tt(v["kim"], v["kim"], v["den"], ALU.mult)

            def complex_product(out_r, out_i, ar, ai, br, bi, t, negate_imaginary=False, signal=chain):
                tt(out_r, ar, br, ALU.mult)
                tt(t, ai, bi, ALU.mult)
                tt(out_r, out_r, t, ALU.subtract)
                tt(out_i, ar, bi, ALU.mult)
                tt(t, ai, br, ALU.mult)
                if negate_imaginary:
                    link(nc.vector.scalar_tensor_tensor(out_i, out_i, -1.0, t, ALU.mult, ALU.subtract), signal)
                else:
                    tt(out_i, out_i, t, ALU.add, signal)

            small = K.at(S5TMP + 512, 16, 16)
            dve.wait_ge(b_in, 32)
            complex_product(kB[:, 0, :, :], kB[:, 1, :, :], braw[:, 0, :, :], braw[:, 1, :, :], over_c(v["kre"]), over_c(v["kim"]), small)
            link(nc.vector.memset(pw[:, 0, 0, :], 1.0))
            link(nc.vector.memset(pw[:, 1, 0, :], 0.0))
            link(nc.vector.tensor_copy(pw[:, 0, 1, :], v["abre"]))
            link(nc.vector.tensor_copy(pw[:, 1, 1, :], v["abim"]))
            n = 1
            while n < TC:
                last_power = lambda ri: pw[:, ri, n:n + 1, :].to_broadcast([P, n, 16])
                complex_product(pw[:, 0, n + 1:2 * n + 1, :], pw[:, 1, n + 1:2 * n + 1, :], pw[:, 0, 1:n + 1, :], pw[:, 1, 1:n + 1, :],
                                last_power(0), last_power(1), small[:, 0:n, :])
                n *= 2
            for ri in range(2):
                for t in range(TC):
                    chain.by(nc.vector.tensor_copy(rev[:, ri, t, :], pw[:, ri, TC - 1 - t, :]))
            dve.wait_ge(order, chain.n)
            by_jsc = lambda a: a.rearrange("p m j -> p j m").unsqueeze(3).to_broadcast([P, 16, 8, 16])
            over_s = lambda a: a.unsqueeze(2).to_broadcast([P, 16, 8, 16])
            whole = K.at(S5TMP, 16, 8, 16)
            complex_product(WTr, WTi, over_s(kB[:, 0, :, :]), over_s(kB[:, 1, :, :]), by_jsc(rev[:, 0, :, :]), by_jsc(rev[:, 1, :, :]), whole,
                            signal=Count(wt_ready))
            dve.wait_ge(c_tr, 1)
            for ri in range(2):
                src = PS[:, 6 + ri, :].rearrange("p (j g c) -> p j g c", g=2, c=16)
                chain.by(nc.vector.tensor_copy(C[0:64, ri, :, :], src[0:64, :, 0, :]))
                last = nc.vector.tensor_copy(C[64:128, ri, :, :], src[64:128, :, 1, :])
                if ri == 1:
                    link(last, Count(c_ready))
            for j0 in (0, 8):
                js = slice(j0, j0 + 8)
                over_m = lambda a: a.unsqueeze(2).to_broadcast([P, 8, 9, 16])
                by_jmc = lambda a: a.rearrange("p m j -> p j m")[:, js, :].unsqueeze(3).to_broadcast([P, 8, 9, 16])
                complex_product(QR[:, js, :, :], QN[:, js, :, :], over_m(C[:, 0, js, :]), over_m(C[:, 1, js, :]),
                                by_jmc(pw[:, 0, :, :]), by_jmc(pw[:, 1, :, :]), K.at(S5TMP, 8, 9, 16), negate_imaginary=True,
                                signal=chain if j0 == 0 else Count(kb_ready))
            link(nc.vector.tensor_copy(Ts[:, :, 0], trig[:, 2, :]))
            link(nc.vector.tensor_copy(Tc[:, :, 0], trig[:, 3, :]))
            n = 1
            while n < NCH:
                last_power = lambda a: a[:, :, n - 1:n].to_broadcast([P, 16, n])
                complex_product(Tc[:, :, n:2 * n], Ts[:, :, n:2 * n], Tc[:, :, 0:n], Ts[:, :, 0:n], last_power(Tc), last_power(Ts),
                                K.at(S5TMP, 16, n))
                n *= 2
            dve.wait_ge(u_tr, 8)
            dve.wait_ge(ds_in, 16)
            link(nc.vector.tensor_tensor(xs, xs, dskip.rearrange("p (g c) -> p g c", c=16).unsqueeze(2).to_broadcast([P, 32, TC, 16]), ALU.mult))
            dve.wait_ge(toeplitz, 16 * TC)
            for q in range(4):
                js = slice(4 * q, 4 * q + 4)
                dve.wait_ge(v_mm, 2 * q + 2)
                vr, vi = (PS[:, 2 * q + ri, :].rearrange("p (a b) -> p a b", b=NCH) for ri in range(2))
                c, sn_ = Tc[:, js, :], Ts[:, js, :]
                for n, (a, b) in enumerate(((vr, c), (vi, sn_), (vi, c), (vr, sn_))):
                    ins = nc.vector.tensor_tensor(tmp[:, n, :, :], a, b, ALU.mult)
                    if n < 3:
                        chain.by(ins)
                    else:
                        ins.then_inc(v_read, 1)
                dve.wait_ge(v_read, q + 1)
                tt(tmp[:, 0, :, :], tmp[:, 0, :, :], tmp[:, 1, :, :], ALU.add)
                tt(tmp[:, 2, :, :], tmp[:, 2, :, :], tmp[:, 3, :, :], ALU.subtract)
                for ri in range(2):
                    for i in range(4):
                        j = 4 * q + i
                        chain.by(nc.vector.tensor_tensor_scan(G[ri][:, j, :], v["rho"][:, j:j + 1].to_broadcast([P, NCH]), tmp[:, 2 * ri, i, :], 0.0,
                                                              ALU.mult, ALU.add))
                dve.wait_ge(order, chain.n)
                gr, gi = G[0][:, js, 0:NCH - 1], G[1][:, js, 0:NCH - 1]
                c, sn_ = Tc[:, js, 0:NCH - 1], Ts[:, js, 0:NCH - 1]
                for n, (a, b) in enumerate(((gr, c), (gi, sn_), (gi, c), (gr, sn_))):
                    chain.by(nc.vector.tensor_tensor(tmp[:, n, :, 0:NCH - 1], a, b, ALU.mult))
                dve.wait_ge(order, chain.n)
                chain.by(nc.vector.tensor_tensor(G[0][:, js, 1:NCH], tmp[:, 0, :, 0:NCH - 1], tmp[:, 1, :, 0:NCH - 1], ALU.subtract))
                chain.by(nc.vector.tensor_tensor(G[1][:, js, 1:NCH], tmp[:, 2, :, 0:NCH - 1], tmp[:, 3, :, 0:NCH - 1], ALU.add))
                chain.by(nc.vector.memset(G[0][:, js, 0:1], 0.0))
                nc.vector.memset(G[1][:, js, 0:1], 0.0).then_inc(h_ready, 1)
                dve.wait_ge(h_ready, q + 1)
            for n in range(8):
                q, g2 = n // 2, n % 2
                dve.wait_ge(y_mm, n + 1)
                for i in range(4):
                    g = 2 * (4 * q + i) + g2
                    dst = xs[:, g, :, :]
                    src = PS[:, n, i * P:(i + 1) * P].rearrange("p (t c) -> p t c", c=16)
                    last = nc.vector.tensor_tensor(dst, dst, src, ALU.add)
                last.then_inc(y_ready, 1)


CQT, CKVT, KRT, YMT = VECS, VECS + 2048, VECS + 3072, VECS + 4096
ROPE = VECS + 8192
YG, YGT, YST, GMT, SECW = 28032, 32128, 36224, 40320, 44416
RMS_EPS = 1e-6


def project_second(K):
    nc, io, PS = K.nc, K.io, K.PS
    ident, cols2, x2T = K.at(IDENT, P), K.at(COLS2, 64), K.at(X2T, KT, S)
    cqT, ckvT, krT = K.at(CQT, 2, S), K.at(CKVT, S), K.at(KRT, S)
    lat = K.at(YMT, NT, 448)
    cos, sin = K.at(ROPE, NT, 32), K.at(ROPE + 256, NT, 32)
    kr2 = K.at(ROPE + 512, NT, P)
    o = ROPE + 1536
    ss, rinv, posr, posf, pcol = K.at(o, NT, 2), K.at(o + 16, NT, 2), K.at(o + 32, P), K.at(o + 160, P), K.at(o + 288, NT)
    invf = K.at(o + 296, 32)
    assert o + 328 <= X2T
    yg, ygT, ysT, gmT = K.at(YG, TC, CH), K.at(YGT, 4, S), K.at(YST, 4, S), K.at(GMT, 4, S)
    sg = K.at(YG, 2, 512)
    ang, kk, squares = K.at(YG + 1024, NT, 32), K.at(YG + 1280, NT, 32), K.at(YG + 2560, 4, 384)
    red, t1, t2 = K.at(YG + 1792, NT, 32), K.at(YG + 2048, NT, 32), K.at(YG + 2304, NT, 32)
    wlat, wt, wglu = K.at(SECW, KT, 448), K.at(SECW + 3584, 2, KT, P), K.at(SECW + 3584 + 2048, 4, CH)
    w = io["w_in_2"][0].rearrange("(k p) n -> p k n", p=P)
    col_of = lambda T: CH + T * P if T < 4 else 2 * CH + 448 + (T - 4) * P
    with ExitStack() as ctx:
        s = lambda n: K.sem(ctx, "p2_" + n)
        lat_in, glu_in, w_in, small_in, order = s("lat_in"), s("glu_in"), [s("w_in0"), s("w_in1")], s("small_in"), s("order")
        y_tr, y_taken, lat_mm, lat_ready, proj_mm, proj_ready, pos_ready, pos_tr = (s(n) for n in ("y_tr", "y_taken", "lat_mm", "lat", "proj_mm", "proj", "posf", "pos_tr"))
        glu_mm, glu_sig, ys_ready, pos_taken, arg_ready, trig_ready, ms_ready, rms_ready = (s(n) for n in ("glu_mm", "glu_sig", "ys", "pos_taken", "arg", "trig", "ms", "rms"))
        rows_ready, l_tr, l_taken, sig_used = s("rows"), s("l_tr"), s("l_taken"), s("sig_used")
        block = ctx.enter_context(nc.Block())

        @block.sync
        def _(sp):
            sp.dma_start(posr[0:NT, :].bitcast(i32), io["positions_2"].rearrange("o (i p) -> (o i) p", p=P)).then_inc(small_in, 16)
            sp.dma_start(invf, bcast_rows(io["inv_freq"])).then_inc(small_in, 16)
            sp.dma_start(wlat, w[:, :, 2 * CH:2 * CH + 448]).then_inc(lat_in, 16)
            for T in range(8):
                if T >= 2:
                    sp.wait_ge(proj_mm, 2 * (T - 1))
                sp.dma_start(wt[:, T % 2, :, :], w[:, :, col_of(T):col_of(T) + P]).then_inc(w_in[T % 2], 16)
                if T == 1:
                    sp.dma_start(wglu, io["w_glu_2"][0].rearrange("(k p) n -> p k n", p=P)).then_inc(glu_in, 16)

        @block.tensor
        def _(pe):
            for n in range(8):
                c, h = n // 2, n % 2
                for i in range(4):
                    last = nc.tensor.transpose(PS[:, n, i * P:(i + 1) * P], yg[:, 4 * h + i, c * P:(c + 1) * P], ident)
                last.then_inc(y_tr, 1)
            pe.wait_ge(pos_ready, 1)
            pe.wait_ge(y_taken, 8)
            nc.tensor.transpose(PS[:, 7, 0:NT], posf[0:NT, :], ident[0:NT, 0:NT]).then_inc(pos_tr, 1)
            pe.wait_ge(lat_in, 16)
            for i in range(NT):
                if i >= 4:
                    pe.wait_ge(lat_ready, i - 3)
                for k in range(KT):
                    last = nc.tensor.matmul(PS[:, i % 4, 0:448], x2T[:, k, i * P:(i + 1) * P], wlat[:, k, :], start=(k == 0), stop=(k == KT - 1))
                last.then_inc(lat_mm, 1)

            def project(n):
                T, h = n // 2, n % 2
                pe.wait_ge(w_in[T % 2], 16 * (T // 2 + 1))
                if n >= 2:
                    pe.wait_ge(proj_ready, n - 1)
                for k in range(KT):
                    last = nc.tensor.matmul(PS[:, 4 + h, :], wt[:, T % 2, k, :], x2T[:, k, h * 512:(h + 1) * 512], start=(k == 0), stop=(k == KT - 1))
                last.then_inc(proj_mm, 1)

            for n in range(8):
                project(n)
            pe.wait_ge(glu_in, 16)
            pe.wait_ge(pos_taken, 1)
            for n in range(8):
                c, h = n // 2, n % 2
                if n >= 2:
                    pe.wait_ge(glu_sig, n - 1)
                for k in range(4):
                    last = nc.tensor.matmul(PS[:, 6 + h, :], wglu[:, k, c * P:(c + 1) * P], ygT[:, k, h * 512:(h + 1) * 512], start=(k == 0), stop=(k == 3))
                last.then_inc(glu_mm, 1)
                project(8 + n)
            pe.wait_ge(rows_ready, 1)
            pe.wait_ge(lat_ready, NT)
            for n in range(8):
                c, h = n // 2, n % 2
                if n >= 4:
                    pe.wait_ge(l_taken, n - 3)
                for i in range(4):
                    src = lat[:, 4 * h + i, c * P:(c + 1) * P] if c < 3 else kr2[:, 4 * h + i, :]
                    last = nc.tensor.transpose(PS[:, n % 4, i * P:(i + 1) * P], src, ident)
                last.then_inc(l_tr, 1)

        @block.scalar
        def _(act):
            for n in range(8):
                c, h = n // 2, n % 2
                act.wait_ge(y_tr, n + 1)
                dst = ygT[:, c, :].rearrange("p (n t) -> p t n", t=TC)[:, 4 * h:4 * h + 4, :]
                nc.scalar.copy(dst, PS[:, n, :].rearrange("p (a b) -> p a b", b=P)).then_inc(y_taken, 1)
            for i in range(NT):
                act.wait_ge(lat_mm, i + 1)
                if i >= 4:
                    act.wait_ge(lat_ready, i - 3)
                nc.scalar.activation(squares[:, i % 4, 0:256], PS[:, i % 4, 0:256], ACT.Square, accum_out=ss[:, i, 0:1])
                nc.scalar.activation(squares[:, i % 4, 256:384], PS[:, i % 4, 256:384], ACT.Square, accum_out=ss[:, i, 1:2])
                nc.scalar.copy(lat[:, i, :], PS[:, i % 4, 0:448]).then_inc(lat_ready, 1)

            def take_projection(n):
                T, h = n // 2, n % 2
                act.wait_ge(proj_mm, n + 1)
                dst = (ysT if T < 4 else gmT)[:, T % 4, h * 512:(h + 1) * 512]
                nc.scalar.activation(dst, PS[:, 4 + h, :], ACT.Silu).then_inc(proj_ready, 1)

            for n in range(8):
                take_projection(n)
            act.wait_ge(arg_ready, 1)
            nc.scalar.activation(sin, red, ACT.Sin).then_inc(trig_ready, 1)
            act.wait_ge(arg_ready, 2)
            nc.scalar.activation(cos, red, ACT.Sin).then_inc(trig_ready, 1)
            act.wait_ge(ms_ready, 1)
            nc.scalar.activation(rinv, rinv, ACT.Sqrt).then_inc(rms_ready, 1)
            for n in range(8):
                c, h = n // 2, n % 2
                act.wait_ge(glu_mm, n + 1)
                if n >= 2:
                    act.wait_ge(ys_ready, n - 1)
                nc.scalar.activation(sg[:, n % 2, :], PS[:, 6 + h, :], ACT.Sigmoid, bias=cols2[:, 32 + c:33 + c]).then_inc(glu_sig, 1)
                take_projection(8 + n)
            for n in range(8):
                c, h = n // 2, n % 2
                act.wait_ge(l_tr, n + 1)
                dst = (cqT[:, c, :] if c < 2 else ckvT if c == 2 else krT)[:, h * 512:(h + 1) * 512]
                scale = cols2[:, 36 + c:37 + c] if c < 3 else 1.0
                nc.scalar.activation(dst, PS[:, n % 4, :], ACT.Copy, scale=scale).then_inc(l_taken, 1)

        @block.vector
        def _(dve):
            chain = Count(order)

            def link(ins, signal=chain):
                signal.by(ins)
                dve.wait_ge(signal.sem, signal.n)

            def tt(out, a, b, op, signal=chain):
                link(nc.vector.tensor_tensor(out, a, b, op), signal)

            args = Count(arg_ready)
            dve.wait_ge(small_in, 32)
            link(nc.vector.tensor_copy(posf[0:NT, :], posr[0:NT, :].bitcast(i32)), Count(pos_ready))
            dve.wait_ge(pos_tr, 1)
            link(nc.vector.tensor_copy(pcol, PS[:, 7, 0:NT]), Count(pos_taken))
            dve.wait_ge(y_tr, 8)
            tt(ang, pcol.unsqueeze(2).to_broadcast([P, NT, 32]), invf.unsqueeze(1).to_broadcast([P, NT, 32]), ALU.mult)
            reduced_sine_argument(nc, link, red, ang, kk)
            link(nc.vector.memset(t1[:, 0, 0:1], 0.0), args)
            dve.wait_ge(trig_ready, 1)
            reduced_sine_argument(nc, link, red, ang, kk, 0.25)
            link(nc.vector.memset(t1[:, 0, 0:1], 0.0), args)
            dve.wait_ge(trig_ready, 2)
            dve.wait_ge(lat_ready, NT)
            for n, width in enumerate((256, 128)):
                link(nc.vector.tensor_scalar(rinv[:, :, n], ss[:, :, n], 1 / width, RMS_EPS, ALU.mult, ALU.add), chain if n == 0 else Count(ms_ready))
            k1, k2 = lat[:, :, 384:416], lat[:, :, 416:448]
            for out, a, b, op in ((0, cos, sin, ALU.subtract), (32, sin, cos, ALU.add)):
                tt(t1, k1, a, ALU.mult)
                tt(t2, k2, b, ALU.mult)
                tt(kr2[:, :, out:out + 32], t1, t2, op)
            link(nc.vector.tensor_copy(kr2[:, :, 64:128], kr2[:, :, 0:64]))
            dve.wait_ge(rms_ready, 1)
            link(nc.vector.reciprocal(rinv, rinv))
            for n, (a, b) in enumerate(((0, 256), (256, 384))):
                tt(lat[:, :, a:b], lat[:, :, a:b], rinv[:, :, n:n + 1].to_broadcast([P, NT, b - a]), ALU.mult,
                   chain if n == 0 else Count(rows_ready))
            for n in range(8):
                c, h = n // 2, n % 2
                dve.wait_ge(proj_ready, n + 1)
                d, y = ysT[:, c, h * 512:(h + 1) * 512], ygT[:, c, h * 512:(h + 1) * 512]
                tt(d, d, y, ALU.mult)
                dve.wait_ge(glu_sig, n + 1)
                nc.vector.tensor_tensor(d, d, sg[:, n % 2, :], ALU.mult).then_inc(ys_ready, 1)


MLA_HEADS, ROPE_D = 4, 64
QK_SCALE = 192 ** -0.5


def latent_attention(K):
    nc, io, PS = K.nc, K.io, K.PS
    ident = K.at(IDENT, P)
    cqT, ckvT, krT, ymT, gmT = K.at(CQT, 2, S), K.at(CKVT, S), K.at(KRT, S), K.at(YMT, 4, S), K.at(GMT, 4, S)
    cos, sin = K.at(ROPE, NT, 32), K.at(ROPE + 256, NT, 32)
    knT, qnT = K.at(X2T, 4, S), K.at(X2T + 4096, 4, S)
    vr = K.at(YG, NT, CH)
    wuq, wukv = K.at(YG + 4096, 2, 4, 192), K.at(YG + 4096 + 1536, 4, 256)
    causal = K.at(YG + 4096 + 2560, S)
    qrT = K.at(SECW, 2, S)
    sb, pt = K.at(SECW + 2048, 2, S), K.at(SECW + 4096, 2, S)
    orow = K.at(SECW + 6144, NT, P)
    rope_rows = K.at(SECW + 2048, NT, 4, 64)
    t1, t2 = K.at(SECW + 4096, 4, 32), K.at(SECW + 4096 + P, 4, 32)
    o = SECW + 7168
    mx, nm, l, rl = K.at(o, 32), K.at(o + 32, 32), K.at(o + 64, 32), K.at(o + 96, 32)
    units = [(h, i) for h in range(MLA_HEADS) for i in range(NT)]
    t_jobs, first_job, out_job = [], {}, {}
    for step in range(len(units) + 2):
        if 1 <= step <= len(units):
            h, i = units[step - 1]
            first_job[step - 1] = len(t_jobs)
            t_jobs += [("p", step - 1, b0, min(b0 + 4, i + 1)) for b0 in range(0, i + 1, 4)]
        if step >= 2 and units[step - 2][1] == NT - 1:
            h = units[step - 2][0]
            out_job[h] = len(t_jobs)
            t_jobs += [("o", h, 0, 4), ("o", h, 4, 8)]
    after_unit = lambda u: first_job[u] + (units[u][1] + 4) // 4
    with ExitStack() as ctx:
        s = lambda n: K.sem(ctx, "ml_" + n)
        w_in, causal_in, order = s("w_in"), s("causal_in"), s("order")
        up_mm, up_ready, r_mm, r_ready, rt, rt_ready = s("up_mm"), s("up"), s("r_mm"), s("r"), s("rt"), s("rt_ready")
        s_done, s_taken, nm_ready, exp_done, t_done, t_taken, pv_done, o_ready, rl_ready = (s(n) for n in ("s", "s_taken", "nm", "exp", "t", "t_taken", "pv", "o", "rl"))
        block = ctx.enter_context(nc.Block())

        @block.sync
        def _(sp):
            sp.dma_start(wuq, io["w_uq_2"][0].rearrange("(k p) (h n) -> p k h n", p=P, h=4)).then_inc(w_in, 16)
            sp.dma_start(wukv, io["w_ukv_2"][0].rearrange("p (h n) -> p h n", h=4)).then_inc(w_in, 16)
            sp.dma_start(causal, io["causal"]).then_inc(causal_in, 16)

        @block.tensor
        def _(pe):
            pe.wait_ge(w_in, 32)
            for i in range(NT):
                if i >= 4:
                    pe.wait_ge(r_ready, i - 3)
                for c in range(2):
                    last = nc.tensor.matmul(PS[:, 4 + i % 4, 0:256], cqT[:, c, i * P:(i + 1) * P], wuq[:, c, :, 128:192], start=(c == 0), stop=(c == 1))
                last.then_inc(r_mm, 1)
            for n in range(24):
                kind, a, h = n // 8, (n % 8) // 2, n % 2
                if n >= 4:
                    pe.wait_ge(up_ready, n - 3)
                out = PS[:, n % 4, :]
                if kind == 0:
                    for c in range(2):
                        last = nc.tensor.matmul(out, wuq[:, c, a, 0:128], cqT[:, c, h * 512:(h + 1) * 512], start=(c == 0), stop=(c == 1))
                elif kind == 1:
                    last = nc.tensor.matmul(out, wukv[:, a, 0:128], ckvT[:, h * 512:(h + 1) * 512], start=True, stop=True)
                else:
                    last = nc.tensor.matmul(out, ckvT[:, (n % 8) * P:(n % 8 + 1) * P], wukv[:, :, 128:256], start=True, stop=True)
                last.then_inc(up_mm, 1)
            pe.wait_ge(r_ready, NT)
            for n in range(4):
                pair, h = n // 2, n % 2
                for i in range(4):
                    last = nc.tensor.transpose(PS[:, 4 + n, i * P:(i + 1) * P], rope_rows[:, 4 * h + i, 2 * pair:2 * pair + 2, :], ident)
                last.then_inc(rt, 1)
            pe.wait_ge(up_ready, 24)
            pe.wait_ge(rt_ready, 4)

            def scores(u):
                h, i = units[u]
                if u >= 2:
                    pe.wait_ge(s_taken, u - 1)
                half = slice(64 * (h % 2), 64 * (h % 2) + 64)
                n = (i + 1) * P
                for c in range(0, n, 512):
                    e = min(n, c + 512)
                    out = PS[:, 2 * (u % 2) + c // 512, 0:e - c]
                    nc.tensor.matmul(out, qnT[:, h, i * P:(i + 1) * P], knT[:, h, c:e], start=True, stop=False)
                    last = nc.tensor.matmul(out, qrT[half, h // 2, i * P:(i + 1) * P], krT[half, c:e], start=False, stop=True)
                last.then_inc(s_done, 1)

            def transposes(g):
                kind, which, b0, b1 = t_jobs[g]
                if g >= 2:
                    pe.wait_ge(t_taken, g - 1)
                for b in range(b0, b1):
                    src = sb[:, which % 2, b * P:(b + 1) * P] if kind == "p" else orow[:, b, :]
                    last = nc.tensor.transpose(PS[:, 4 + g % 2, (b - b0) * P:(b - b0 + 1) * P], src, ident)
                last.then_inc(t_done, 1)

            for step in range(len(units) + 2):
                if step < len(units):
                    scores(step)
                if 1 <= step <= len(units):
                    u = step - 1
                    pe.wait_ge(exp_done, u + 1)
                    for g in range(first_job[u], after_unit(u)):
                        transposes(g)
                if step >= 2:
                    u = step - 2
                    h, i = units[u]
                    pe.wait_ge(t_taken, after_unit(u))
                    if u >= 2:
                        pe.wait_ge(o_ready, u - 1)
                    for b in range(i + 1):
                        last = nc.tensor.matmul(PS[:, 6 + u % 2, 0:P], pt[:, u % 2, b * P:(b + 1) * P], vr[:, b, h * P:(h + 1) * P],
                                                start=(b == 0), stop=(b == i))
                    last.then_inc(pv_done, 1)
                    if i == NT - 1:
                        pe.wait_ge(o_ready, u + 1)
                        for g in range(out_job[h], out_job[h] + 2):
                            transposes(g)

        @block.scalar
        def _(act):
            for n in range(24):
                kind, a, h = n // 8, (n % 8) // 2, n % 2
                act.wait_ge(up_mm, n + 1)
                dst = vr[:, n % 8, :] if kind == 2 else (qnT, knT)[kind][:, a, h * 512:(h + 1) * 512]
                nc.scalar.copy(dst, PS[:, n % 4, :]).then_inc(up_ready, 1)
            for step in range(len(units) + 2):
                if step < len(units):
                    h, i = units[step]
                    n = (i + 1) * P
                    act.wait_ge(nm_ready, step + 1)
                    nc.scalar.activation(sb[:, step % 2, 0:n], sb[:, step % 2, 0:n], ACT.Exp, bias=nm[:, step:step + 1], scale=QK_SCALE,
                                         accum_out=l[:, step:step + 1]).then_inc(exp_done, 1)
                if step >= 2:
                    u = step - 2
                    h, i = units[u]
                    act.wait_ge(pv_done, u + 1)
                    act.wait_ge(rl_ready, u + 1)
                    if h >= 1:
                        act.wait_ge(t_done, out_job[h - 1] + 2)
                    nc.scalar.activation(orow[:, i, :], PS[:, 6 + u % 2, 0:P], ACT.Copy, scale=rl[:, u:u + 1]).then_inc(o_ready, 1)

        @block.vector
        def _(dve):
            chain = Count(order)

            def link(ins, signal=chain):
                signal.by(ins)
                dve.wait_ge(signal.sem, signal.n)

            for i in range(NT):
                dve.wait_ge(r_mm, i + 1)
                x = PS[:, 4 + i % 4, 0:256].rearrange("p (h e) -> p h e", h=4)
                c, sn = (a[:, i, :].unsqueeze(1).to_broadcast([P, 4, 32]) for a in (cos, sin))
                for out, a, b, op in ((0, c, sn, ALU.subtract), (32, sn, c, ALU.add)):
                    link(nc.vector.tensor_tensor(t1, x[:, :, 0:32], a, ALU.mult))
                    link(nc.vector.tensor_tensor(t2, x[:, :, 32:64], b, ALU.mult))
                    ins = nc.vector.tensor_tensor(rope_rows[:, i, :, out:out + 32], t1, t2, op)
                    if out:
                        ins.then_inc(r_ready, 1)
                        dve.wait_ge(r_ready, i + 1)
                    else:
                        link(ins)
            for n in range(4):
                dve.wait_ge(rt, n + 1)
                nc.vector.tensor_copy(qrT[:, n // 2, (n % 2) * 512:(n % 2 + 1) * 512], PS[:, 4 + n, :]).then_inc(rt_ready, 1)
            dve.wait_ge(causal_in, 16)

            def take(g, dst, gate=None):
                dve.wait_ge(t_done, g + 1)
                src = PS[:, 4 + g % 2, 0:dst.shape[1]]
                if gate is None:
                    nc.vector.tensor_copy(dst, src).then_inc(t_taken, 1)
                else:
                    nc.vector.tensor_tensor(dst, src, gate, ALU.mult).then_inc(t_taken, 1)

            for step in range(len(units) + 2):
                if step < len(units):
                    h, i = units[step]
                    n = (i + 1) * P
                    dve.wait_ge(s_done, step + 1)
                    if step >= 2:
                        dve.wait_ge(t_done, after_unit(step - 2))
                    src = PS[:, 2 * (step % 2):2 * (step % 2) + 2, :].rearrange("p a b -> p (a b)")[:, 0:n]
                    nc.vector.tensor_tensor_reduce(out=sb[:, step % 2, 0:n], in0=src, in1=causal[:, S - n:S], scale=1.0, scalar=-3e38,
                                                   op0=ALU.add, op1=ALU.max, accum_out=mx[:, step:step + 1]).then_inc(s_taken, 1)
                    dve.wait_ge(s_taken, step + 1)
                    nc.vector.tensor_scalar(nm[:, step:step + 1], mx[:, step:step + 1], -QK_SCALE, None, ALU.mult).then_inc(nm_ready, 1)
                if 1 <= step <= len(units):
                    u = step - 1
                    if u >= 2:
                        dve.wait_ge(pv_done, u - 1)
                    for g in range(first_job[u], after_unit(u)):
                        _, _, b0, b1 = t_jobs[g]
                        take(g, pt[:, u % 2, b0 * P:b1 * P])
                    dve.wait_ge(exp_done, u + 1)
                    nc.vector.reciprocal(rl[:, u:u + 1], l[:, u:u + 1]).then_inc(rl_ready, 1)
                if step >= 2 and units[step - 2][1] == NT - 1:
                    h = units[step - 2][0]
                    for n, g in enumerate(range(out_job[h], out_job[h] + 2)):
                        take(g, ymT[:, h, n * 512:(n + 1) * 512], gmT[:, h, n * 512:(n + 1) * 512])


def second_output(K):
    nc, io, PS = K.nc, K.io, K.PS
    ident = K.at(IDENT, P)
    ysT, ymT, x2r = K.at(YST, 4, S), K.at(YMT, 4, S), K.at(X2R, NT, D)
    wout, wpg, wpp = K.at(GMT, KT, D), K.at(YG, KT, D), K.at(X2T, 2, D)
    prow, pT = K.at(X2T + 2048, NT, 256), K.at(X2T + 4096, 2, NT, P)
    uT = K.at(X2T + 6144, 2, KT, P)
    vec = K.at(VECS, 2, D)
    sg = K.at(VECS + 2048, 2, D)
    stat = K.at(ROPE, 16)
    out_class = io["out"][0].rearrange("(n r) d -> n r d", r=8)
    with ExitStack() as ctx:
        s = lambda n: K.sem(ctx, "so_" + n)
        wout_in, wpg_in, wpp_in, p_in, vec_in, order = s("wout_in"), s("wpg_in"), s("wpp_in"), s("p_in"), s("vec_in"), s("order")
        p_tr, p_taken, mix, u_ready, ut, ut_taken, pg, pp, sig, pp_used, var, std, row_ready = (s(n) for n in (
            "p_tr", "p_taken", "mix", "u", "ut", "ut_taken", "pg", "pp", "sig", "pp_used", "var", "std", "row"))
        block = ctx.enter_context(nc.Block())

        @block.sync
        def _(sp):
            sp.dma_start(prow, io["p_2"][0, 0].rearrange("(n r) e -> n r e", r=8)).then_inc(p_in, 16)
            sp.dma_start(wout, io["w_out_2"][0].rearrange("(k p) n -> p k n", p=P)).then_inc(wout_in, 16)
            sp.dma_start(wpp, io["w_pp_2"][0].rearrange("(k p) n -> p k n", p=P)).then_inc(wpp_in, 16)
            sp.dma_start(wpg, io["w_pg_2"][0].rearrange("(k p) n -> p k n", p=P)).then_inc(wpg_in, 16)
            for n, name in enumerate(("ln_g_2", "ln_b_2")):
                sp.dma_start(vec[:, n, :], bcast_rows(io[name][0])).then_inc(vec_in, 16)
            for r in range(NT):
                sp.wait_ge(row_ready, r + 1)
                sp.dma_start(out_class[:, r, :], x2r[:, r, :]).then_inc(K.out_done, 16)
            sp.wait_ge(K.out_done, 16 * NT)

        @block.tensor
        def _(pe):
            pe.wait_ge(p_in, 16)
            for n in range(4):
                k, h = n // 2, n % 2
                for i in range(4):
                    last = nc.tensor.transpose(PS[:, 4 + n, i * P:(i + 1) * P], prow[:, 4 * h + i, k * P:(k + 1) * P], ident)
                last.then_inc(p_tr, 1)

            def mixed(r):
                if r >= 1:
                    pe.wait_ge(u_ready, r)
                for h in range(2):
                    for k in range(KT):
                        src = (ysT if k < 4 else ymT)[:, k % 4, r:S:8]
                        last = nc.tensor.matmul(PS[:, h, :], src, wout[:, k, h * 512:(h + 1) * 512], start=(k == 0), stop=(k == KT - 1))
                last.then_inc(mix, 1)

            pe.wait_ge(wout_in, 16)
            mixed(0)
            pe.wait_ge(wpp_in, 16)
            pe.wait_ge(p_taken, 4)
            for r in range(NT):
                if r >= 1:
                    pe.wait_ge(pp_used, r)
                for h in range(2):
                    for k in range(2):
                        last = nc.tensor.matmul(PS[:, 6 + h, :], pT[:, k, r, :], wpp[:, k, h * 512:(h + 1) * 512], start=(k == 0), stop=(k == 1))
                last.then_inc(pp, 1)
                if r + 1 < NT:
                    mixed(r + 1)
                pe.wait_ge(u_ready, r + 1)
                for g in range(2):
                    if r >= 1:
                        pe.wait_ge(ut_taken, 2 * r - 1 + g)
                    for i in range(4):
                        k = 4 * g + i
                        last = nc.tensor.transpose(PS[:, 2 + g, i * P:(i + 1) * P], x2r[:, r, k * P:(k + 1) * P], ident)
                    last.then_inc(ut, 1)
                pe.wait_ge(wpg_in, 16)
                pe.wait_ge(ut_taken, 2 * r + 2)
                if r >= 1:
                    pe.wait_ge(sig, r)
                for h in range(2):
                    for k in range(KT):
                        last = nc.tensor.matmul(PS[:, 4 + h, :], uT[:, r % 2, k, :], wpg[:, k, h * 512:(h + 1) * 512], start=(k == 0), stop=(k == KT - 1))
                last.then_inc(pg, 1)

        @block.scalar
        def _(act):
            for n in range(4):
                act.wait_ge(p_tr, n + 1)
                nc.scalar.copy(pT[:, n // 2, 4 * (n % 2):4 * (n % 2) + 4, :], PS[:, 4 + n, :].rearrange("p (a b) -> p a b", b=P)).then_inc(p_taken, 1)
            for r in range(NT + 1):
                if r < NT:
                    for g in range(2):
                        act.wait_ge(ut, 2 * r + g + 1)
                        nc.scalar.copy(uT[:, r % 2, 4 * g:4 * g + 4, :], PS[:, 2 + g, :].rearrange("p (a b) -> p a b", b=P)).then_inc(ut_taken, 1)
                if r < NT:
                    act.wait_ge(pg, r + 1)
                    if r >= 2:
                        act.wait_ge(pp_used, r - 1)
                    nc.scalar.activation(sg[:, r % 2, :], PS[:, 4:6, :].rearrange("p a b -> p (a b)"), ACT.Sigmoid).then_inc(sig, 1)
                    act.wait_ge(var, r + 1)
                    nc.scalar.activation(stat[:, 15:16], stat[:, 14:15], ACT.Sqrt).then_inc(std, 1)

        @block.vector
        def _(dve):
            chain = Count(order)

            def link(ins, signal=chain):
                signal.by(ins)
                dve.wait_ge(signal.sem, signal.n)

            norm = RowNorm(nc, dve, link, stat, Count(var), std)
            u, used, rows = Count(u_ready), Count(pp_used), Count(row_ready)

            def residual(r):
                dve.wait_ge(mix, r + 1)
                link(nc.vector.scalar_tensor_tensor(x2r[:, r, :], x2r[:, r, :], ALPHA, PS[:, 0:2, :].rearrange("p a b -> p (a b)"), ALU.mult, ALU.add), u)

            dve.wait_ge(vec_in, 32)
            residual(0)
            for r in range(NT):
                if r + 1 < NT:
                    residual(r + 1)
                dve.wait_ge(sig, r + 1)
                dve.wait_ge(pp, r + 1)
                link(nc.vector.tensor_tensor(sg[:, r % 2, :], PS[:, 6:8, :].rearrange("p a b -> p (a b)"), sg[:, r % 2, :], ALU.mult), used)
                link(nc.vector.tensor_tensor(x2r[:, r, :], x2r[:, r, :], sg[:, r % 2, :], ALU.add))
                norm(x2r[:, r, :], vec[:, 0, :], vec[:, 1, :], rows)


def hybrid_kernel(nc, io):
    K = Kernel(nc, io)
    with K.ctx:
        GHY = FWORK + 9728
        yhyT = K.at(X1T, 4, S)
        steps = [lambda: prepare(K),
                 lambda: project_hyena(K, 0, 8, LF),
                 lambda: long_convolution(K, 0, FWORK),
                 lambda: project_hyena(K, 8, 16, LF, K.at(X1T, 4, S), K.at(GHY, 4, S)),
                 lambda: long_convolution(K, 1, FWORK, K.at(X1T, 4, S), K.at(GHY, 4, S), yhyT),
                 lambda: dilated_attention(K),
                 lambda: merge_branches(K),
                 lambda: first_output(K),
                 lambda: s5_states(K),
                 lambda: project_second(K),
                 lambda: latent_attention(K),
                 lambda: second_output(K)]
        for step in steps:
            step()
            K.end_phase()


INPUTS = ["x", "c", "w_ada", "b_ada", "w_in", "b_in", "conv_w", "conv_b", "filt_w1", "filt_b1", "filt_w2", "filt_b2",
          "filt_w3", "filt_b3", "filt_w4", "filt_freq", "filt_bias", "w_proj_attn", "w_proj_hyena", "w_out", "b_out",
          "ln_g", "ln_b", "p_2", "positions_2", "ln_emb_g_2", "ln_emb_b_2", "w_in_2", "a_re_2", "a_im_2", "log_dt_2",
          "b_re_2", "b_im_2", "c_re_2", "c_im_2", "d_skip_2", "w_glu_2", "b_glu_2", "q_norm_g_2", "w_uq_2",
          "kv_norm_g_2", "w_ukv_2", "w_out_2", "w_pg_2", "w_pp_2", "ln_g_2", "ln_b_2"]


def kernel(**inputs):
    import concourse.bacc as bacc
    from concourse.bass_utils import run_bass_kernel_spmd as run

    nc = bacc.Bacc("TRN2", target_bir_lowering=False, num_devices=1)
    arrays, io = {}, {}
    for name, value in [(n, inputs[n]) for n in INPUTS] + list(shape_constants().items()):
        a = np.ascontiguousarray(value)
        arrays[f"in_{name}"] = a
        io[name] = nc.dram_tensor(f"in_{name}", a.shape, mybir.dt.from_np(a.dtype), kind="ExternalInput").ap()
    io["out"] = nc.dram_tensor("out_x", (1, S, D), fp32, kind="ExternalOutput").ap()
    hybrid_kernel(nc, io)
    r = run(nc, [arrays], core_ids=[0])
    return r.results[0]["out_x"]
```

```python
import math
from contextlib import ExitStack

import numpy as np

import concourse.bass as bass
from concourse import mybir

fp32 = mybir.dt.float32
i32 = mybir.dt.int32
ALU = mybir.AluOpType
ACT = mybir.ActivationFunctionType
AX = mybir.AxisListType

P = 128
S = 1024
D = 1024
KT = D // P
NT = S // P
HD = 64
CH = 512
N_QKV = 4608
COL_GATTN = N_QKV
COL_HY = COL_GATTN + CH
COL_R = COL_HY + 4 * CH
ALPHA = 2 ** 0.25
TWO_PI = 2 * math.pi
ROUND = 1.5 * 2 ** 23
R2 = math.sqrt(0.5)
FAR = 1e32

PI_A = float(np.float32(6.28125))
PI_B = float(np.float32(np.round((TWO_PI - PI_A) * 2 ** 22) / 2 ** 22))
PI_C = float(np.float32(TWO_PI - PI_A - PI_B))
PI_CLIP = float(np.nextafter(np.float32(math.pi), np.float32(0)))


def leaf_tables():
    fwd, inv = {}, {}
    t = np.arange(256)[None, :]
    for name, phase in (("P", math.pi / 4), ("M", 5 * math.pi / 4)):
        k = np.arange(256)[:, None]
        a = (phase + 2 * math.pi * k) / 256 * t
        c, s = np.cos(a), np.sin(a)
        fwd[name] = np.block([[c.T, s.T], [-s.T, c.T]])
        inv[name] = np.block([[c, -s], [s, c]]) / 256 / 4
    for name, n, k, roots, scale in (("B", 512, 256, math.pi * (2 * np.arange(256) + 1) / 512, 2 / 512 / 4),
                                     ("N", 256, 128, math.pi * (2 * np.arange(128) + 1) / 256, 2 / 256 / 8),
                                     ("C", 256, 256, 2 * math.pi * np.arange(256) / 256, 1 / 256 / 8)):
        a = roots[:, None] * np.arange(n)[None, :]
        c, s = np.cos(a), np.sin(a)
        fwd[name] = np.hstack([c.T, s.T])
        inv[name] = np.vstack([c, s]) * scale
    order = "PMBNC"
    return {f"fwd_{n}": fwd[n].astype(np.float32) for n in order} | {f"inv_{n}": inv[n].astype(np.float32) for n in order}


def shape_constants():
    f32 = np.float32
    out = {"ident": np.eye(P, dtype=f32)}
    L = S
    pos = np.concatenate([np.arange(L), (L - np.arange(L)) % L])
    t = np.linspace(0.0, 1.0, L, dtype=f32)[:, None]
    bands = 16
    w = (2.0 * math.pi * np.arange(L, dtype=f32)[:, None] / L).astype(f32)
    f = np.linspace(1e-4, bands - 1, bands, dtype=f32)[None, :]
    feat = np.concatenate([t, np.cos(f * w), -np.sin(f * w)], axis=-1).astype(f32)
    out["posT"] = np.ascontiguousarray(feat[pos].T)
    deltas = np.linspace(math.log(1e-2) / 1.5, math.log(1e-2) / 0.3, CH, dtype=f32)
    decay = np.exp(-t * np.abs(deltas)[None, :]).astype(f32)[pos]
    decay[L] = 0.0
    out["decay"] = decay
    out.update(leaf_tables())
    q, key = np.arange(P)[:, None], np.arange(256)[None, :]
    tables = []
    for shift in (0, 64, 128):
        rel = np.abs(key - shift - q)
        tables.append(np.where(rel <= 64, rel, FAR))
    for a in range(2):
        rel = np.abs(key - (2 * q + a))
        same = np.abs(key[:, :P] - q)
        tables += [np.where(rel <= 64, 4 * rel, FAR), np.where(same % 2 == 0, 8 * same, FAR)]
    out["dist"] = np.concatenate(tables, axis=1).astype(f32)
    out["causal"] = np.concatenate([np.zeros((P, 7 * P)), np.where(np.arange(P)[None, :] <= q, 0.0, -1e30)], axis=1).astype(f32)
    out["inv_freq"] = (np.float32(1.0) / np.power(np.float32(10000.0), np.arange(0, 64, 2, dtype=f32) / np.float32(64))).astype(f32)
    return out


class Count:

    def __init__(self, sem):
        self.sem, self.n = sem, 0

    def by(self, ins):
        self.n += 1
        return ins.then_inc(self.sem, 1)


class Kernel:
    def __init__(self, nc, io):
        self.nc, self.io = nc, io
        self.ctx = ExitStack()
        self.A = self.ctx.enter_context(nc.sbuf_tensor("arena", [P, 52400], fp32))
        self.PS = self.ctx.enter_context(nc.psum_tensor("banks", [P, 8, 512], fp32))
        self.phase_sems = []
        self.out_done = self.ctx.enter_context(nc.semaphore("out_done"))

    def at(self, off, *dims):
        n = int(np.prod(dims))
        assert off + n <= 52400, (off, n)
        v = self.A[:, off:off + n]
        if len(dims) == 2:
            v = v.rearrange("p (a b) -> p a b", a=dims[0])
        if len(dims) == 3:
            v = v.rearrange("p (a b c) -> p a b c", a=dims[0], b=dims[1])
        if len(dims) == 4:
            v = v.rearrange("p (a b c d) -> p a b c d", a=dims[0], b=dims[1], c=dims[2])
        return v

    def sem(self, name):
        self.phase_sems.append(self.nc.alloc_semaphore(name))
        return self.phase_sems[-1]

    def end_phase(self):
        self.nc.clear_and_free_semaphores(self.phase_sems)
        self.nc.all_engine_barrier()
        self.phase_sems = []


def bcast_rows(ap1d, n=P):
    return ap1d.partition_broadcast(n)


IDENT = 0
COLS1 = 128
COLS2 = COLS1 + 128
MODT = COLS2 + 64
GATE = MODT + 16
MLPC = GATE + 1024
HT = 1408
assert MLPC + 8 <= HT
H3 = HT + 8192
FREE1 = H3 + 2048
N_COLS1 = 120


def reduced_sine_argument(nc, link, out, x, k, quarter=0.0):
    link(nc.vector.tensor_scalar(k, x, 1 / TWO_PI, ROUND + quarter if not quarter else quarter, ALU.mult, ALU.add))
    if quarter:
        link(nc.vector.tensor_scalar(k, k, ROUND, None, ALU.add))
    link(nc.vector.tensor_scalar(k, k, ROUND, None, ALU.subtract))
    link(nc.vector.scalar_tensor_tensor(out, k, -PI_A, x, ALU.mult, ALU.add))
    link(nc.vector.scalar_tensor_tensor(out, k, -PI_B, out, ALU.mult, ALU.add))
    link(nc.vector.scalar_tensor_tensor(out, k, -PI_C, out, ALU.mult, ALU.add))
    if quarter:
        link(nc.vector.tensor_scalar(out, out, quarter * TWO_PI, PI_CLIP, ALU.add, ALU.min))
        link(nc.vector.tensor_scalar(out, out, -PI_CLIP, None, ALU.max))
    else:
        link(nc.vector.tensor_scalar(out, out, PI_CLIP, -PI_CLIP, ALU.min, ALU.max))


def prepare(K):
    nc, io = K.nc, K.io
    o = FREE1
    xr = K.at(o, NT, D); o += NT * D
    wada = K.at(o, 2, KT, 512); o += 2 * KT * 512
    bada = K.at(o, 3 * D); o += 3 * D
    mod = K.at(o, 6, 512); o += 3 * D
    cbc = K.at(o, KT, P); o += KT * P
    stats = K.at(o, NT, 12); o += NT * 12
    mv = K.at(o, NT, 2); o += NT * 2
    std = K.at(o, NT); o += NT
    rows = K.at(o, 2, P); o += 2 * P
    one = K.at(o, 1); o += 1
    ident, hT, modT, gate = K.at(IDENT, P), K.at(HT, KT, S), K.at(MODT, 16), K.at(GATE, D)
    cols1, cols2 = K.at(COLS1, N_COLS1), K.at(COLS2, 64)
    PS = K.PS
    with ExitStack() as ctx:
        s = lambda n: K.sem("prep_" + n)
        x_in, c_in, row_in = [s(f"x_in{i}") for i in range(4)], s("c_in"), s("row_in")
        wada_in = [s("wada_in0"), s("wada_in1")]
        order, cbc_ready, mod_done, mod_ready, col_done, modT_ready = s("order"), s("cbc"), s("mod_done"), s("mod_ready"), s("col_done"), s("modT")
        var_ready, std_ready, norm_ready, tr_done, hT_ready = s("var"), s("std"), s("norm"), s("tr"), s("hT")
        rows_tr, rows_ready = s("rows_tr"), s("rows_ready")
        zero_ready = s("zero")
        block = ctx.enter_context(nc.Block())

        @block.sync
        def _(sp):
            sp.dma_start(ident, io["ident"]).then_inc(row_in, 16)
            sp.wait_ge(zero_ready, 1)
            sp.dma_start(rows[0:72, 0, :], io["b_in"].rearrange("o (n p) -> (o n) p", p=P)).then_inc(row_in, 16)
            sp.dma_start(rows[72:108, 0, :], io["conv_w"].rearrange("o t (n p) -> (o t n) p", p=P)).then_inc(row_in, 16)
            sp.dma_start(rows[108:120, 0, :], io["conv_b"].rearrange("o (n p) -> (o n) p", p=P)).then_inc(row_in, 16)
            sp.dma_start(rows[0:16, 1, :], io["a_re_2"].rearrange("o (j g) p -> (o j) (g p)", g=2)).then_inc(row_in, 16)
            sp.dma_start(rows[16:32, 1, :], io["a_im_2"].rearrange("o (j g) p -> (o j) (g p)", g=2)).then_inc(row_in, 16)
            sp.dma_start(rows[32:36, 1, :], io["b_glu_2"].rearrange("o (n p) -> (o n) p", p=P)).then_inc(row_in, 16)
            sp.dma_start(rows[36:38, 1, :], io["q_norm_g_2"].rearrange("o (n p) -> (o n) p", p=P)).then_inc(row_in, 16)
            sp.dma_start(rows[38:39, 1, :], io["kv_norm_g_2"]).then_inc(row_in, 16)
            sp.dma_start(rows[39:47, 1, :], io["c"].rearrange("o (k p) -> (o k) p", p=P)).then_inc(row_in, 16)
            for i in range(4):
                sp.dma_start(xr[:, 2 * i:2 * i + 2, :], io["x"][0, 2 * i * P:(2 * i + 2) * P, :].rearrange("(a p) n -> p a n", p=P)).then_inc(x_in[i], 16)
            sp.dma_start(bada, bcast_rows(io["b_ada"][0])).then_inc(c_in, 16)

        @block.gpsimd
        def _(pool):
            nc.gpsimd.memset(rows[:, :, :], 0.0).then_inc(zero_ready, 1)
            w = io["w_ada"][0].rearrange("(k p) n -> p k n", p=P)
            for c in range(6):
                if c >= 2:
                    pool.wait_ge(mod_done, c - 1)
                pool.dma_start(wada[:, c % 2, :, :], w[:, :, c * 512:(c + 1) * 512]).then_inc(wada_in[c % 2], 16)

        @block.scalar
        def _(act):
            act.wait_ge(var_ready, 1)
            nc.scalar.activation(std, mv[:, :, 1], ACT.Sqrt).then_inc(std_ready, 1)
            act.wait_ge(modT_ready, 1)
            for n in range(16):
                k, h = n // 2, n % 2
                act.wait_ge(tr_done, n + 1)
                nc.scalar.activation(hT[:, k, h * 512:(h + 1) * 512], PS[:, n % 4, :], ACT.Identity,
                                     bias=modT[:, k:k + 1], scale=modT[:, 8 + k:9 + k]).then_inc(hT_ready, 1)

        @block.vector
        def _(dve):
            chain = Count(order)

            def link(ins, signal=chain):
                signal.by(ins)
                dve.wait_ge(signal.sem, signal.n)

            nc.vector.memset(one, 1.0)
            dve.wait_ge(rows_tr, 1)
            nc.vector.tensor_copy(cols1, PS[:, 7, 0:N_COLS1])
            nc.vector.tensor_copy(cols2, PS[:, 7, 128:192]).then_inc(rows_ready, 1)
            dve.wait_ge(rows_ready, 1)
            nc.vector.tensor_copy(cbc, cols2[:, 39:39 + KT].unsqueeze(2).to_broadcast([P, KT, P])).then_inc(cbc_ready, 1)
            for i in range(NT):
                dve.wait_ge(x_in[i // 2], 16)
                nc.vector.bn_stats(stats[:, i, 0:6], xr[:, i, 0:512])
                link(nc.vector.bn_stats(stats[:, i, 6:12], xr[:, i, 512:1024]))
            for i in range(NT):
                link(nc.vector.bn_aggr(mv[:, i, :], stats[:, i, :]))
            link(nc.vector.tensor_scalar(mv[:, :, 1], mv[:, :, 1], 1e-5, None, ALU.add), Count(var_ready))
            dve.wait_ge(std_ready, 1)
            link(nc.vector.reciprocal(std, std))
            for i in range(NT):
                nc.vector.tensor_scalar(xr[:, i, :], xr[:, i, :], mv[:, i, 0:1], std[:, i:i + 1],
                                        ALU.subtract, ALU.mult).then_inc(norm_ready, 1)
            dve.wait_ge(c_in, 16)
            for c in range(6):
                dve.wait_ge(mod_done, c + 1)
                nc.vector.tensor_tensor(mod[:, c, :], PS[:, 4 + c % 2, :], bada[:, c * 512:(c + 1) * 512],
                                        ALU.add).then_inc(mod_ready, 1)
            dve.wait_ge(mod_ready, 6)
            nc.vector.tensor_copy(gate, mod[:, 4:6, :].rearrange("p a b -> p (a b)"))
            dve.wait_ge(col_done, 1)
            link(nc.vector.tensor_copy(modT, PS[:, 6, 0:16]))
            nc.vector.tensor_scalar(modT[:, 8:16], modT[:, 8:16], 1.0, None, ALU.add).then_inc(modT_ready, 1)

        @block.tensor
        def _(pe):
            pe.wait_ge(row_in, 16 * 10)
            nc.tensor.transpose(PS[:, 7, 0:128], rows[:, 0, :], ident)
            nc.tensor.transpose(PS[:, 7, 128:256], rows[:, 1, :], ident).then_inc(rows_tr, 1)
            pe.wait_ge(cbc_ready, 1)
            for c in range(6):
                pe.wait_ge(wada_in[c % 2], 16 * (c // 2 + 1))
                if c >= 2:
                    pe.wait_ge(mod_ready, c - 1)
                for k in range(KT):
                    last = nc.tensor.matmul(PS[:, 4 + c % 2, :], cbc[:, k, :], wada[:, c % 2, k, :],
                                            start=(k == 0), stop=(k == KT - 1))
                last.then_inc(mod_done, 1)
            pe.wait_ge(mod_ready, 4)
            for k in range(16):
                last = nc.tensor.matmul(PS[:, 6, k:k + 1], mod[0:1, k // 4, (k % 4) * P:(k % 4 + 1) * P],
                                        one[0:1, 0:1], start=True, stop=True)
            last.then_inc(col_done, 1)
            pe.wait_ge(norm_ready, NT)
            for n in range(16):
                k, h = n // 2, n % 2
                if n >= 4:
                    pe.wait_ge(hT_ready, n - 3)
                for i in range(4):
                    last = nc.tensor.transpose(PS[:, n % 4, i * P:(i + 1) * P], xr[:, 4 * h + i, k * P:(k + 1) * P], ident)
                last.then_inc(tr_done, 1)


ZV, X1T = FREE1, FREE1 + 4096
LF = X1T + 4096
HS = LF + 8192
FWORK = HS + 18 * 512
GHY = FWORK + 10240


class FilterNetwork:

    def __init__(self, K):
        self.K, nc, io = K, K.nc, K.io
        s = lambda n: K.sem("fn_" + n)
        self.small_in, self.mm, self.taken, self.arg, self.sin = s("small_in"), s("mm"), s("taken"), s("arg"), s("sin")
        self.posT, self.hA, self.kk, self.wf = K.at(LF, 2048), K.at(LF + 2048, 2048), K.at(LF + 4096, 2048), K.at(LF + 6144, 3, HD)
        self.mlpc, self.h3 = K.at(MLPC, 8), K.at(H3, 2048)

    def load(self, pool):
        io, put = self.K.io, self.small_in
        for n, name in enumerate(("filt_b1", "filt_b2", "filt_b3", "filt_freq")):
            pool.dma_start(self.mlpc[0:HD, n:n + 1], io[name].rearrange("o (p a) -> p (o a)", a=1)).then_inc(put, 16)
        pool.dma_start(self.posT[0:33, :], io["posT"]).then_inc(put, 16)
        pool.dma_start(self.wf[0:33, 0, :], io["filt_w1"][0]).then_inc(put, 16)
        pool.dma_start(self.wf[0:HD, 1, :], io["filt_w2"][0]).then_inc(put, 16)
        pool.dma_start(self.wf[0:HD, 2, :], io["filt_w3"][0]).then_inc(put, 16)

    def pe(self, pe, layer):
        nc, PS = self.K.nc, self.K.PS
        if layer == 0:
            pe.wait_ge(self.small_in, 16 * 8)
        else:
            pe.wait_ge(self.sin, layer)
        rows = 33 if layer == 0 else HD
        src = self.posT if layer == 0 else self.hA
        for n in range(4):
            job = 4 * layer + n
            if job >= 2:
                pe.wait_ge(self.taken, job - 1)
            nc.tensor.matmul(PS[0:HD, 4 + job % 2, :], self.wf[0:rows, layer, :], src[0:rows, n * 512:(n + 1) * 512],
                             start=True, stop=True).then_inc(self.mm, 1)

    def dve(self, dve, link, layer):
        nc, PS = self.K.nc, self.K.PS
        taken = Count(self.taken)
        taken.n = 4 * layer
        dve.wait_ge(self.small_in, 16 * 8)
        for n in range(4):
            job = 4 * layer + n
            dve.wait_ge(self.mm, job + 1)
            link(nc.vector.tensor_scalar(self.kk[0:HD, n * 512:(n + 1) * 512], PS[0:HD, 4 + job % 2, :],
                                         self.mlpc[0:HD, layer:layer + 1], self.mlpc[0:HD, 3:4], ALU.add, ALU.mult), taken)
        reduced_sine_argument(nc, link, self.hA[0:HD, :], self.kk[0:HD, :], self.posT[0:HD, :])
        nc.vector.memset(self.posT[0:1, 0:1], 0.0).then_inc(self.arg, 1)

    def act(self, act, layer):
        act.wait_ge(self.arg, layer + 1)
        dst = self.h3 if layer == 2 else self.hA
        self.K.nc.scalar.activation(dst[0:HD, :], self.hA[0:HD, :], ACT.Sin).then_inc(self.sin, 1)


class HyenaProjections:

    def __init__(self, K, name, first, x2=None, ghy=None):
        self.K, self.x2, self.ghy = K, x2, ghy
        self.tiles = list(range(first, first + 8))
        self.wt, self.pb, self.ub = K.at(HS, 4, KT, P), K.at(HS + 4096, 2, S + 2), K.at(HS + 4096 + 2 * (S + 2), 2, S)
        self.hT, self.cols1, self.ident = K.at(HT, KT, S), K.at(COLS1, N_COLS1), K.at(IDENT, P)
        self.rows_of = [K.at(ZV, 8, CH), K.at(X1T, 8, CH)]
        s = lambda n: K.sem(name + n)
        self.w_in = [s(f"w_in{b}") for b in range(4)]
        self.proj_done, self.p_ready, self.conv_done, self.tr_done, self.z_ready, self.border_ready = (
            s(n) for n in ("proj", "p_ready", "conv", "tr", "z", "border"))

    def load(self, sp, conv):
        w = self.K.io["w_in"][0].rearrange("(k p) n -> p k n", p=P)
        for n, t in enumerate(self.tiles):
            if n >= 4:
                sp.wait_ge(self.proj_done, n - 3)
            c0 = COL_HY + t * P
            sp.dma_start(self.wt[:, n % 4, :, :], w[:, :, c0:c0 + P]).then_inc(self.w_in[n % 4], 16)
            if n >= 3:
                for t in {3: range(0, 4), 4: range(4, 6), 5: range(6, 10), 6: range(10, 16)}.get(n, ()):
                    conv.load_decay(sp, t)

    def project(self, pe, n):
        nc, PS = self.K.nc, self.K.PS
        pe.wait_ge(self.w_in[n % 4], 16 * (n // 4 + 1))
        if n >= 2:
            pe.wait_ge(self.p_ready, n - 1)
        for h in range(2):
            for k in range(KT):
                last = nc.tensor.matmul(PS[:, 2 * (n % 2) + h, :], self.wt[:, n % 4, k, :], self.hT[:, k, h * 512:(h + 1) * 512],
                                        start=(k == 0), stop=(k == KT - 1))
        last.then_inc(self.proj_done, 1)

    def to_rows(self, pe, n):
        nc, PS = self.K.nc, self.K.PS
        if self.tiles[n] >= 8:
            return
        pe.wait_ge(self.conv_done, n + 1)
        if n >= 1:
            pe.wait_ge(self.z_ready, n)
        for i in range(NT):
            last = nc.tensor.transpose(PS[:, 6 + i // 4, (i % 4) * P:(i % 4 + 1) * P], self.ub[:, n % 2, i * P:(i + 1) * P], self.ident)
        last.then_inc(self.tr_done, 1)

    def take_projection(self, act, n):
        nc, PS, t = self.K.nc, self.K.PS, self.tiles[n]
        act.wait_ge(self.proj_done, n + 1)
        if n >= 2 and t < 12:
            act.wait_ge(self.conv_done, n - 1)
        bias = self.cols1[:, COL_HY // P + t:COL_HY // P + t + 1]
        for h in range(2):
            src = PS[:, 2 * (n % 2) + h, :]
            if t < 12:
                last = nc.scalar.activation(self.pb[:, n % 2, 1 + h * 512:1 + (h + 1) * 512], src, ACT.Identity, bias=bias)
            else:
                last = nc.scalar.activation(self.ghy[:, t - 12, h * 512:(h + 1) * 512], src, ACT.Silu, bias=bias)
        last.then_inc(self.p_ready, 1)

    def take_rows(self, act, n):
        nc, PS = self.K.nc, self.K.PS
        if self.tiles[n] >= 8:
            return
        act.wait_ge(self.tr_done, n + 1)
        dst = self.rows_of[self.tiles[n] // 4][:, :, (self.tiles[n] % 4) * P:(self.tiles[n] % 4 + 1) * P]
        for h in range(2):
            last = nc.scalar.copy(dst[:, 4 * h:4 * h + 4, :], PS[:, 6 + h, :].rearrange("p (i c) -> p i c", c=P))
        last.then_inc(self.z_ready, 1)

    def border(self, dve):
        nc = self.K.nc
        nc.vector.memset(self.pb[:, :, 0:1], 0.0)
        nc.vector.memset(self.pb[:, :, S + 1:S + 2], 0.0).then_inc(self.border_ready, 1)

    def convolve(self, dve, link, n):
        nc, t, pb = self.K.nc, self.tiles[n], self.pb
        if t >= 12:
            return
        dve.wait_ge(self.p_ready, n + 1)
        if n >= 2 and t < 8:
            dve.wait_ge(self.tr_done, n - 1)
        u = self.ub[:, n % 2, :] if t < 8 else self.x2[:, t - 8, :]
        tap = lambda j: self.cols1[:, 72 + 12 * j + t:73 + 12 * j + t]
        link(nc.vector.tensor_scalar(u, pb[:, n % 2, 1:S + 1], tap(1), self.cols1[:, 108 + t:109 + t], ALU.mult, ALU.add))
        link(nc.vector.scalar_tensor_tensor(u, pb[:, n % 2, 0:S], tap(0), u, ALU.mult, ALU.add))
        nc.vector.scalar_tensor_tensor(u, pb[:, n % 2, 2:S + 2], tap(2), u, ALU.mult, ALU.add).then_inc(self.conv_done, 1)


LEAVES = {"P": (4, 0, 2), "M": (4, 4, 2), "B": (4, 8, 2), "N": (2, 12, 1), "C": (2, 14, 2)}
NAMES = "PMBNC"


def leaf_inputs(name, neg, cyc):
    return {"P": [neg[0], neg[1], neg[4], neg[5]], "M": [neg[2], neg[3], neg[6], neg[7]],
            "B": cyc[0:4], "N": cyc[4:6], "C": cyc[6:8]}[name]


def spectrum_pair(H, name, q):
    kt, first, pairs = LEAVES[name]
    return H[:, first + q, :], H[:, first + pairs + q, :]


class LongConvolution:

    def __init__(self, K, order_no):
        self.K, self.order_no, io = K, order_no, K.io
        o = FWORK
        self.w4, self.dec, self.bias_row = K.at(o, 2, CH), K.at(o + 1024, 4, CH), K.at(o + 3072, CH)
        self.cyc2 = K.at(o, 8, CH)
        self.mat, self.tmp = K.at(o + 4096, 2, 2048), K.at(o + 8192, 4, CH)
        self.z, self.x1t, self.h3 = K.at(ZV, 8, CH), K.at(X1T, 8, CH), K.at(H3, 2048)
        self.neg, self.cyc, self.H = K.at(LF, 8, CH), K.at(LF + 4096, 8, CH), K.at(HS, 18, CH)
        self.rec = {"P": K.at(LF, 4, CH), "M": K.at(LF + 2048, 4, CH), "A": K.at(LF + 4096, 4, CH), "B": K.at(LF + 6144, 4, CH)}
        r = self.rec
        self.rec_of = {"P": r["P"], "M": r["M"], "B": r["B"], "N": r["A"][:, 0:2, :], "C": r["A"][:, 2:4, :]}
        s = lambda n: K.sem(f"lc{order_no}_" + n)
        self.w_in, self.dec_in, self.mat_in = s("w_in"), [s(f"dec_in{b}") for b in range(4)], [s("mat_in0"), s("mat_in1")]
        self.f_mm, self.f_ready, self.lf_ready, self.hs_mm, self.hs_ready, self.zl_ready, self.zs_mm, self.zs_ready, self.iv_mm, self.iv_ready = (
            s(n) for n in ("f_mm", "f_ready", "lf", "hs_mm", "hs", "zl", "zs_mm", "zs", "iv_mm", "iv"))
        self.matrices = [("fwd_" + n) for n in NAMES] * 2 + [("inv_" + n) for n in NAMES]
        self.jobs = 16 if order_no == 0 else 20

    def matrix(self, n):
        rows, cols = self.K.io[self.matrices[n]].shape
        return self.mat[:, n % 2, 0:rows // P * cols].rearrange("p (k c) -> p k c", c=cols)

    def used_after(self, stage, name):
        kt, first, pairs = LEAVES[name]
        if stage < 2:
            return first + 2 * pairs
        upto = NAMES[:NAMES.index(name) + 1]
        return 4 * len(upto) if self.order_no else sum(self.K.io["inv_" + m].shape[1] // P for m in upto)

    def load_filter(self, sp):
        io = self.K.io
        for d in range(2):
            c0 = self.order_no * 1024 + d * CH
            sp.dma_start(self.w4[0:HD, d, :], io["filt_w4"][0, :, c0:c0 + CH]).then_inc(self.w_in, 16)
        sp.dma_start(self.bias_row[0:1, :], io["filt_bias"][0, self.order_no:self.order_no + 1, :]).then_inc(self.w_in, 16)

    def load_decay(self, queue, t):
        if t >= 4:
            queue.wait_ge(self.f_ready, t - 3)
        queue.dma_start(self.dec[:, t % 4, :], self.K.io["decay"][t * P:(t + 1) * P, :]).then_inc(self.dec_in[t % 4], 16)

    def load_matrices(self, pool):
        for n, name in enumerate(self.matrices):
            if n >= 2:
                pool.wait_ge((self.hs_mm, self.zs_mm, self.iv_mm)[(n - 2) // 5], self.used_after((n - 2) // 5, NAMES[(n - 2) % 5]))
            pool.dma_start(self.matrix(n), self.K.io[name].rearrange("(k p) c -> p k c", p=P)).then_inc(self.mat_in[n % 2], 16)

    def filter_rows(self, pe, t0, t1):
        if t0 == 0:
            pe.wait_ge(self.w_in, 48)
        for t in range(t0, t1):
            if t >= 2:
                pe.wait_ge(self.f_ready, t - 1)
            self.K.nc.tensor.matmul(self.K.PS[:, 4 + t % 2, :], self.h3[0:HD, t * P:(t + 1) * P], self.w4[0:HD, t // 8, :],
                                    start=True, stop=True).then_inc(self.f_mm, 1)

    def forward(self, pe, n, name, neg_in, cyc_in, mm_sem, bank_free):
        kt, first, pairs = LEAVES[name]
        ins, m = leaf_inputs(name, [neg_in[:, i, :] for i in range(8)], [cyc_in[:, i, :] for i in range(8)]), self.matrix(n)
        pe.wait_ge(self.mat_in[n % 2], 16 * (n // 2 + 1))
        f = m.shape[2] // 2
        for q in range(pairs):
            for part in range(2):
                t = first + 2 * q + part
                bank_free(t)
                for k in range(kt):
                    last = self.K.nc.tensor.matmul(self.K.PS[:, t % 8, :], m[:, k, part * f + q * P:part * f + (q + 1) * P], ins[k],
                                                   start=(k == 0), stop=(k == kt - 1))
                last.then_inc(mm_sem, 1)

    def spectra(self, pe):
        def bank_free_h(t):
            if t >= 8:
                pe.wait_ge(self.hs_ready, t - 7)

        def bank_free_z(t):
            if t < 8:
                pe.wait_ge(self.hs_ready, 18)
            elif t % 2 == 0:
                pe.wait_ge(self.zs_ready, t // 2 - 3)

        pe.wait_ge(self.lf_ready, 1)
        for n, name in enumerate(NAMES):
            self.forward(pe, n, name, self.neg, self.cyc, self.hs_mm, bank_free_h)
        pe.wait_ge(self.zl_ready, 1)
        for n, name in enumerate(NAMES):
            self.forward(pe, 5 + n, name, self.z, self.cyc2, self.zs_mm, bank_free_z)

    def inverse(self, pe):
        nc, PS, H, job = self.K.nc, self.K.PS, self.H, 0
        for n, name in enumerate(NAMES):
            kt, first, pairs = LEAVES[name]
            m = self.matrix(10 + n)
            freq = 2 * pairs
            out_tiles = m.shape[2] // P
            pe.wait_ge(self.mat_in[(10 + n) % 2], 16 * ((10 + n) // 2 + 1))
            pe.wait_ge(self.zs_ready, 9)
            for i in range(out_tiles if self.order_no == 0 else 4):
                if job >= 8:
                    pe.wait_ge(self.iv_ready, job - 7)
                for k in range(freq):
                    if self.order_no == 0:
                        last = nc.tensor.matmul(PS[:, job % 8, :], m[:, k, i * P:(i + 1) * P], H[:, first + k, :],
                                                start=(k == 0), stop=(k == freq - 1))
                    else:
                        last = nc.tensor.matmul(PS[:, job % 8, 0:out_tiles * P], H[:, first + k, i * P:(i + 1) * P], m[:, k, :],
                                                start=(k == 0), stop=(k == freq - 1))
                last.then_inc(self.iv_mm, 1)
                job += 1

    def take_filter_spectra(self, act):
        t = 0
        for name in NAMES:
            for q in range(LEAVES[name][2]):
                for dst in spectrum_pair(self.H, name, q):
                    act.wait_ge(self.hs_mm, t + 1)
                    self.K.nc.scalar.copy(dst, self.K.PS[:, t % 8, :]).then_inc(self.hs_ready, 1)
                    t += 1

    def take_inverse(self, act):
        nc, PS, job = self.K.nc, self.K.PS, 0
        for name in NAMES:
            out_tiles = self.K.io["inv_" + name].shape[1] // P
            act.wait_ge(self.zs_ready, 9)
            for i in range(out_tiles if self.order_no == 0 else 4):
                act.wait_ge(self.iv_mm, job + 1)
                if self.order_no == 0:
                    nc.scalar.copy(self.rec_of[name][:, i, :], PS[:, job % 8, :]).then_inc(self.iv_ready, 1)
                else:
                    dst = self.rec_of[name][:, :, i * P:(i + 1) * P]
                    nc.scalar.copy(dst, PS[:, job % 8, 0:out_tiles * P].rearrange("p (a b) -> p a b", b=P)).then_inc(self.iv_ready, 1)
                job += 1

    def total_and_difference(self, link, a, b):
        nc = self.K.nc
        link(nc.vector.tensor_tensor(b, a, b, ALU.add))
        link(nc.vector.scalar_tensor_tensor(a, a, 2.0, b, ALU.mult, ALU.subtract))

    def split_negacyclic(self, link, v):
        nc = self.K.nc
        self.total_and_difference(link, v[:, 2:4, :], v[:, 6:8, :])
        for lo, hi in ((0, 2), (4, 6)):
            link(nc.vector.scalar_tensor_tensor(v[:, hi:hi + 2, :], v[:, hi:hi + 2, :], -R2, v[:, lo:lo + 2, :], ALU.mult, ALU.add))
            link(nc.vector.scalar_tensor_tensor(v[:, lo:lo + 2, :], v[:, lo:lo + 2, :], 2.0, v[:, hi:hi + 2, :], ALU.mult, ALU.subtract))

    def decay_rows(self, dve, t0, t1):
        for t in range(t0, t1):
            dve.wait_ge(self.f_mm, t + 1)
            dve.wait_ge(self.dec_in[t % 4], 16 * (t // 4 + 1))
            dst = (self.neg if t < 8 else self.cyc)[:, t % 8, :]
            self.K.nc.vector.tensor_tensor(dst, self.K.PS[:, 4 + t % 2, :], self.dec[:, t % 4, :], ALU.mult).then_inc(self.f_ready, 1)

    def filter_leaves(self, dve, link):
        nc, neg, cyc = self.K.nc, self.neg, self.cyc
        dve.wait_ge(self.f_ready, 16)
        link(nc.vector.tensor_tensor(neg[0:1, 0, :], neg[0:1, 0, :], self.bias_row[0:1, :], ALU.add))
        self.total_and_difference(link, neg[:, :, :], cyc[:, :, :])
        self.total_and_difference(link, cyc[:, 0:4, :], cyc[:, 4:8, :])
        self.total_and_difference(link, cyc[:, 4:6, :], cyc[:, 6:8, :])
        self.split_negacyclic(link, neg)
        nc.vector.memset(self.tmp[:, 0, 0:1], 0.0).then_inc(self.lf_ready, 1)

    def z_leaves(self, dve, link):
        nc, z, cyc = self.K.nc, self.z, self.cyc2
        link(nc.vector.tensor_tensor(cyc[:, 0:4, :], z[:, 0:4, :], z[:, 4:8, :], ALU.subtract))
        link(nc.vector.tensor_tensor(cyc[:, 4:8, :], z[:, 0:4, :], z[:, 4:8, :], ALU.add))
        self.total_and_difference(link, cyc[:, 4:6, :], cyc[:, 6:8, :])
        self.split_negacyclic(link, z)
        nc.vector.memset(self.tmp[:, 0, 0:1], 0.0).then_inc(self.zl_ready, 1)

    def multiply_spectra(self, dve, link):
        nc, PS, H, tmp, pair = self.K.nc, self.K.PS, self.H, self.tmp, 0
        dve.wait_ge(self.hs_ready, 18)
        for name in NAMES:
            kt, first, pairs = LEAVES[name]
            for q in range(pairs):
                t = first + 2 * q
                dve.wait_ge(self.zs_mm, t + 2)
                if pair:
                    dve.wait_ge(self.zs_ready, pair)
                else:
                    dve.wait_ge(self.zl_ready, 1)
                pair += 1
                hr, hi = spectrum_pair(H, name, q)
                zr, zi = PS[:, t % 8, :], PS[:, (t + 1) % 8, :]
                for dst, a, b in ((0, zr, hr), (1, zi, hi), (2, zr, hi)):
                    nc.vector.tensor_tensor(tmp[:, dst, :], a, b, ALU.mult)
                link(nc.vector.tensor_tensor(tmp[:, 3, :], zi, hr, ALU.mult))
                nc.vector.tensor_tensor(hr, tmp[:, 0, :], tmp[:, 1, :], ALU.subtract)
                nc.vector.tensor_tensor(hi, tmp[:, 2, :], tmp[:, 3, :], ALU.add).then_inc(self.zs_ready, 1)

    def recombine(self, dve, link):
        nc, y = self.K.nc, self.z
        Pm, Mm, Am, Bm = self.rec["P"], self.rec["M"], self.rec["A"], self.rec["B"]
        self.total_and_difference(link, Pm, Mm)
        self.total_and_difference(link, Pm[:, 0:2, :], Pm[:, 2:4, :])
        link(nc.vector.tensor_tensor(Am[:, 0:2, :], Am[:, 0:2, :], Am[:, 2:4, :], ALU.add))
        link(nc.vector.scalar_tensor_tensor(Am[:, 2:4, :], Am[:, 2:4, :], 2.0, Am[:, 0:2, :], ALU.mult, ALU.subtract))
        self.total_and_difference(link, Am, Bm)
        link(nc.vector.tensor_tensor(y[:, 0:2, :], Mm[:, 0:2, :], Bm[:, 0:2, :], ALU.add))
        link(nc.vector.scalar_tensor_tensor(y[:, 2:4, :], Pm[:, 2:4, :], R2, Bm[:, 2:4, :], ALU.mult, ALU.add))
        link(nc.vector.tensor_tensor(y[:, 4:6, :], Mm[:, 2:4, :], Am[:, 0:2, :], ALU.add))
        link(nc.vector.scalar_tensor_tensor(y[:, 6:8, :], Pm[:, 0:2, :], -R2, Am[:, 2:4, :], ALU.mult, ALU.add))


def hyena(K):
    nc = K.nc
    x2, ghy, yT = K.at(X1T, 4, S), K.at(GHY, 4, S), K.at(X1T, 4, S)
    with ExitStack() as ctx:
        order, yT_ready = K.sem("hyena_order"), K.sem("hyena_y")
        net = FilterNetwork(K)
        hy = [HyenaProjections(K, "hy0_", 0), HyenaProjections(K, "hy8_", 8, x2, ghy)]
        lc = [LongConvolution(K, 0), LongConvolution(K, 1)]
        rows_after = {3: (0, 6), 4: (6, 12), 5: (12, 16)}
        block = ctx.enter_context(nc.Block())

        @block.sync
        def _(sp):
            for o in range(2):
                if o == 1:
                    sp.wait_ge(lc[0].zs_mm, 18)
                lc[o].load_filter(sp)
                if o == 1:
                    sp.wait_ge(lc[0].iv_mm, lc[0].jobs)
                hy[o].load(sp, lc[o])

        @block.gpsimd
        def _(pool):
            net.load(pool)
            lc[0].load_matrices(pool)
            pool.wait_ge(lc[0].iv_mm, lc[0].jobs)
            lc[1].load_matrices(pool)

        @block.tensor
        def _(pe):
            for o in range(2):
                if o == 1:
                    pe.wait_ge(lc[0].iv_ready, lc[0].jobs)
                for n in range(8):
                    hy[o].project(pe, n)
                    if n >= 2:
                        hy[o].to_rows(pe, n - 2)
                    if o == 0 and n < 3:
                        net.pe(pe, n)
                    if n in rows_after:
                        if o == 0 and n == 3:
                            pe.wait_ge(net.sin, 3)
                            pe.wait_ge(net.taken, 12)
                        lc[o].filter_rows(pe, *rows_after[n])
                hy[o].to_rows(pe, 6)
                hy[o].to_rows(pe, 7)
                pe.wait_ge(hy[o].p_ready, 8)
                if o == 0:
                    pe.wait_ge(hy[o].z_ready, 8)
                lc[o].spectra(pe)
                lc[o].inverse(pe)

        @block.scalar
        def _(act):
            for o in range(2):
                act.wait_ge(hy[o].border_ready, 1)
                for n in range(8):
                    hy[o].take_projection(act, n)
                    if n >= 2:
                        hy[o].take_rows(act, n - 2)
                    if o == 0 and n < 3:
                        net.act(act, n)
                hy[o].take_rows(act, 6)
                hy[o].take_rows(act, 7)
                lc[o].take_filter_spectra(act)
                lc[o].take_inverse(act)

        @block.vector
        def _(dve):
            chain = Count(order)

            def link(ins, signal=chain):
                signal.by(ins)
                dve.wait_ge(signal.sem, signal.n)

            for o in range(2):
                if o == 1:
                    dve.wait_ge(lc[0].iv_ready, lc[0].jobs)
                hy[o].border(dve)
                if o == 1:
                    lc[0].recombine(dve, link)
                    link(nc.vector.tensor_tensor(lc[0].z, lc[0].z, lc[0].x1t, ALU.mult))
                for n in range(8):
                    hy[o].convolve(dve, link, n)
                    if o == 0 and n < 3:
                        net.dve(dve, link, n)
                    if n in rows_after:
                        lc[o].decay_rows(dve, *rows_after[n])
                    if n == 5:
                        lc[o].filter_leaves(dve, link)
                if o == 0:
                    dve.wait_ge(hy[0].z_ready, 8)
                lc[o].z_leaves(dve, link)
                lc[o].multiply_spectra(dve, link)
            dve.wait_ge(lc[1].iv_ready, lc[1].jobs)
            lc[1].recombine(dve, link)
            for c in range(4):
                yc = lc[1].z[:, :, c * P:(c + 1) * P]
                blocks = lambda a: a.rearrange("p (a b) -> p a b", b=P)
                link(nc.vector.tensor_tensor(blocks(yT[:, c, :]), yc, blocks(x2[:, c, :]), ALU.mult))
                link(nc.vector.tensor_tensor(yT[:, c, :], yT[:, c, :], ghy[:, c, :], ALU.mult))


YATT, YHY = ZV, X1T
SLOPES = [2.0 ** (-(h + 1)) for h in range(8)]
TILES = 10
UNITS = 32


def unit_kind(u):
    return u < 16, (u % 16) // 2, u % 2


def first_key(i):
    return min(max(P * i - 64, 0), S - 256)


V_TILES = ([(0, 0, 1), (0, 128, 1)] + [(0, 64 + P * m, 1) for m in range(7)] + [(0, 768, 1), (0, 896, 1)]
           + [(1, c + 512 * half, 4) for c in range(4) for half in range(2)] + [(2, r, 8) for r in range(8)])
V_GROUPS = [list(range(g, min(g + 4, len(V_TILES)))) for g in range(0, len(V_TILES), 4)]


def unit_blocks(u):
    strided, i, _ = unit_kind(u)
    if strided:
        return [V_TILES.index((1, i % 4, 4)), V_TILES.index((1, i % 4 + 512, 4)), V_TILES.index((2, i, 8))]
    return [V_TILES.index((0, first_key(i), 1)), V_TILES.index((0, first_key(i) + P, 1))]


def dilated_attention(K):
    nc, io, PS = K.nc, K.io, K.PS
    o = LF
    wt = K.at(o, 2, KT, P); o += 2 * 1024
    qk = K.at(o, 2, 6, S); o += 12 * S
    vT = K.at(o, 3, S); o += 3 * S
    gat = K.at(o, 2, S); o += 2 * S
    vrows = K.at(o, 27, P); o += 27 * P
    dist = K.at(o, 1536); o += 1536
    bias = K.at(o, 2, 1536); o += 3072
    sb = K.at(o, 3, 384); o += 3 * 384
    st_b = K.at(o, 8, 2, 66); o += 1056
    outs = K.at(o, NT, P); o += NT * P
    back = K.at(o, 8, 2, 66); o += 1056
    o = H3
    pt = K.at(o, 2, 384); o += 768
    st_a = K.at(o, 8, 2, 66); o += 1056
    nm = K.at(o, 4); o += 4
    mx = K.at(o, 16); o += 16
    ex = K.at(o, 2, 16); o += 32
    den = K.at(o, 16); o += 16
    assert o <= FREE1
    yT, hT, cols1, ident = K.at(YATT, 4, S), K.at(HT, KT, S), K.at(COLS1, N_COLS1), K.at(IDENT, P)
    w = io["w_in"][0].rearrange("(k p) n -> p k n", p=P)
    scratch = nc.dram_tensor("strided_sums", (S, 132), fp32, kind="Internal").ap()
    pairs = 4
    halves = 2 * TILES

    def tile_column(T):
        j, t = T // TILES, T % TILES
        return (36 + j) if t == 9 else (t // 3) * 12 + (t % 3) * 4 + j

    def dest(T):
        j, t = T // TILES, T % TILES
        return gat[:, j % 2, :] if t == 9 else (vT[:, t - 6, :] if t >= 6 else qk[:, j % 2, t, :])

    def projections(j):
        after = [[] for _ in range(UNITS + 1)]
        if j + 1 < pairs:
            for n in range(halves):
                after[min(2 * n, UNITS) if n < 16 else UNITS].append((j + 1) * halves + n)
        return after

    def bank_of_t(j, n):
        g = j * 41 + n
        return g, 2 + g % 2

    with ExitStack() as ctx:
        s = lambda n: K.sem("da_" + n)
        w_in, dist_in = [s(f"w_in{b}") for b in range(2)], s("dist_in")
        proj_mm, proj_ready, order = s("proj_mm"), s("proj_ready"), s("order")
        t_done, t_taken, bias_ready = s("t_done"), s("t_taken"), s("bias")
        s_done, s_taken, nm_ready, exp_done, pv_done, o_ready = s("s_done"), s("s_taken"), s("nm"), s("exp"), s("pv"), s("o")
        sums_out, sums_in, comb_d, comb_e, comb_done, y_ready = s("sums_out"), s("sums_in"), s("comb_d"), s("comb_e"), s("comb"), s("y")
        block = ctx.enter_context(nc.Block())

        @block.sync
        def _(sp):
            sp.dma_start(dist, io["dist"]).then_inc(dist_in, 16)

            def load(T):
                if T >= 2:
                    sp.wait_ge(proj_mm, 2 * (T - 1))
                c0 = tile_column(T) * P
                sp.dma_start(wt[:, T % 2, :, :], w[:, :, c0:c0 + P]).then_inc(w_in[T % 2], 16)

            for T in range(TILES * pairs):
                load(T)

        @block.gpsimd
        def _(pool):
            for j in range(pairs):
                pool.wait_ge(o_ready, UNITS * j + 16)
                pool.dma_start(scratch.rearrange("(n r) c -> n r c", r=8), st_b.rearrange("p r h c -> p r (h c)")).then_inc(sums_out, 16)
                pool.wait_ge(sums_out, 16 * (j + 1))
                if j >= 1:
                    pool.wait_ge(comb_done, j)
                pool.dma_start(back.rearrange("p r h c -> p r (h c)"), scratch.rearrange("(i p) c -> p i c", p=P)).then_inc(sums_in, 16)

        @block.tensor
        def _(pe):
            def project(n):
                T, h = n // 2, n % 2
                pe.wait_ge(w_in[T % 2], 16 * (T // 2 + 1))
                if n >= 2:
                    pe.wait_ge(proj_ready, n - 1)
                for k in range(KT):
                    last = nc.tensor.matmul(PS[:, 6 + h, :], wt[:, T % 2, k, :], hT[:, k, h * 512:(h + 1) * 512],
                                            start=(k == 0), stop=(k == KT - 1))
                last.then_inc(proj_mm, 1)

            def transposes(j, n, sources):
                g, b = bank_of_t(j, n)
                if g >= 2:
                    pe.wait_ge(t_taken, g - 1)
                for i, src in enumerate(sources):
                    last = nc.tensor.transpose(PS[:, b, i * P:(i + 1) * P], src, ident)
                last.then_inc(t_done, 1)

            def scores(j, u):
                U = UNITS * j + u
                strided, i, h = unit_kind(u)
                if U >= 2:
                    pe.wait_ge(s_taken, U - 1)
                head = slice(64 * h, 64 * h + 64)
                q = lambda g: qk[head, j % 2, g, :]
                k = lambda g: qk[head, j % 2, 3 + g, :]
                b = PS[:, U % 2, :]
                if strided:
                    nc.tensor.matmul(b[:, 0:256], q(1)[:, i:S:8], k(1)[:, i % 4:S:4], start=True, stop=True)
                    last = nc.tensor.matmul(b[:, 256:384], q(2)[:, i:S:8], k(2)[:, i:S:8], start=True, stop=True)
                else:
                    k0 = first_key(i)
                    last = nc.tensor.matmul(b[:, 0:256], q(0)[:, i * P:(i + 1) * P], k(0)[:, k0:k0 + 256], start=True, stop=True)
                last.then_inc(s_done, 1)

            def prob_transposes(j, u):
                U = UNITS * j + u
                pe.wait_ge(exp_done, U + 1)
                transposes(j, 7 + u, [sb[:, U % 3, b * P:(b + 1) * P] for b in range(len(unit_blocks(u)))])

            def values(j, u):
                U = UNITS * j + u
                _, _, h = unit_kind(u)
                pe.wait_ge(t_taken, bank_of_t(j, 7 + u)[0] + 1)
                if U >= 2:
                    pe.wait_ge(o_ready, U - 1)
                blocks = unit_blocks(u)
                for b, v in enumerate(blocks):
                    last = nc.tensor.matmul(PS[:, 4 + U % 2, 0:HD], pt[:, U % 2, b * P:(b + 1) * P], vrows[:, v, h * HD:(h + 1) * HD],
                                            start=(b == 0), stop=(b == len(blocks) - 1))
                last.then_inc(pv_done, 1)

            for n in range(halves):
                project(n)
            for j in range(pairs):
                pe.wait_ge(proj_ready, halves * (j + 1))
                for g, tiles in enumerate(V_GROUPS):
                    transposes(j, g, [vT[:, V_TILES[v][0], V_TILES[v][1]:V_TILES[v][1] + P * V_TILES[v][2] - V_TILES[v][2] + 1:V_TILES[v][2]] for v in tiles])
                extra = projections(j)
                for u in range(UNITS + 2):
                    if u < UNITS:
                        scores(j, u)
                        for n in extra[u]:
                            project(n)
                    if 1 <= u <= UNITS:
                        prob_transposes(j, u - 1)
                    if u >= 2:
                        values(j, u - 2)
                for n in extra[UNITS]:
                    project(n)
                pe.wait_ge(comb_done, j + 1)
                for g in range(2):
                    transposes(j, 39 + g, [outs[:, i, :] for i in range(4 * g, 4 * g + 4)])

        @block.scalar
        def _(act):
            def take_projection(n):
                T, h = n // 2, n % 2
                t = T % TILES
                act.wait_ge(proj_mm, n + 1)
                if t == 9 and T // TILES >= 2:
                    act.wait_ge(y_ready, T // TILES - 1)
                c = tile_column(T)
                nc.scalar.activation(dest(T)[:, h * 512:(h + 1) * 512], PS[:, 6 + h, :], ACT.Silu if t == 9 else ACT.Identity,
                                     bias=cols1[:, c:c + 1]).then_inc(proj_ready, 1)

            def stats_of(u):
                strided, i, h = unit_kind(u)
                return (st_b if strided else st_a)[:, i, h, :]

            def exponentials(j, u):
                U = UNITS * j + u
                n = 384 if unit_kind(u)[0] else 256
                act.wait_ge(nm_ready, U + 1)
                nc.scalar.activation(sb[:, U % 3, 0:n], sb[:, U % 3, 0:n], ACT.Exp, bias=nm[:, U % 4:U % 4 + 1], scale=0.125,
                                     accum_out=stats_of(u)[:, 64:65]).then_inc(exp_done, 1)

            def take_output(j, u):
                U = UNITS * j + u
                act.wait_ge(pv_done, U + 1)
                nc.scalar.copy(stats_of(u)[:, 0:HD], PS[:, 4 + U % 2, 0:HD]).then_inc(o_ready, 1)

            for n in range(halves):
                take_projection(n)
            for j in range(pairs):
                if j >= 1:
                    act.wait_ge(sums_out, 16 * j)
                    act.wait_ge(comb_done, j)
                extra = projections(j)
                for u in range(UNITS + 2):
                    if u < UNITS:
                        exponentials(j, u)
                        for n in extra[u]:
                            take_projection(n)
                    if u >= 2:
                        take_output(j, u - 2)
                act.wait_ge(comb_d, j + 1)
                nc.scalar.activation(ex, ex, ACT.Exp, scale=0.125).then_inc(comb_e, 1)
                for n in extra[UNITS]:
                    take_projection(n)

        @block.vector
        def _(dve):
            chain = Count(order)
            done = Count(comb_done)
            diff = Count(comb_d)

            def link(ins, signal=chain):
                signal.by(ins)
                dve.wait_ge(signal.sem, signal.n)

            def take_scores(j, u):
                U = UNITS * j + u
                strided, i, h = unit_kind(u)
                n = 384 if strided else 256
                col = 768 + 384 * (i // 4) if strided else 256 * (0 if i == 0 else 2 if i == NT - 1 else 1)
                st = (st_b if strided else st_a)[:, i, h, :]
                dve.wait_ge(s_done, U + 1)
                if U >= 3:
                    dve.wait_ge(t_done, bank_of_t((U - 3) // UNITS, 7 + (U - 3) % UNITS)[0] + 1)
                nc.vector.tensor_tensor_reduce(out=sb[:, U % 3, 0:n], in0=PS[:, U % 2, 0:n], in1=bias[:, h, col:col + n],
                                               scale=1.0, scalar=-3e38, op0=ALU.add, op1=ALU.max, accum_out=st[:, 65:66]).then_inc(s_taken, 1)
                dve.wait_ge(s_taken, U + 1)
                nc.vector.tensor_scalar(nm[:, U % 4:U % 4 + 1], st[:, 65:66], -0.125, None, ALU.mult).then_inc(nm_ready, 1)

            def take_transposes(j, n, dst, wait=None):
                g, b = bank_of_t(j, n)
                dve.wait_ge(t_done, g + 1)
                cols = dst.shape[1] * (dst.shape[2] if len(dst.shape) == 3 else 1)
                src = PS[:, b, 0:cols]
                if len(dst.shape) == 3:
                    src = src.rearrange("p (a b) -> p a b", a=dst.shape[1])
                return src

            for j in range(pairs):
                if j == 0:
                    dve.wait_ge(dist_in, 16)
                else:
                    dve.wait_ge(s_taken, UNITS * j)
                for h in range(2):
                    link(nc.vector.tensor_scalar(bias[:, h, :], dist, -8.0 * SLOPES[2 * j + h], None, ALU.mult))
                for g, tiles in enumerate(V_GROUPS):
                    dst = vrows[:, tiles[0]:tiles[-1] + 1, :]
                    nc.vector.tensor_copy(dst, take_transposes(j, g, dst)).then_inc(t_taken, 1)
                if j >= 1:
                    dve.wait_ge(sums_out, 16 * j)
                for u in range(UNITS + 1):
                    if u < UNITS:
                        take_scores(j, u)
                    if u >= 1:
                        U = UNITS * j + u - 1
                        if U >= 2:
                            dve.wait_ge(pv_done, U - 1)
                        n = 384 if unit_kind(u - 1)[0] else 256
                        dst = pt[:, U % 2, 0:n]
                        nc.vector.tensor_copy(dst, take_transposes(j, 6 + u, dst)).then_inc(t_taken, 1)
                dve.wait_ge(o_ready, UNITS * (j + 1))
                dve.wait_ge(sums_in, 16 * (j + 1))
                pick = lambda st, c: st[:, :, :, c:c + 1].rearrange("p r h c -> p (r h) c")[:, :, 0]
                link(nc.vector.tensor_tensor(mx, pick(st_a, 65), pick(back, 65), ALU.max))
                link(nc.vector.tensor_tensor(ex[:, 0, :], pick(st_a, 65), mx, ALU.subtract))
                link(nc.vector.tensor_tensor(ex[:, 1, :], pick(back, 65), mx, ALU.subtract), diff)
                dve.wait_ge(comb_e, j + 1)
                link(nc.vector.tensor_tensor(mx, pick(st_a, 64), ex[:, 0, :], ALU.mult))
                link(nc.vector.tensor_tensor(den, pick(back, 64), ex[:, 1, :], ALU.mult))
                link(nc.vector.tensor_tensor(den, den, mx, ALU.add))
                link(nc.vector.reciprocal(den, den))
                for n in range(2):
                    link(nc.vector.tensor_tensor(ex[:, n, :], ex[:, n, :], den, ALU.mult))
                for n, st in enumerate((st_a, back)):
                    v = st[:, :, :, 0:HD].rearrange("p r h c -> p (r h) c")
                    link(nc.vector.tensor_tensor(v, v, ex[:, n, :].unsqueeze(2).to_broadcast([P, 16, HD]), ALU.mult))
                    if n == 1:
                        link(nc.vector.tensor_tensor(outs.rearrange("p r (h c) -> p (r h) c", h=2), v,
                                                     st_a[:, :, :, 0:HD].rearrange("p r h c -> p (r h) c"), ALU.add), done)
                for g in range(2):
                    dst = yT[:, j, g * 512:(g + 1) * 512]
                    ins = nc.vector.tensor_tensor(dst, take_transposes(j, 39 + g, dst), gat[:, j % 2, g * 512:(g + 1) * 512], ALU.mult)
                    ins.then_inc(t_taken, 1)
                dve.wait_ge(t_taken, bank_of_t(j, 40)[0] + 1)
                nc.vector.memset(mx[:, 0:1], 0.0).then_inc(y_ready, 1)


WPROJ = LF
MERGED = 34176
WOUT = MERGED + 8192


def merge_branches(K):
    nc, io, PS = K.nc, K.io, K.PS
    wp = K.at(WPROJ, 2, 4, D)
    wr = K.at(WPROJ + 8192, 2, 2, KT, P)
    tmp = K.at(WPROJ + 8192 + 4096, 2, 2, 512)
    sg = K.at(H3, 2, 2, 512)
    hT, cols1, merged, wout = K.at(HT, KT, S), K.at(COLS1, N_COLS1), K.at(MERGED, KT, S), K.at(WOUT, KT, D)
    branch = [K.at(YATT, 4, S), K.at(YHY, 4, S)]
    w = io["w_in"][0].rearrange("(k p) n -> p k n", p=P)
    with ExitStack() as ctx:
        s = lambda n: K.sem("mg_" + n)
        w_in, wp_in, wout_in = [s("w_in0"), s("w_in1")], s("wp_in"), s("wout_in")
        r_mm, y_mm, sig_ready, merged_ready, order = s("r_mm"), s("y_mm"), s("sig"), s("merged"), s("order")
        block = ctx.enter_context(nc.Block())

        @block.sync
        def _(sp):
            def load(k):
                if k >= 2:
                    sp.wait_ge(r_mm, 2 * (k - 1))
                for a in range(2):
                    c0 = COL_R + a * D + k * P
                    sp.dma_start(wr[:, k % 2, a, :, :], w[:, :, c0:c0 + P]).then_inc(w_in[k % 2], 16)

            load(0)
            for a, name in enumerate(("w_proj_attn", "w_proj_hyena")):
                sp.dma_start(wp[:, a, :, :], io[name][0].rearrange("(k p) n -> p k n", p=P)).then_inc(wp_in, 16)
            load(1)
            sp.dma_start(wout, io["w_out"][0].rearrange("(k p) n -> p k n", p=P)).then_inc(wout_in, 16)
            for k in range(2, KT):
                load(k)
            sp.wait_ge(wout_in, 16)

        @block.tensor
        def _(pe):
            for k in range(KT):
                pe.wait_ge(w_in[k % 2], 32 * (k // 2 + 1))
                for h in range(2):
                    n = 2 * k + h
                    b = 4 * (n % 2)
                    if n >= 2:
                        pe.wait_ge(sig_ready, n - 1)
                    for a in range(2):
                        for c in range(KT):
                            last = nc.tensor.matmul(PS[:, b + a, :], wr[:, k % 2, a, c, :], hT[:, c, h * 512:(h + 1) * 512],
                                                    start=(c == 0), stop=(c == KT - 1))
                    last.then_inc(r_mm, 1)
                    if n == 0:
                        pe.wait_ge(wp_in, 32)
                    if n >= 2:
                        pe.wait_ge(merged_ready, n - 1)
                    for a in range(2):
                        for c in range(4):
                            last = nc.tensor.matmul(PS[:, b + 2 + a, :], wp[:, a, c, k * P:(k + 1) * P], branch[a][:, c, h * 512:(h + 1) * 512],
                                                    start=(c == 0), stop=(c == 3))
                    last.then_inc(y_mm, 1)

        @block.scalar
        def _(act):
            for n in range(2 * KT):
                k = n // 2
                act.wait_ge(r_mm, n + 1)
                if n >= 2:
                    act.wait_ge(merged_ready, n - 1)
                for a in range(2):
                    col = COL_R // P + 8 * a + k
                    last = nc.scalar.activation(sg[:, n % 2, a, :], PS[:, 4 * (n % 2) + a, :], ACT.Sigmoid, bias=cols1[:, col:col + 1])
                last.then_inc(sig_ready, 1)

        @block.vector
        def _(dve):
            chain = Count(order)

            def link(ins, signal=chain):
                signal.by(ins)
                dve.wait_ge(signal.sem, signal.n)

            for n in range(2 * KT):
                k, h, b = n // 2, n % 2, 4 * (n % 2)
                dve.wait_ge(sig_ready, n + 1)
                dve.wait_ge(y_mm, n + 1)
                for a in range(2):
                    last = nc.vector.tensor_tensor(tmp[:, n % 2, a, :], PS[:, b + 2 + a, :], sg[:, n % 2, a, :], ALU.mult)
                link(last)
                nc.vector.tensor_tensor(merged[:, k, h * 512:(h + 1) * 512], tmp[:, n % 2, 0, :], tmp[:, n % 2, 1, :], ALU.add).then_inc(merged_ready, 1)


VECS = 1408 + 64
X2T = 11648
X2R = X2T + 8192


class RowNorm:

    def __init__(self, nc, dve, link, stat, var_signal, std_sem):
        self.nc, self.dve, self.link, self.stat, self.var, self.std = nc, dve, link, stat, var_signal, std_sem

    def __call__(self, row, gamma, beta, final=None):
        nc, st = self.nc, self.stat
        self.link(nc.vector.bn_stats(st[:, 0:6], row[:, 0:512]))
        self.link(nc.vector.bn_stats(st[:, 6:12], row[:, 512:1024]))
        self.link(nc.vector.bn_aggr(st[:, 12:14], st[:, 0:12]))
        self.link(nc.vector.tensor_scalar(st[:, 14:15], st[:, 13:14], 1e-5, None, ALU.add), self.var)
        self.dve.wait_ge(self.std, self.var.n)
        self.link(nc.vector.reciprocal(st[:, 15:16], st[:, 15:16]))
        self.link(nc.vector.tensor_scalar(row, row, st[:, 12:13], st[:, 15:16], ALU.subtract, ALU.mult))
        self.link(nc.vector.tensor_tensor(row, row, gamma, ALU.mult))
        self.link(nc.vector.tensor_tensor(row, row, beta, ALU.add), *([final] if final else []))


def first_output(K):
    nc, io, PS = K.nc, K.io, K.PS
    vec = K.at(VECS, 5, D)
    xin = K.at(VECS + 5 * D, 2, D)
    work = K.at(VECS + 7 * D, 2, D)
    stat = K.at(28032, 16)
    gate, merged, wout, ident = K.at(GATE, D), K.at(MERGED, KT, S), K.at(WOUT, KT, D), K.at(IDENT, P)
    x2r, x2T = K.at(X2R, NT, D), K.at(X2T, KT, S)
    x_class = io["x"][0].rearrange("(n r) d -> n r d", r=8)
    with ExitStack() as ctx:
        s = lambda n: K.sem("fo_" + n)
        x_in, vec_in, mm, t_read, x_used, order = [s("x_in0"), s("x_in1")], s("vec_in"), s("mm"), s("t_read"), s("x_used"), s("order")
        var, std, row_ready, tr, tr_taken, gated = s("var"), s("std"), s("row"), s("tr"), s("tr_taken"), s("gated")
        block = ctx.enter_context(nc.Block())

        @block.sync
        def _(sp):
            for n, v in enumerate((io["b_out"][0], io["ln_g"][0], io["ln_b"][0], io["ln_emb_g_2"], io["ln_emb_b_2"])):
                sp.dma_start(vec[:, n, :], bcast_rows(v)).then_inc(vec_in, 16)
            for r in range(NT):
                if r >= 2:
                    sp.wait_ge(x_used, r - 1)
                sp.dma_start(xin[:, r % 2, :], x_class[:, r, :]).then_inc(x_in[r % 2], 16)

        @block.tensor
        def _(pe):
            def out_rows(r):
                if r >= 2:
                    pe.wait_ge(t_read, r - 1)
                for h in range(2):
                    for k in range(KT):
                        last = nc.tensor.matmul(PS[:, 2 * (r % 2) + h, :], merged[:, k, r:S:8], wout[:, k, h * 512:(h + 1) * 512],
                                                start=(k == 0), stop=(k == KT - 1))
                last.then_inc(mm, 1)

            def to_columns(r):
                pe.wait_ge(row_ready, r + 1)
                for g in range(2):
                    n = 2 * r + g
                    if n >= 4:
                        pe.wait_ge(tr_taken, n - 3)
                    for i in range(4):
                        k = 4 * g + i
                        last = nc.tensor.transpose(PS[:, 4 + n % 4, i * P:(i + 1) * P], x2r[:, r, k * P:(k + 1) * P], ident)
                    last.then_inc(tr, 1)

            for r in range(NT):
                out_rows(r)
                if r >= 1:
                    to_columns(r - 1)
            to_columns(NT - 1)

        @block.scalar
        def _(act):
            def take_columns(r):
                for g in range(2):
                    n = 2 * r + g
                    act.wait_ge(tr, n + 1)
                    nc.scalar.copy(x2T[:, 4 * g:4 * g + 4, r:S:8], PS[:, 4 + n % 4, :].rearrange("p (a b) -> p a b", b=P)).then_inc(tr_taken, 1)

            for r in range(NT):
                for n in range(2 * r, 2 * r + 2):
                    act.wait_ge(var, n + 1)
                    nc.scalar.activation(stat[:, 15:16], stat[:, 14:15], ACT.Sqrt).then_inc(std, 1)
                if r >= 1:
                    take_columns(r - 1)
            take_columns(NT - 1)

        @block.gpsimd
        def _(pool):
            for r in range(NT):
                pool.wait_ge(t_read, r + 1)
                nc.gpsimd.tensor_tensor(work[:, r % 2, :], work[:, r % 2, :], gate, ALU.mult).then_inc(gated, 1)

        @block.vector
        def _(dve):
            chain = Count(order)

            def link(ins, signal=chain):
                signal.by(ins)
                dve.wait_ge(signal.sem, signal.n)

            norm = RowNorm(nc, dve, link, stat, Count(var), std)
            rows, used, read = Count(row_ready), Count(x_used), Count(t_read)
            dve.wait_ge(vec_in, 80)
            for r in range(NT):
                dve.wait_ge(mm, r + 1)
                src = PS[:, 2 * (r % 2):2 * (r % 2) + 2, :].rearrange("p a b -> p (a b)")
                link(nc.vector.tensor_tensor(work[:, r % 2, :], src, vec[:, 0, :], ALU.add), read)
                dve.wait_ge(gated, r + 1)
                dve.wait_ge(x_in[r % 2], 16 * (r // 2 + 1))
                row = x2r[:, r, :]
                link(nc.vector.scalar_tensor_tensor(row, xin[:, r % 2, :], ALPHA, work[:, r % 2, :], ALU.mult, ALU.add), used)
                norm(row, vec[:, 1, :], vec[:, 2, :])
                norm(row, vec[:, 3, :], vec[:, 4, :], rows)


XS = VECS
QTAP = XS + 4096
S5S = QTAP + 4608
S5T = 28032
S5W, S5M, S5U, S5G, S5TMP = S5T + 4096, S5T + 8192, S5T + 12288, S5T + 16384, S5T + 20480
S5B = S5TMP + 2048
TC = 8
NCH = S // TC


def s5_states(K):
    nc, io, PS = K.nc, K.io, K.PS
    ident, cols2, x2T = K.at(IDENT, P), K.at(COLS2, 64), K.at(X2T, KT, S)
    xs = K.at(XS, 32, TC, 16)
    yg = K.at(S5T, TC, CH)
    QR, QN = K.at(QTAP, 16, 9, 16), K.at(QTAP + 2304, 16, 9, 16)
    Tc, Ts = K.at(S5T, 16, NCH), K.at(S5T + 2048, 16, NCH)
    W = K.at(S5W, 16, 2, P)
    M, U = K.at(S5M, 2, 16, P), K.at(S5U, 2, 16, P)
    WTr, WTi = K.at(S5M, 16, 8, 16), K.at(S5M + 2048, 16, 8, 16)
    wxs, Ksb = K.at(S5G, KT, CH), K.at(S5G, 2, 16, P)
    G = [K.at(S5G, 16, NCH), K.at(S5G + 2048, 16, NCH)]
    tmp = K.at(S5TMP, 4, 4, NCH)
    braw = K.at(S5TMP, 2, 16, 16)
    craw = K.at(S5W, 2, 4, P)
    kB, C = K.at(S5B, 2, 16, 16), K.at(S5B + 512, 2, 16, 16)
    pw, rev = K.at(S5B + 1024, 2, 9, 16), K.at(S5B + 1312, 2, 8, 16)
    o = S5S
    dskip = K.at(o, CH); o += CH
    ldt = K.at(o, 32); o += 32
    names = ("dt", "arg", "magarg", "kk", "sn", "cs", "mag", "rho", "den", "nr", "kre", "kim", "ta", "tb", "abre", "abim", "s8", "c8", "arg2", "argc")
    v = {}
    for n in names:
        v[n] = K.at(o, 16); o += 16
    args = K.at(o, 4, 16); o += 64
    trig = K.at(o, 4, 16); o += 64
    assert o <= X2T
    are, aim = cols2[:, 0:16], cols2[:, 16:32]
    over_c = lambda a: a.unsqueeze(2).to_broadcast([P, 16, 16])
    with ExitStack() as ctx:
        s = lambda n: K.sem("s5_" + n)
        wxs_in, dt_in, b_in, c_in, ds_in = s("wxs_in"), s("dt_in"), s("b_in"), s("c_in"), s("ds_in")
        order, aorder = s("order"), s("aorder")
        c_tr, c_ready, xs_mm, xs_ready, u_tr, u_ready = s("c_tr"), s("c_ready"), s("xs_mm"), s("xs_ready"), s("u_tr"), s("u_ready")
        dt_ready, arg_ready, trig_ready = s("dt"), s("arg"), s("trig")
        wt_ready, w_tr, w_ready, kb_ready, k_mm, k_ready, m_clear, toeplitz = s("wt"), s("w_tr"), s("w"), s("kb"), s("k_mm"), s("k"), s("m_clear"), s("toeplitz")
        v_mm, v_read, h_ready, y_mm, y_ready, gelu_done = s("v_mm"), s("v_read"), s("h"), s("y_mm"), s("y"), s("gelu")
        block = ctx.enter_context(nc.Block())

        @block.sync
        def _(sp):
            sp.dma_start(ldt, bcast_rows(io["log_dt_2"][0])).then_inc(dt_in, 16)
            for n, name in enumerate(("b_re_2", "b_im_2")):
                sp.dma_start(braw[:, n, :, :], io[name][0].rearrange("(j g) p c -> (g p) j c", g=2)).then_inc(b_in, 16)
            for n, name in enumerate(("c_re_2", "c_im_2")):
                rows = io[name][0].rearrange("(q g) c p -> (g c) q p", q=4)
                for dup in range(2):
                    sp.dma_start(craw[:, n, :, dup * 64:dup * 64 + 64], rows).then_inc(c_in, 16)
            sp.dma_start(wxs, io["w_in_2"][0, :, 0:CH].rearrange("(k p) n -> p k n", p=P)).then_inc(wxs_in, 16)
            sp.dma_start(dskip, bcast_rows(io["d_skip_2"][0])).then_inc(ds_in, 16)
            sp.wait_ge(k_ready, 8)
            sp.wait_ge(m_clear, 1)
            for t in range(TC):
                sp.dma_start(M[16 * t:16 * t + 16, :, :, 16 * t:P], Ksb[0:16, :, :, 0:P - 16 * t]).then_inc(toeplitz, 16)

        @block.gpsimd
        def _(pool):
            pool.wait_ge(w_tr, 8)
            nc.gpsimd.memset(K.at(S5M, 4096), 0.0).then_inc(m_clear, 1)

        @block.tensor
        def _(pe):
            pe.wait_ge(c_in, 64)
            for n in range(2):
                for q in range(4):
                    last = nc.tensor.transpose(PS[:, 6 + n, q * P:(q + 1) * P], craw[:, n, q, :], ident)
            last.then_inc(c_tr, 1)
            pe.wait_ge(wxs_in, 16)
            for t in range(TC):
                if t >= 6:
                    pe.wait_ge(xs_ready, t - 5)
                for k in range(KT):
                    last = nc.tensor.matmul(PS[:, t % 6, :], x2T[:, k, t:S:TC], wxs[:, k, :], start=(k == 0), stop=(k == KT - 1))
                last.then_inc(xs_mm, 1)
            pe.wait_ge(xs_ready, TC)
            pe.wait_ge(c_ready, 1)
            for n in range(8):
                q, g2 = n // 2, n % 2
                for i in range(4):
                    g = 2 * (4 * q + i) + g2
                    last = nc.tensor.transpose(PS[:, n, i * P:(i + 1) * P], xs[:, g, :, :], ident)
                last.then_inc(u_tr, 1)
            pe.wait_ge(wt_ready, 1)
            for n in range(8):
                pe.wait_ge(u_ready, n + 1)
                q, ri = n // 2, n % 2
                for i in range(4):
                    last = nc.tensor.transpose(PS[:, n, i * P:(i + 1) * P], (WTr, WTi)[ri][:, 4 * q + i, :, :], ident)
                last.then_inc(w_tr, 1)
            pe.wait_ge(kb_ready, 1)
            for n in range(8):
                pe.wait_ge(w_ready, n + 1)
                q, g2 = n // 2, n % 2
                half = slice(64 * g2, 64 * g2 + 64)
                for i in range(4):
                    j = 4 * q + i
                    nc.tensor.matmul(PS[0:16, n, i * P:(i + 1) * P], kB[half, 0, j, :], QR[half, j, 0:8, :], start=True, stop=False)
                    last = nc.tensor.matmul(PS[0:16, n, i * P:(i + 1) * P], kB[half, 1, j, :], QN[half, j, 0:8, :], start=False, stop=True)
                last.then_inc(k_mm, 1)
            for n in range(8):
                pe.wait_ge(k_ready, n + 1)
                q, ri = n // 2, n % 2
                for i in range(4):
                    j = 4 * q + i
                    for g2 in range(2):
                        half = slice(64 * g2, 64 * g2 + 64)
                        last = nc.tensor.matmul(PS[half, n, i * P:(i + 1) * P], W[:, j, ri, half], U[:, g2, j, :], start=True, stop=True)
                last.then_inc(v_mm, 1)
            pe.wait_ge(toeplitz, 16 * TC)
            for n in range(8):
                q, g2 = n // 2, n % 2
                pe.wait_ge(v_read, 4)
                pe.wait_ge(h_ready, q + 1)
                half = slice(64 * g2, 64 * g2 + 64)
                for i in range(4):
                    j = 4 * q + i
                    out = PS[:, n, i * P:(i + 1) * P]
                    nc.tensor.matmul(out, U[:, g2, j, :], M[:, g2, j, :], start=True, stop=False)
                    nc.tensor.matmul(out, G[0][half, j, :], QR[half, j, 1:9, :], start=False, stop=False)
                    last = nc.tensor.matmul(out, G[1][half, j, :], QN[half, j, 1:9, :], start=False, stop=True)
                last.then_inc(y_mm, 1)

        @block.scalar
        def _(act):
            act.wait_ge(dt_ready, 1)
            nc.scalar.activation(v["dt"], v["dt"], ACT.Exp).then_inc(aorder, 1)
            act.wait_ge(arg_ready, 1)
            nc.scalar.activation(v["mag"], v["magarg"], ACT.Exp)
            nc.scalar.activation(v["rho"], v["magarg"], ACT.Exp, scale=float(TC))
            nc.scalar.activation(trig, args, ACT.Sin).then_inc(trig_ready, 1)
            for t in range(TC):
                act.wait_ge(xs_mm, t + 1)
                nc.scalar.copy(xs[:, :, t, :], PS[:, t % 6, :].rearrange("p (g c) -> p g c", c=16)).then_inc(xs_ready, 1)
            act.wait_ge(c_tr, 1)
            for n in range(8):
                act.wait_ge(u_tr, n + 1)
                nc.scalar.copy(U[:, n % 2, 4 * (n // 2):4 * (n // 2) + 4, :], PS[:, n, :].rearrange("p (a b) -> p a b", b=P)).then_inc(u_ready, 1)
            for n in range(8):
                act.wait_ge(w_tr, n + 1)
                nc.scalar.copy(W[:, 4 * (n // 2):4 * (n // 2) + 4, n % 2, :], PS[:, n, :].rearrange("p (a b) -> p a b", b=P)).then_inc(w_ready, 1)
            for n in range(8):
                act.wait_ge(k_mm, n + 1)
                nc.scalar.copy(Ksb[0:16, n % 2, 4 * (n // 2):4 * (n // 2) + 4, :], PS[0:16, n, :].rearrange("p (a b) -> p a b", b=P)).then_inc(k_ready, 1)
            for q in range(4):
                act.wait_ge(y_ready, 2 * q + 2)
                nc.scalar.activation(yg[:, :, q * P:(q + 1) * P].rearrange("p t (g c) -> p g t c", c=16), xs[:, 8 * q:8 * q + 8, :, :],
                                     ACT.Gelu_apprx_tanh).then_inc(gelu_done, 1)

        @block.vector
        def _(dve):
            chain = Count(order)

            def link(ins, signal=chain):
                signal.by(ins)
                dve.wait_ge(signal.sem, signal.n)

            def tt(out, a, b, op, signal=chain):
                link(nc.vector.tensor_tensor(out, a, b, op), signal)

            dve.wait_ge(dt_in, 16)
            nc.vector.tensor_copy(v["dt"][0:64, :], ldt[0:64, 0:32:2])
            link(nc.vector.tensor_copy(v["dt"][64:128, :], ldt[64:128, 1:32:2]), Count(dt_ready))
            dve.wait_ge(aorder, 1)
            tt(v["magarg"], v["dt"], are, ALU.mult)
            tt(v["arg"], v["dt"], aim, ALU.mult)
            link(nc.vector.tensor_scalar(v["arg2"], v["arg"], float(TC), None, ALU.mult))
            for n, (src, quarter) in enumerate(((v["arg"], 0.0), (v["arg"], 0.25), (v["arg2"], 0.0), (v["arg2"], 0.25))):
                reduced_sine_argument(nc, link, args[:, n, :], src, v["kk"], quarter)
            link(nc.vector.memset(v["ta"], 0.0), Count(arg_ready))
            dve.wait_ge(trig_ready, 1)
            sn, cs = trig[:, 0, :], trig[:, 1, :]
            tt(v["abre"], v["mag"], cs, ALU.mult)
            tt(v["abim"], v["mag"], sn, ALU.mult)
            tt(v["den"], are, are, ALU.mult)
            tt(v["ta"], aim, aim, ALU.mult)
            tt(v["den"], v["den"], v["ta"], ALU.add)
            link(nc.vector.reciprocal(v["den"], v["den"]))
            link(nc.vector.tensor_scalar(v["nr"], v["abre"], 1.0, None, ALU.subtract))
            tt(v["ta"], v["nr"], are, ALU.mult)
            tt(v["tb"], v["abim"], aim, ALU.mult)
            tt(v["kre"], v["ta"], v["tb"], ALU.add)
            tt(v["kre"], v["kre"], v["den"], ALU.mult)
            tt(v["ta"], v["abim"], are, ALU.mult)
            tt(v["tb"], v["nr"], aim, ALU.mult)
            tt(v["kim"], v["ta"], v["tb"], ALU.subtract)
            tt(v["kim"], v["kim"], v["den"], ALU.mult)

            def complex_product(out_r, out_i, ar, ai, br, bi, t, negate_imaginary=False, signal=chain):
                tt(out_r, ar, br, ALU.mult)
                tt(t, ai, bi, ALU.mult)
                tt(out_r, out_r, t, ALU.subtract)
                tt(out_i, ar, bi, ALU.mult)
                tt(t, ai, br, ALU.mult)
                if negate_imaginary:
                    link(nc.vector.scalar_tensor_tensor(out_i, out_i, -1.0, t, ALU.mult, ALU.subtract), signal)
                else:
                    tt(out_i, out_i, t, ALU.add, signal)

            small = K.at(S5TMP + 512, 16, 16)
            dve.wait_ge(b_in, 32)
            complex_product(kB[:, 0, :, :], kB[:, 1, :, :], braw[:, 0, :, :], braw[:, 1, :, :], over_c(v["kre"]), over_c(v["kim"]), small)
            link(nc.vector.memset(pw[:, 0, 0, :], 1.0))
            link(nc.vector.memset(pw[:, 1, 0, :], 0.0))
            link(nc.vector.tensor_copy(pw[:, 0, 1, :], v["abre"]))
            link(nc.vector.tensor_copy(pw[:, 1, 1, :], v["abim"]))
            n = 1
            while n < TC:
                last_power = lambda ri: pw[:, ri, n:n + 1, :].to_broadcast([P, n, 16])
                complex_product(pw[:, 0, n + 1:2 * n + 1, :], pw[:, 1, n + 1:2 * n + 1, :], pw[:, 0, 1:n + 1, :], pw[:, 1, 1:n + 1, :],
                                last_power(0), last_power(1), small[:, 0:n, :])
                n *= 2
            for ri in range(2):
                for t in range(TC):
                    chain.by(nc.vector.tensor_copy(rev[:, ri, t, :], pw[:, ri, TC - 1 - t, :]))
            dve.wait_ge(order, chain.n)
            by_jsc = lambda a: a.rearrange("p m j -> p j m").unsqueeze(3).to_broadcast([P, 16, 8, 16])
            over_s = lambda a: a.unsqueeze(2).to_broadcast([P, 16, 8, 16])
            whole = K.at(S5TMP, 16, 8, 16)
            complex_product(WTr, WTi, over_s(kB[:, 0, :, :]), over_s(kB[:, 1, :, :]), by_jsc(rev[:, 0, :, :]), by_jsc(rev[:, 1, :, :]), whole,
                            signal=Count(wt_ready))
            dve.wait_ge(c_tr, 1)
            for ri in range(2):
                src = PS[:, 6 + ri, :].rearrange("p (j g c) -> p j g c", g=2, c=16)
                chain.by(nc.vector.tensor_copy(C[0:64, ri, :, :], src[0:64, :, 0, :]))
                last = nc.vector.tensor_copy(C[64:128, ri, :, :], src[64:128, :, 1, :])
                if ri == 1:
                    link(last, Count(c_ready))
            for j0 in (0, 8):
                js = slice(j0, j0 + 8)
                over_m = lambda a: a.unsqueeze(2).to_broadcast([P, 8, 9, 16])
                by_jmc = lambda a: a.rearrange("p m j -> p j m")[:, js, :].unsqueeze(3).to_broadcast([P, 8, 9, 16])
                complex_product(QR[:, js, :, :], QN[:, js, :, :], over_m(C[:, 0, js, :]), over_m(C[:, 1, js, :]),
                                by_jmc(pw[:, 0, :, :]), by_jmc(pw[:, 1, :, :]), K.at(S5TMP, 8, 9, 16), negate_imaginary=True,
                                signal=chain if j0 == 0 else Count(kb_ready))
            link(nc.vector.tensor_copy(Ts[:, :, 0], trig[:, 2, :]))
            link(nc.vector.tensor_copy(Tc[:, :, 0], trig[:, 3, :]))
            n = 1
            while n < NCH:
                last_power = lambda a: a[:, :, n - 1:n].to_broadcast([P, 16, n])
                complex_product(Tc[:, :, n:2 * n], Ts[:, :, n:2 * n], Tc[:, :, 0:n], Ts[:, :, 0:n], last_power(Tc), last_power(Ts),
                                K.at(S5TMP, 16, n))
                n *= 2
            dve.wait_ge(u_tr, 8)
            dve.wait_ge(ds_in, 16)
            link(nc.vector.tensor_tensor(xs, xs, dskip.rearrange("p (g c) -> p g c", c=16).unsqueeze(2).to_broadcast([P, 32, TC, 16]), ALU.mult))
            dve.wait_ge(toeplitz, 16 * TC)
            for q in range(4):
                js = slice(4 * q, 4 * q + 4)
                dve.wait_ge(v_mm, 2 * q + 2)
                vr, vi = (PS[:, 2 * q + ri, :].rearrange("p (a b) -> p a b", b=NCH) for ri in range(2))
                c, sn_ = Tc[:, js, :], Ts[:, js, :]
                for n, (a, b) in enumerate(((vr, c), (vi, sn_), (vi, c), (vr, sn_))):
                    ins = nc.vector.tensor_tensor(tmp[:, n, :, :], a, b, ALU.mult)
                    if n < 3:
                        chain.by(ins)
                    else:
                        ins.then_inc(v_read, 1)
                dve.wait_ge(v_read, q + 1)
                tt(tmp[:, 0, :, :], tmp[:, 0, :, :], tmp[:, 1, :, :], ALU.add)
                tt(tmp[:, 2, :, :], tmp[:, 2, :, :], tmp[:, 3, :, :], ALU.subtract)
                for ri in range(2):
                    for i in range(4):
                        j = 4 * q + i
                        chain.by(nc.vector.tensor_tensor_scan(G[ri][:, j, :], v["rho"][:, j:j + 1].to_broadcast([P, NCH]), tmp[:, 2 * ri, i, :], 0.0,
                                                              ALU.mult, ALU.add))
                dve.wait_ge(order, chain.n)
                gr, gi = G[0][:, js, 0:NCH - 1], G[1][:, js, 0:NCH - 1]
                c, sn_ = Tc[:, js, 0:NCH - 1], Ts[:, js, 0:NCH - 1]
                for n, (a, b) in enumerate(((gr, c), (gi, sn_), (gi, c), (gr, sn_))):
                    chain.by(nc.vector.tensor_tensor(tmp[:, n, :, 0:NCH - 1], a, b, ALU.mult))
                dve.wait_ge(order, chain.n)
                chain.by(nc.vector.tensor_tensor(G[0][:, js, 1:NCH], tmp[:, 0, :, 0:NCH - 1], tmp[:, 1, :, 0:NCH - 1], ALU.subtract))
                chain.by(nc.vector.tensor_tensor(G[1][:, js, 1:NCH], tmp[:, 2, :, 0:NCH - 1], tmp[:, 3, :, 0:NCH - 1], ALU.add))
                chain.by(nc.vector.memset(G[0][:, js, 0:1], 0.0))
                nc.vector.memset(G[1][:, js, 0:1], 0.0).then_inc(h_ready, 1)
                dve.wait_ge(h_ready, q + 1)
            for n in range(8):
                q, g2 = n // 2, n % 2
                dve.wait_ge(y_mm, n + 1)
                for i in range(4):
                    g = 2 * (4 * q + i) + g2
                    dst = xs[:, g, :, :]
                    src = PS[:, n, i * P:(i + 1) * P].rearrange("p (t c) -> p t c", c=16)
                    last = nc.vector.tensor_tensor(dst, dst, src, ALU.add)
                last.then_inc(y_ready, 1)


CQT, CKVT, KRT, YMT = VECS, VECS + 2048, VECS + 3072, VECS + 4096
ROPE = VECS + 8192
YG, YGT, YST, GMT, SECW = 28032, 32128, 36224, 40320, 44416
RMS_EPS = 1e-6


def project_second(K):
    nc, io, PS = K.nc, K.io, K.PS
    ident, cols2, x2T = K.at(IDENT, P), K.at(COLS2, 64), K.at(X2T, KT, S)
    cqT, ckvT, krT = K.at(CQT, 2, S), K.at(CKVT, S), K.at(KRT, S)
    lat = K.at(YMT, NT, 448)
    cos, sin = K.at(ROPE, NT, 32), K.at(ROPE + 256, NT, 32)
    kr2 = K.at(ROPE + 512, NT, P)
    o = ROPE + 1536
    ss, rinv, posr, posf, pcol = K.at(o, NT, 2), K.at(o + 16, NT, 2), K.at(o + 32, P), K.at(o + 160, P), K.at(o + 288, NT)
    invf = K.at(o + 296, 32)
    assert o + 328 <= X2T
    yg, ygT, ysT, gmT = K.at(YG, TC, CH), K.at(YGT, 4, S), K.at(YST, 4, S), K.at(GMT, 4, S)
    sg = K.at(YG, 2, 512)
    ang, kk, squares = K.at(YG + 1024, NT, 32), K.at(YG + 1280, NT, 32), K.at(YG + 2560, 4, 384)
    red, t1, t2 = K.at(YG + 1792, NT, 32), K.at(YG + 2048, NT, 32), K.at(YG + 2304, NT, 32)
    wlat, wt, wglu = K.at(SECW, KT, 448), K.at(SECW + 3584, 2, KT, P), K.at(SECW + 3584 + 2048, 4, CH)
    w = io["w_in_2"][0].rearrange("(k p) n -> p k n", p=P)
    col_of = lambda T: CH + T * P if T < 4 else 2 * CH + 448 + (T - 4) * P
    with ExitStack() as ctx:
        s = lambda n: K.sem("p2_" + n)
        lat_in, glu_in, w_in, small_in, order = s("lat_in"), s("glu_in"), [s("w_in0"), s("w_in1")], s("small_in"), s("order")
        y_tr, y_taken, lat_mm, lat_ready, proj_mm, proj_ready, pos_ready, pos_tr = (s(n) for n in ("y_tr", "y_taken", "lat_mm", "lat", "proj_mm", "proj", "posf", "pos_tr"))
        glu_mm, glu_sig, ys_ready, pos_taken, arg_ready, trig_ready, ms_ready, rms_ready = (s(n) for n in ("glu_mm", "glu_sig", "ys", "pos_taken", "arg", "trig", "ms", "rms"))
        rows_ready, l_tr, l_taken, sig_used = s("rows"), s("l_tr"), s("l_taken"), s("sig_used")
        block = ctx.enter_context(nc.Block())

        @block.sync
        def _(sp):
            sp.dma_start(posr[0:NT, :].bitcast(i32), io["positions_2"].rearrange("o (i p) -> (o i) p", p=P)).then_inc(small_in, 16)
            sp.dma_start(invf, bcast_rows(io["inv_freq"])).then_inc(small_in, 16)
            sp.dma_start(wlat, w[:, :, 2 * CH:2 * CH + 448]).then_inc(lat_in, 16)
            for T in range(8):
                if T >= 2:
                    sp.wait_ge(proj_mm, 2 * (T - 1))
                sp.dma_start(wt[:, T % 2, :, :], w[:, :, col_of(T):col_of(T) + P]).then_inc(w_in[T % 2], 16)
                if T == 1:
                    sp.dma_start(wglu, io["w_glu_2"][0].rearrange("(k p) n -> p k n", p=P)).then_inc(glu_in, 16)

        @block.tensor
        def _(pe):
            for n in range(8):
                c, h = n // 2, n % 2
                for i in range(4):
                    last = nc.tensor.transpose(PS[:, n, i * P:(i + 1) * P], yg[:, 4 * h + i, c * P:(c + 1) * P], ident)
                last.then_inc(y_tr, 1)
            pe.wait_ge(pos_ready, 1)
            pe.wait_ge(y_taken, 8)
            nc.tensor.transpose(PS[:, 7, 0:NT], posf[0:NT, :], ident[0:NT, 0:NT]).then_inc(pos_tr, 1)
            pe.wait_ge(lat_in, 16)
            for i in range(NT):
                if i >= 4:
                    pe.wait_ge(lat_ready, i - 3)
                for k in range(KT):
                    last = nc.tensor.matmul(PS[:, i % 4, 0:448], x2T[:, k, i * P:(i + 1) * P], wlat[:, k, :], start=(k == 0), stop=(k == KT - 1))
                last.then_inc(lat_mm, 1)

            def project(n):
                T, h = n // 2, n % 2
                pe.wait_ge(w_in[T % 2], 16 * (T // 2 + 1))
                if n >= 2:
                    pe.wait_ge(proj_ready, n - 1)
                for k in range(KT):
                    last = nc.tensor.matmul(PS[:, 4 + h, :], wt[:, T % 2, k, :], x2T[:, k, h * 512:(h + 1) * 512], start=(k == 0), stop=(k == KT - 1))
                last.then_inc(proj_mm, 1)

            for n in range(8):
                project(n)
            pe.wait_ge(glu_in, 16)
            pe.wait_ge(pos_taken, 1)
            for n in range(8):
                c, h = n // 2, n % 2
                if n >= 2:
                    pe.wait_ge(glu_sig, n - 1)
                for k in range(4):
                    last = nc.tensor.matmul(PS[:, 6 + h, :], wglu[:, k, c * P:(c + 1) * P], ygT[:, k, h * 512:(h + 1) * 512], start=(k == 0), stop=(k == 3))
                last.then_inc(glu_mm, 1)
                project(8 + n)
            pe.wait_ge(rows_ready, 1)
            pe.wait_ge(lat_ready, NT)
            for n in range(8):
                c, h = n // 2, n % 2
                if n >= 4:
                    pe.wait_ge(l_taken, n - 3)
                for i in range(4):
                    src = lat[:, 4 * h + i, c * P:(c + 1) * P] if c < 3 else kr2[:, 4 * h + i, :]
                    last = nc.tensor.transpose(PS[:, n % 4, i * P:(i + 1) * P], src, ident)
                last.then_inc(l_tr, 1)

        @block.scalar
        def _(act):
            for n in range(8):
                c, h = n // 2, n % 2
                act.wait_ge(y_tr, n + 1)
                dst = ygT[:, c, :].rearrange("p (n t) -> p t n", t=TC)[:, 4 * h:4 * h + 4, :]
                nc.scalar.copy(dst, PS[:, n, :].rearrange("p (a b) -> p a b", b=P)).then_inc(y_taken, 1)
            for i in range(NT):
                act.wait_ge(lat_mm, i + 1)
                if i >= 4:
                    act.wait_ge(lat_ready, i - 3)
                nc.scalar.activation(squares[:, i % 4, 0:256], PS[:, i % 4, 0:256], ACT.Square, accum_out=ss[:, i, 0:1])
                nc.scalar.activation(squares[:, i % 4, 256:384], PS[:, i % 4, 256:384], ACT.Square, accum_out=ss[:, i, 1:2])
                nc.scalar.copy(lat[:, i, :], PS[:, i % 4, 0:448]).then_inc(lat_ready, 1)

            def take_projection(n):
                T, h = n // 2, n % 2
                act.wait_ge(proj_mm, n + 1)
                dst = (ysT if T < 4 else gmT)[:, T % 4, h * 512:(h + 1) * 512]
                nc.scalar.activation(dst, PS[:, 4 + h, :], ACT.Silu).then_inc(proj_ready, 1)

            for n in range(8):
                take_projection(n)
            act.wait_ge(arg_ready, 1)
            nc.scalar.activation(sin, red, ACT.Sin).then_inc(trig_ready, 1)
            act.wait_ge(arg_ready, 2)
            nc.scalar.activation(cos, red, ACT.Sin).then_inc(trig_ready, 1)
            act.wait_ge(ms_ready, 1)
            nc.scalar.activation(rinv, rinv, ACT.Sqrt).then_inc(rms_ready, 1)
            for n in range(8):
                c, h = n // 2, n % 2
                act.wait_ge(glu_mm, n + 1)
                if n >= 2:
                    act.wait_ge(ys_ready, n - 1)
                nc.scalar.activation(sg[:, n % 2, :], PS[:, 6 + h, :], ACT.Sigmoid, bias=cols2[:, 32 + c:33 + c]).then_inc(glu_sig, 1)
                take_projection(8 + n)
            for n in range(8):
                c, h = n // 2, n % 2
                act.wait_ge(l_tr, n + 1)
                dst = (cqT[:, c, :] if c < 2 else ckvT if c == 2 else krT)[:, h * 512:(h + 1) * 512]
                scale = cols2[:, 36 + c:37 + c] if c < 3 else 1.0
                nc.scalar.activation(dst, PS[:, n % 4, :], ACT.Copy, scale=scale).then_inc(l_taken, 1)

        @block.vector
        def _(dve):
            chain = Count(order)

            def link(ins, signal=chain):
                signal.by(ins)
                dve.wait_ge(signal.sem, signal.n)

            def tt(out, a, b, op, signal=chain):
                link(nc.vector.tensor_tensor(out, a, b, op), signal)

            args = Count(arg_ready)
            dve.wait_ge(small_in, 32)
            link(nc.vector.tensor_copy(posf[0:NT, :], posr[0:NT, :].bitcast(i32)), Count(pos_ready))
            dve.wait_ge(pos_tr, 1)
            link(nc.vector.tensor_copy(pcol, PS[:, 7, 0:NT]), Count(pos_taken))
            dve.wait_ge(y_tr, 8)
            tt(ang, pcol.unsqueeze(2).to_broadcast([P, NT, 32]), invf.unsqueeze(1).to_broadcast([P, NT, 32]), ALU.mult)
            reduced_sine_argument(nc, link, red, ang, kk)
            link(nc.vector.memset(t1[:, 0, 0:1], 0.0), args)
            dve.wait_ge(trig_ready, 1)
            reduced_sine_argument(nc, link, red, ang, kk, 0.25)
            link(nc.vector.memset(t1[:, 0, 0:1], 0.0), args)
            dve.wait_ge(trig_ready, 2)
            dve.wait_ge(lat_ready, NT)
            for n, width in enumerate((256, 128)):
                link(nc.vector.tensor_scalar(rinv[:, :, n], ss[:, :, n], 1 / width, RMS_EPS, ALU.mult, ALU.add), chain if n == 0 else Count(ms_ready))
            k1, k2 = lat[:, :, 384:416], lat[:, :, 416:448]
            for out, a, b, op in ((0, cos, sin, ALU.subtract), (32, sin, cos, ALU.add)):
                tt(t1, k1, a, ALU.mult)
                tt(t2, k2, b, ALU.mult)
                tt(kr2[:, :, out:out + 32], t1, t2, op)
            link(nc.vector.tensor_copy(kr2[:, :, 64:128], kr2[:, :, 0:64]))
            dve.wait_ge(rms_ready, 1)
            link(nc.vector.reciprocal(rinv, rinv))
            for n, (a, b) in enumerate(((0, 256), (256, 384))):
                tt(lat[:, :, a:b], lat[:, :, a:b], rinv[:, :, n:n + 1].to_broadcast([P, NT, b - a]), ALU.mult,
                   chain if n == 0 else Count(rows_ready))
            for n in range(8):
                c, h = n // 2, n % 2
                dve.wait_ge(proj_ready, n + 1)
                d, y = ysT[:, c, h * 512:(h + 1) * 512], ygT[:, c, h * 512:(h + 1) * 512]
                tt(d, d, y, ALU.mult)
                dve.wait_ge(glu_sig, n + 1)
                nc.vector.tensor_tensor(d, d, sg[:, n % 2, :], ALU.mult).then_inc(ys_ready, 1)


MLA_HEADS, ROPE_D = 4, 64
QK_SCALE = 192 ** -0.5


def latent_attention(K):
    nc, io, PS = K.nc, K.io, K.PS
    ident = K.at(IDENT, P)
    cqT, ckvT, krT, ymT, gmT = K.at(CQT, 2, S), K.at(CKVT, S), K.at(KRT, S), K.at(YMT, 4, S), K.at(GMT, 4, S)
    cos, sin = K.at(ROPE, NT, 32), K.at(ROPE + 256, NT, 32)
    knT, qnT = K.at(X2T, 4, S), K.at(X2T + 4096, 4, S)
    vr = K.at(YG, NT, CH)
    wuq, wukv = K.at(YG + 4096, 2, 4, 192), K.at(YG + 4096 + 1536, 4, 256)
    causal = K.at(YG + 4096 + 2560, S)
    qrT = K.at(SECW, 2, S)
    sb, pt = K.at(SECW + 2048, 2, S), K.at(SECW + 4096, 2, S)
    orow = K.at(SECW + 6144, NT, P)
    rope_rows = K.at(SECW + 2048, NT, 4, 64)
    t1, t2 = K.at(SECW + 4096, 4, 32), K.at(SECW + 4096 + P, 4, 32)
    o = SECW + 7168
    mx, nm, l, rl = K.at(o, 32), K.at(o + 32, 32), K.at(o + 64, 32), K.at(o + 96, 32)
    units = [(h, i) for h in range(MLA_HEADS) for i in range(NT)]
    t_jobs, first_job, out_job = [], {}, {}
    for step in range(len(units) + 2):
        if 1 <= step <= len(units):
            h, i = units[step - 1]
            first_job[step - 1] = len(t_jobs)
            t_jobs += [("p", step - 1, b0, min(b0 + 4, i + 1)) for b0 in range(0, i + 1, 4)]
        if step >= 2 and units[step - 2][1] == NT - 1:
            h = units[step - 2][0]
            out_job[h] = len(t_jobs)
            t_jobs += [("o", h, 0, 4), ("o", h, 4, 8)]
    after_unit = lambda u: first_job[u] + (units[u][1] + 4) // 4
    with ExitStack() as ctx:
        s = lambda n: K.sem("ml_" + n)
        w_in, causal_in, order = s("w_in"), s("causal_in"), s("order")
        up_mm, up_ready, r_mm, r_ready, rt, rt_ready = s("up_mm"), s("up"), s("r_mm"), s("r"), s("rt"), s("rt_ready")
        s_done, s_taken, nm_ready, exp_done, t_done, t_taken, pv_done, o_ready, rl_ready = (s(n) for n in ("s", "s_taken", "nm", "exp", "t", "t_taken", "pv", "o", "rl"))
        block = ctx.enter_context(nc.Block())

        @block.sync
        def _(sp):
            sp.dma_start(wuq, io["w_uq_2"][0].rearrange("(k p) (h n) -> p k h n", p=P, h=4)).then_inc(w_in, 16)
            sp.dma_start(wukv, io["w_ukv_2"][0].rearrange("p (h n) -> p h n", h=4)).then_inc(w_in, 16)
            sp.dma_start(causal, io["causal"]).then_inc(causal_in, 16)

        @block.tensor
        def _(pe):
            pe.wait_ge(w_in, 32)
            for i in range(NT):
                if i >= 4:
                    pe.wait_ge(r_ready, i - 3)
                for c in range(2):
                    last = nc.tensor.matmul(PS[:, 4 + i % 4, 0:256], cqT[:, c, i * P:(i + 1) * P], wuq[:, c, :, 128:192], start=(c == 0), stop=(c == 1))
                last.then_inc(r_mm, 1)
            for n in range(24):
                kind, a, h = n // 8, (n % 8) // 2, n % 2
                if n >= 4:
                    pe.wait_ge(up_ready, n - 3)
                out = PS[:, n % 4, :]
                if kind == 0:
                    for c in range(2):
                        last = nc.tensor.matmul(out, wuq[:, c, a, 0:128], cqT[:, c, h * 512:(h + 1) * 512], start=(c == 0), stop=(c == 1))
                elif kind == 1:
                    last = nc.tensor.matmul(out, wukv[:, a, 0:128], ckvT[:, h * 512:(h + 1) * 512], start=True, stop=True)
                else:
                    last = nc.tensor.matmul(out, ckvT[:, (n % 8) * P:(n % 8 + 1) * P], wukv[:, :, 128:256], start=True, stop=True)
                last.then_inc(up_mm, 1)
            pe.wait_ge(r_ready, NT)
            for n in range(4):
                pair, h = n // 2, n % 2
                for i in range(4):
                    last = nc.tensor.transpose(PS[:, 4 + n, i * P:(i + 1) * P], rope_rows[:, 4 * h + i, 2 * pair:2 * pair + 2, :], ident)
                last.then_inc(rt, 1)
            pe.wait_ge(up_ready, 24)
            pe.wait_ge(rt_ready, 4)

            def scores(u):
                h, i = units[u]
                if u >= 2:
                    pe.wait_ge(s_taken, u - 1)
                half = slice(64 * (h % 2), 64 * (h % 2) + 64)
                n = (i + 1) * P
                for c in range(0, n, 512):
                    e = min(n, c + 512)
                    out = PS[:, 2 * (u % 2) + c // 512, 0:e - c]
                    nc.tensor.matmul(out, qnT[:, h, i * P:(i + 1) * P], knT[:, h, c:e], start=True, stop=False)
                    last = nc.tensor.matmul(out, qrT[half, h // 2, i * P:(i + 1) * P], krT[half, c:e], start=False, stop=True)
                last.then_inc(s_done, 1)

            def transposes(g):
                kind, which, b0, b1 = t_jobs[g]
                if g >= 2:
                    pe.wait_ge(t_taken, g - 1)
                for b in range(b0, b1):
                    src = sb[:, which % 2, b * P:(b + 1) * P] if kind == "p" else orow[:, b, :]
                    last = nc.tensor.transpose(PS[:, 4 + g % 2, (b - b0) * P:(b - b0 + 1) * P], src, ident)
                last.then_inc(t_done, 1)

            for step in range(len(units) + 2):
                if step < len(units):
                    scores(step)
                if 1 <= step <= len(units):
                    u = step - 1
                    pe.wait_ge(exp_done, u + 1)
                    for g in range(first_job[u], after_unit(u)):
                        transposes(g)
                if step >= 2:
                    u = step - 2
                    h, i = units[u]
                    pe.wait_ge(t_taken, after_unit(u))
                    if u >= 2:
                        pe.wait_ge(o_ready, u - 1)
                    for b in range(i + 1):
                        last = nc.tensor.matmul(PS[:, 6 + u % 2, 0:P], pt[:, u % 2, b * P:(b + 1) * P], vr[:, b, h * P:(h + 1) * P],
                                                start=(b == 0), stop=(b == i))
                    last.then_inc(pv_done, 1)
                    if i == NT - 1:
                        pe.wait_ge(o_ready, u + 1)
                        for g in range(out_job[h], out_job[h] + 2):
                            transposes(g)

        @block.scalar
        def _(act):
            for n in range(24):
                kind, a, h = n // 8, (n % 8) // 2, n % 2
                act.wait_ge(up_mm, n + 1)
                dst = vr[:, n % 8, :] if kind == 2 else (qnT, knT)[kind][:, a, h * 512:(h + 1) * 512]
                nc.scalar.copy(dst, PS[:, n % 4, :]).then_inc(up_ready, 1)
            for step in range(len(units) + 2):
                if step < len(units):
                    h, i = units[step]
                    n = (i + 1) * P
                    act.wait_ge(nm_ready, step + 1)
                    nc.scalar.activation(sb[:, step % 2, 0:n], sb[:, step % 2, 0:n], ACT.Exp, bias=nm[:, step:step + 1], scale=QK_SCALE,
                                         accum_out=l[:, step:step + 1]).then_inc(exp_done, 1)
                if step >= 2:
                    u = step - 2
                    h, i = units[u]
                    act.wait_ge(pv_done, u + 1)
                    act.wait_ge(rl_ready, u + 1)
                    if h >= 1:
                        act.wait_ge(t_done, out_job[h - 1] + 2)
                    nc.scalar.activation(orow[:, i, :], PS[:, 6 + u % 2, 0:P], ACT.Copy, scale=rl[:, u:u + 1]).then_inc(o_ready, 1)

        @block.vector
        def _(dve):
            chain = Count(order)

            def link(ins, signal=chain):
                signal.by(ins)
                dve.wait_ge(signal.sem, signal.n)

            for i in range(NT):
                dve.wait_ge(r_mm, i + 1)
                x = PS[:, 4 + i % 4, 0:256].rearrange("p (h e) -> p h e", h=4)
                c, sn = (a[:, i, :].unsqueeze(1).to_broadcast([P, 4, 32]) for a in (cos, sin))
                for out, a, b, op in ((0, c, sn, ALU.subtract), (32, sn, c, ALU.add)):
                    link(nc.vector.tensor_tensor(t1, x[:, :, 0:32], a, ALU.mult))
                    link(nc.vector.tensor_tensor(t2, x[:, :, 32:64], b, ALU.mult))
                    ins = nc.vector.tensor_tensor(rope_rows[:, i, :, out:out + 32], t1, t2, op)
                    if out:
                        ins.then_inc(r_ready, 1)
                        dve.wait_ge(r_ready, i + 1)
                    else:
                        link(ins)
            for n in range(4):
                dve.wait_ge(rt, n + 1)
                nc.vector.tensor_copy(qrT[:, n // 2, (n % 2) * 512:(n % 2 + 1) * 512], PS[:, 4 + n, :]).then_inc(rt_ready, 1)
            dve.wait_ge(causal_in, 16)

            def take(g, dst, gate=None):
                dve.wait_ge(t_done, g + 1)
                src = PS[:, 4 + g % 2, 0:dst.shape[1]]
                if gate is None:
                    nc.vector.tensor_copy(dst, src).then_inc(t_taken, 1)
                else:
                    nc.vector.tensor_tensor(dst, src, gate, ALU.mult).then_inc(t_taken, 1)

            for step in range(len(units) + 2):
                if step < len(units):
                    h, i = units[step]
                    n = (i + 1) * P
                    dve.wait_ge(s_done, step + 1)
                    if step >= 2:
                        dve.wait_ge(t_done, after_unit(step - 2))
                    src = PS[:, 2 * (step % 2):2 * (step % 2) + 2, :].rearrange("p a b -> p (a b)")[:, 0:n]
                    nc.vector.tensor_tensor_reduce(out=sb[:, step % 2, 0:n], in0=src, in1=causal[:, S - n:S], scale=1.0, scalar=-3e38,
                                                   op0=ALU.add, op1=ALU.max, accum_out=mx[:, step:step + 1]).then_inc(s_taken, 1)
                    dve.wait_ge(s_taken, step + 1)
                    nc.vector.tensor_scalar(nm[:, step:step + 1], mx[:, step:step + 1], -QK_SCALE, None, ALU.mult).then_inc(nm_ready, 1)
                if 1 <= step <= len(units):
                    u = step - 1
                    if u >= 2:
                        dve.wait_ge(pv_done, u - 1)
                    for g in range(first_job[u], after_unit(u)):
                        _, _, b0, b1 = t_jobs[g]
                        take(g, pt[:, u % 2, b0 * P:b1 * P])
                    dve.wait_ge(exp_done, u + 1)
                    nc.vector.reciprocal(rl[:, u:u + 1], l[:, u:u + 1]).then_inc(rl_ready, 1)
                if step >= 2 and units[step - 2][1] == NT - 1:
                    h = units[step - 2][0]
                    for n, g in enumerate(range(out_job[h], out_job[h] + 2)):
                        take(g, ymT[:, h, n * 512:(n + 1) * 512], gmT[:, h, n * 512:(n + 1) * 512])


def second_output(K):
    nc, io, PS = K.nc, K.io, K.PS
    ident = K.at(IDENT, P)
    ysT, ymT, x2r = K.at(YST, 4, S), K.at(YMT, 4, S), K.at(X2R, NT, D)
    wout, wpg, wpp = K.at(GMT, KT, D), K.at(YG, KT, D), K.at(X2T, 2, D)
    prow, pT = K.at(X2T + 2048, NT, 256), K.at(X2T + 4096, 2, NT, P)
    uT = K.at(X2T + 6144, 2, KT, P)
    vec = K.at(VECS, 2, D)
    sg = K.at(VECS + 2048, 2, D)
    stat = K.at(ROPE, 16)
    out_class = io["out"][0].rearrange("(n r) d -> n r d", r=8)
    with ExitStack() as ctx:
        s = lambda n: K.sem("so_" + n)
        wout_in, wpg_in, wpp_in, p_in, vec_in, order = s("wout_in"), s("wpg_in"), s("wpp_in"), s("p_in"), s("vec_in"), s("order")
        p_tr, p_taken, mix, u_ready, ut, ut_taken, pg, pp, sig, pp_used, var, std, row_ready = (s(n) for n in (
            "p_tr", "p_taken", "mix", "u", "ut", "ut_taken", "pg", "pp", "sig", "pp_used", "var", "std", "row"))
        block = ctx.enter_context(nc.Block())

        @block.sync
        def _(sp):
            sp.dma_start(prow, io["p_2"][0, 0].rearrange("(n r) e -> n r e", r=8)).then_inc(p_in, 16)
            sp.dma_start(wout, io["w_out_2"][0].rearrange("(k p) n -> p k n", p=P)).then_inc(wout_in, 16)
            sp.dma_start(wpp, io["w_pp_2"][0].rearrange("(k p) n -> p k n", p=P)).then_inc(wpp_in, 16)
            sp.dma_start(wpg, io["w_pg_2"][0].rearrange("(k p) n -> p k n", p=P)).then_inc(wpg_in, 16)
            for n, name in enumerate(("ln_g_2", "ln_b_2")):
                sp.dma_start(vec[:, n, :], bcast_rows(io[name][0])).then_inc(vec_in, 16)
            for r in range(NT):
                sp.wait_ge(row_ready, r + 1)
                sp.dma_start(out_class[:, r, :], x2r[:, r, :]).then_inc(K.out_done, 16)
            sp.wait_ge(K.out_done, 16 * NT)

        @block.tensor
        def _(pe):
            pe.wait_ge(p_in, 16)
            for n in range(4):
                k, h = n // 2, n % 2
                for i in range(4):
                    last = nc.tensor.transpose(PS[:, 4 + n, i * P:(i + 1) * P], prow[:, 4 * h + i, k * P:(k + 1) * P], ident)
                last.then_inc(p_tr, 1)

            def mixed(r):
                if r >= 1:
                    pe.wait_ge(u_ready, r)
                for h in range(2):
                    for k in range(KT):
                        src = (ysT if k < 4 else ymT)[:, k % 4, r:S:8]
                        last = nc.tensor.matmul(PS[:, h, :], src, wout[:, k, h * 512:(h + 1) * 512], start=(k == 0), stop=(k == KT - 1))
                last.then_inc(mix, 1)

            pe.wait_ge(wout_in, 16)
            mixed(0)
            pe.wait_ge(wpp_in, 16)
            pe.wait_ge(p_taken, 4)
            for r in range(NT):
                if r >= 1:
                    pe.wait_ge(pp_used, r)
                for h in range(2):
                    for k in range(2):
                        last = nc.tensor.matmul(PS[:, 6 + h, :], pT[:, k, r, :], wpp[:, k, h * 512:(h + 1) * 512], start=(k == 0), stop=(k == 1))
                last.then_inc(pp, 1)
                if r + 1 < NT:
                    mixed(r + 1)
                pe.wait_ge(u_ready, r + 1)
                for g in range(2):
                    if r >= 1:
                        pe.wait_ge(ut_taken, 2 * r - 1 + g)
                    for i in range(4):
                        k = 4 * g + i
                        last = nc.tensor.transpose(PS[:, 2 + g, i * P:(i + 1) * P], x2r[:, r, k * P:(k + 1) * P], ident)
                    last.then_inc(ut, 1)
                pe.wait_ge(wpg_in, 16)
                pe.wait_ge(ut_taken, 2 * r + 2)
                if r >= 1:
                    pe.wait_ge(sig, r)
                for h in range(2):
                    for k in range(KT):
                        last = nc.tensor.matmul(PS[:, 4 + h, :], uT[:, r % 2, k, :], wpg[:, k, h * 512:(h + 1) * 512], start=(k == 0), stop=(k == KT - 1))
                last.then_inc(pg, 1)

        @block.scalar
        def _(act):
            for n in range(4):
                act.wait_ge(p_tr, n + 1)
                nc.scalar.copy(pT[:, n // 2, 4 * (n % 2):4 * (n % 2) + 4, :], PS[:, 4 + n, :].rearrange("p (a b) -> p a b", b=P)).then_inc(p_taken, 1)
            for r in range(NT + 1):
                if r < NT:
                    for g in range(2):
                        act.wait_ge(ut, 2 * r + g + 1)
                        nc.scalar.copy(uT[:, r % 2, 4 * g:4 * g + 4, :], PS[:, 2 + g, :].rearrange("p (a b) -> p a b", b=P)).then_inc(ut_taken, 1)
                if r < NT:
                    act.wait_ge(pg, r + 1)
                    if r >= 2:
                        act.wait_ge(pp_used, r - 1)
                    nc.scalar.activation(sg[:, r % 2, :], PS[:, 4:6, :].rearrange("p a b -> p (a b)"), ACT.Sigmoid).then_inc(sig, 1)
                    act.wait_ge(var, r + 1)
                    nc.scalar.activation(stat[:, 15:16], stat[:, 14:15], ACT.Sqrt).then_inc(std, 1)

        @block.vector
        def _(dve):
            chain = Count(order)

            def link(ins, signal=chain):
                signal.by(ins)
                dve.wait_ge(signal.sem, signal.n)

            norm = RowNorm(nc, dve, link, stat, Count(var), std)
            u, used, rows = Count(u_ready), Count(pp_used), Count(row_ready)

            def residual(r):
                dve.wait_ge(mix, r + 1)
                link(nc.vector.scalar_tensor_tensor(x2r[:, r, :], x2r[:, r, :], ALPHA, PS[:, 0:2, :].rearrange("p a b -> p (a b)"), ALU.mult, ALU.add), u)

            dve.wait_ge(vec_in, 32)
            residual(0)
            for r in range(NT):
                if r + 1 < NT:
                    residual(r + 1)
                dve.wait_ge(sig, r + 1)
                dve.wait_ge(pp, r + 1)
                link(nc.vector.tensor_tensor(sg[:, r % 2, :], PS[:, 6:8, :].rearrange("p a b -> p (a b)"), sg[:, r % 2, :], ALU.mult), used)
                link(nc.vector.tensor_tensor(x2r[:, r, :], x2r[:, r, :], sg[:, r % 2, :], ALU.add))
                norm(x2r[:, r, :], vec[:, 0, :], vec[:, 1, :], rows)


def hybrid_kernel(nc, io):
    K = Kernel(nc, io)
    with K.ctx:
        steps = [lambda: prepare(K),
                 lambda: hyena(K),
                 lambda: dilated_attention(K),
                 lambda: merge_branches(K),
                 lambda: first_output(K),
                 lambda: s5_states(K),
                 lambda: project_second(K),
                 lambda: latent_attention(K),
                 lambda: second_output(K)]
        for step in steps:
            step()
            K.end_phase()


INPUTS = ["x", "c", "w_ada", "b_ada", "w_in", "b_in", "conv_w", "conv_b", "filt_w1", "filt_b1", "filt_w2", "filt_b2",
          "filt_w3", "filt_b3", "filt_w4", "filt_freq", "filt_bias", "w_proj_attn", "w_proj_hyena", "w_out", "b_out",
          "ln_g", "ln_b", "p_2", "positions_2", "ln_emb_g_2", "ln_emb_b_2", "w_in_2", "a_re_2", "a_im_2", "log_dt_2",
          "b_re_2", "b_im_2", "c_re_2", "c_im_2", "d_skip_2", "w_glu_2", "b_glu_2", "q_norm_g_2", "w_uq_2",
          "kv_norm_g_2", "w_ukv_2", "w_out_2", "w_pg_2", "w_pp_2", "ln_g_2", "ln_b_2"]


def kernel(**inputs):
    import concourse.bacc as bacc
    from concourse.bass_utils import run_bass_kernel_spmd as run

    nc = bacc.Bacc("TRN2", target_bir_lowering=False, num_devices=1)
    arrays, io = {}, {}
    for name, value in [(n, inputs[n]) for n in INPUTS] + list(shape_constants().items()):
        a = np.ascontiguousarray(value)
        arrays[f"in_{name}"] = a
        io[name] = nc.dram_tensor(f"in_{name}", a.shape, mybir.dt.from_np(a.dtype), kind="ExternalInput").ap()
    io["out"] = nc.dram_tensor("out_x", (1, S, D), fp32, kind="ExternalOutput").ap()
    hybrid_kernel(nc, io)
    r = run(nc, [arrays], core_ids=[0])
    return r.results[0]["out_x"]
```

```python
import math
from contextlib import ExitStack

import numpy as np

import concourse.bass as bass
from concourse import mybir

fp32 = mybir.dt.float32
fp32r = mybir.dt.float32r
i32 = mybir.dt.int32
ALU = mybir.AluOpType
ACT = mybir.ActivationFunctionType
AX = mybir.AxisListType

P = 128
ARENA = 52400
S = 1024
D = 1024
KT = D // P
NT = S // P
HD = 64
CH = 512
N_QKV = 4608
COL_GATTN = N_QKV
COL_HY = COL_GATTN + CH
COL_R = COL_HY + 4 * CH
ALPHA = 2 ** 0.25
TWO_PI = 2 * math.pi
ROUND = 1.5 * 2 ** 23
R2 = math.sqrt(0.5)
FAR = 1e32

PI_A = float(np.float32(6.28125))
PI_B = float(np.float32(np.round((TWO_PI - PI_A) * 2 ** 22) / 2 ** 22))
PI_C = float(np.float32(TWO_PI - PI_A - PI_B))
PI_CLIP = float(np.nextafter(np.float32(math.pi), np.float32(0)))


def leaf_tables():
    fwd, inv = {}, {}
    t = np.arange(256)[None, :]
    for name, phase in (("P", math.pi / 4), ("M", 5 * math.pi / 4)):
        k = np.arange(256)[:, None]
        a = (phase + 2 * math.pi * k) / 256 * t
        c, s = np.cos(a), np.sin(a)
        fwd[name] = np.block([[c.T, s.T], [-s.T, c.T]])
        inv[name] = np.block([[c, -s], [s, c]]) / 256 / 4
    for name, n, k, roots, scale in (("B", 512, 256, math.pi * (2 * np.arange(256) + 1) / 512, 2 / 512 / 4),
                                     ("N", 256, 128, math.pi * (2 * np.arange(128) + 1) / 256, 2 / 256 / 8),
                                     ("C", 256, 256, 2 * math.pi * np.arange(256) / 256, 1 / 256 / 8)):
        a = roots[:, None] * np.arange(n)[None, :]
        c, s = np.cos(a), np.sin(a)
        fwd[name] = np.hstack([c.T, s.T])
        inv[name] = np.vstack([c, s]) * scale
    order = "PMBNC"
    return {f"fwd_{n}": fwd[n].astype(np.float32) for n in order} | {f"inv_{n}": inv[n].astype(np.float32) for n in order}


def shape_constants():
    f32 = np.float32
    out = {"ident": np.eye(P, dtype=f32)}
    L = S
    pos = np.concatenate([np.arange(L), (L - np.arange(L)) % L])
    t = np.linspace(0.0, 1.0, L, dtype=f32)[:, None]
    bands = 16
    w = (2.0 * math.pi * np.arange(L, dtype=f32)[:, None] / L).astype(f32)
    f = np.linspace(1e-4, bands - 1, bands, dtype=f32)[None, :]
    feat = np.concatenate([t, np.cos(f * w), -np.sin(f * w)], axis=-1).astype(f32)
    out["posT"] = np.ascontiguousarray(feat[pos].T)
    deltas = np.linspace(math.log(1e-2) / 1.5, math.log(1e-2) / 0.3, CH, dtype=f32)
    decay = np.exp(-t * np.abs(deltas)[None, :]).astype(f32)[pos]
    decay[L] = 0.0
    out["decay"] = decay
    out.update(leaf_tables())
    q, key = np.arange(P)[:, None], np.arange(256)[None, :]
    tables = []
    for shift in (0, 64, 128):
        rel = np.abs(key - shift - q)
        tables.append(np.where(rel <= 64, rel, FAR))
    for a in range(2):
        rel = np.abs(key - (2 * q + a))
        same = np.abs(key[:, :P] - q)
        tables += [np.where(rel <= 64, 4 * rel, FAR), np.where(same % 2 == 0, 8 * same, FAR)]
    out["dist"] = np.concatenate(tables, axis=1).astype(f32)
    out["causal"] = np.concatenate([np.zeros((P, 7 * P)), np.where(np.arange(P)[None, :] <= q, 0.0, -1e30)], axis=1).astype(f32)
    out["inv_freq"] = (np.float32(1.0) / np.power(np.float32(10000.0), np.arange(0, 64, 2, dtype=f32) / np.float32(64))).astype(f32)
    return out


class Count:

    def __init__(self, sem):
        self.sem, self.n = sem, 0

    def by(self, ins):
        self.n += 1
        return ins.then_inc(self.sem, 1)


class Kernel:
    def __init__(self, nc, io):
        self.nc, self.io = nc, io
        self.ctx = ExitStack()
        self.A = self.ctx.enter_context(nc.sbuf_tensor("arena", [P, ARENA], fp32))
        self.base = nc.sbuf_base - ARENA * 4
        self.PS = self.ctx.enter_context(nc.psum_tensor("banks", [P, 8, 512], fp32))
        self.phase_sems = []
        self.out_done = self.ctx.enter_context(nc.semaphore("out_done"))

    def at(self, off, *dims):
        assert off + int(np.prod(dims)) <= ARENA, (off, dims)
        return self.shaped(self.A[:, off:off + int(np.prod(dims))], dims)

    def part(self, name, off, *dims):
        n = int(np.prod(dims))
        assert off + n <= ARENA, (off, n)
        t = self.nc.alloc_sbuf_tensor_at(name, [P, n], fp32r, offset=self.base + 4 * off)
        return self.shaped(t[:, :], dims)

    @staticmethod
    def shaped(v, dims):
        if len(dims) == 2:
            v = v.rearrange("p (a b) -> p a b", a=dims[0])
        if len(dims) == 3:
            v = v.rearrange("p (a b c) -> p a b c", a=dims[0], b=dims[1])
        if len(dims) == 4:
            v = v.rearrange("p (a b c d) -> p a b c d", a=dims[0], b=dims[1], c=dims[2])
        return v

    def sem(self, name):
        self.phase_sems.append(self.nc.alloc_semaphore(name))
        return self.phase_sems[-1]

    def end_phase(self):
        self.nc.clear_and_free_semaphores(self.phase_sems)
        self.nc.all_engine_barrier()
        self.phase_sems = []


def split_product(nc, out, lhs, rhs, start, stop):
    (lh, ll), (rh, rl) = lhs, rhs
    nc.tensor.matmul(out, ll, rh, start=start, stop=False)
    nc.tensor.matmul(out, lh, rl, start=False, stop=False)
    return nc.tensor.matmul(out, lh, rh, start=False, stop=stop)


def bcast_rows(ap1d, n=P):
    return ap1d.partition_broadcast(n)


IDENT = 0
COLS1 = 128
COLS2 = COLS1 + 128
MODT = COLS2 + 64
GATE = MODT + 16
MLPC = GATE + 1024
HT = 1408
assert MLPC + 8 <= HT
H3 = HT + 8192
FREE1 = H3 + 2048
N_COLS1 = 120


def reduced_sine_argument(nc, link, out, x, k, quarter=0.0):
    link(nc.vector.tensor_scalar(k, x, 1 / TWO_PI, ROUND + quarter if not quarter else quarter, ALU.mult, ALU.add))
    if quarter:
        link(nc.vector.tensor_scalar(k, k, ROUND, None, ALU.add))
    link(nc.vector.tensor_scalar(k, k, ROUND, None, ALU.subtract))
    link(nc.vector.scalar_tensor_tensor(out, k, -PI_A, x, ALU.mult, ALU.add))
    link(nc.vector.scalar_tensor_tensor(out, k, -PI_B, out, ALU.mult, ALU.add))
    link(nc.vector.scalar_tensor_tensor(out, k, -PI_C, out, ALU.mult, ALU.add))
    if quarter:
        link(nc.vector.tensor_scalar(out, out, quarter * TWO_PI, PI_CLIP, ALU.add, ALU.min))
        link(nc.vector.tensor_scalar(out, out, -PI_CLIP, None, ALU.max))
    else:
        link(nc.vector.tensor_scalar(out, out, PI_CLIP, -PI_CLIP, ALU.min, ALU.max))


def prepare(K):
    nc, io = K.nc, K.io
    o = FREE1
    xr = K.at(o, NT, D); o += NT * D
    wada = K.at(o, 2, KT, 512); o += 2 * KT * 512
    bada = K.at(o, 3 * D); o += 3 * D
    mod = K.at(o, 6, 512); o += 3 * D
    cbc = K.at(o, KT, P); o += KT * P
    stats = K.at(o, NT, 12); o += NT * 12
    mv = K.at(o, NT, 2); o += NT * 2
    std = K.at(o, NT); o += NT
    rows = K.at(o, 2, P); o += 2 * P
    one = K.at(o, 1); o += 1
    ident, hT, modT, gate = K.at(IDENT, P), K.at(HT, KT, S), K.at(MODT, 16), K.at(GATE, D)
    cols1, cols2 = K.at(COLS1, N_COLS1), K.at(COLS2, 64)
    PS = K.PS
    with ExitStack() as ctx:
        s = lambda n: K.sem("prep_" + n)
        x_in, c_in, row_in = [s(f"x_in{i}") for i in range(4)], s("c_in"), s("row_in")
        wada_in = [s("wada_in0"), s("wada_in1")]
        order, cbc_ready, mod_done, mod_ready, col_done, modT_ready = s("order"), s("cbc"), s("mod_done"), s("mod_ready"), s("col_done"), s("modT")
        var_ready, std_ready, norm_ready, tr_done, hT_ready = s("var"), s("std"), s("norm"), s("tr"), s("hT")
        rows_tr, rows_ready = s("rows_tr"), s("rows_ready")
        zero_ready = s("zero")
        block = ctx.enter_context(nc.Block())

        @block.sync
        def _(sp):
            sp.dma_start(ident, io["ident"]).then_inc(row_in, 16)
            sp.wait_ge(zero_ready, 1)
            sp.dma_start(rows[0:72, 0, :], io["b_in"].rearrange("o (n p) -> (o n) p", p=P)).then_inc(row_in, 16)
            sp.dma_start(rows[72:108, 0, :], io["conv_w"].rearrange("o t (n p) -> (o t n) p", p=P)).then_inc(row_in, 16)
            sp.dma_start(rows[108:120, 0, :], io["conv_b"].rearrange("o (n p) -> (o n) p", p=P)).then_inc(row_in, 16)
            sp.dma_start(rows[0:16, 1, :], io["a_re_2"].rearrange("o (j g) p -> (o j) (g p)", g=2)).then_inc(row_in, 16)
            sp.dma_start(rows[16:32, 1, :], io["a_im_2"].rearrange("o (j g) p -> (o j) (g p)", g=2)).then_inc(row_in, 16)
            sp.dma_start(rows[32:36, 1, :], io["b_glu_2"].rearrange("o (n p) -> (o n) p", p=P)).then_inc(row_in, 16)
            sp.dma_start(rows[36:38, 1, :], io["q_norm_g_2"].rearrange("o (n p) -> (o n) p", p=P)).then_inc(row_in, 16)
            sp.dma_start(rows[38:39, 1, :], io["kv_norm_g_2"]).then_inc(row_in, 16)
            sp.dma_start(rows[39:47, 1, :], io["c"].rearrange("o (k p) -> (o k) p", p=P)).then_inc(row_in, 16)
            for i in range(4):
                sp.dma_start(xr[:, 2 * i:2 * i + 2, :], io["x"][0, 2 * i * P:(2 * i + 2) * P, :].rearrange("(a p) n -> p a n", p=P)).then_inc(x_in[i], 16)
            sp.dma_start(bada, bcast_rows(io["b_ada"][0])).then_inc(c_in, 16)

        @block.gpsimd
        def _(pool):
            nc.gpsimd.memset(rows[:, :, :], 0.0).then_inc(zero_ready, 1)
            w = io["w_ada"][0].rearrange("(k p) n -> p k n", p=P)
            for c in range(6):
                if c >= 2:
                    pool.wait_ge(mod_done, c - 1)
                pool.dma_start(wada[:, c % 2, :, :], w[:, :, c * 512:(c + 1) * 512]).then_inc(wada_in[c % 2], 16)

        @block.scalar
        def _(act):
            act.wait_ge(var_ready, 1)
            nc.scalar.activation(std, mv[:, :, 1], ACT.Sqrt).then_inc(std_ready, 1)
            act.wait_ge(modT_ready, 1)
            for n in range(16):
                k, h = n // 2, n % 2
                act.wait_ge(tr_done, n + 1)
                nc.scalar.activation(hT[:, k, h * 512:(h + 1) * 512], PS[:, n % 4, :], ACT.Identity,
                                     bias=modT[:, k:k + 1], scale=modT[:, 8 + k:9 + k]).then_inc(hT_ready, 1)

        @block.vector
        def _(dve):
            chain = Count(order)

            def link(ins, signal=chain):
                signal.by(ins)
                dve.wait_ge(signal.sem, signal.n)

            nc.vector.memset(one, 1.0)
            dve.wait_ge(rows_tr, 1)
            nc.vector.tensor_copy(cols1, PS[:, 7, 0:N_COLS1])
            nc.vector.tensor_copy(cols2, PS[:, 7, 128:192]).then_inc(rows_ready, 1)
            dve.wait_ge(rows_ready, 1)
            nc.vector.tensor_copy(cbc, cols2[:, 39:39 + KT].unsqueeze(2).to_broadcast([P, KT, P])).then_inc(cbc_ready, 1)
            for i in range(NT):
                dve.wait_ge(x_in[i // 2], 16)
                nc.vector.bn_stats(stats[:, i, 0:6], xr[:, i, 0:512])
                link(nc.vector.bn_stats(stats[:, i, 6:12], xr[:, i, 512:1024]))
            for i in range(NT):
                link(nc.vector.bn_aggr(mv[:, i, :], stats[:, i, :]))
            link(nc.vector.tensor_scalar(mv[:, :, 1], mv[:, :, 1], 1e-5, None, ALU.add), Count(var_ready))
            dve.wait_ge(std_ready, 1)
            link(nc.vector.reciprocal(std, std))
            for i in range(NT):
                nc.vector.tensor_scalar(xr[:, i, :], xr[:, i, :], mv[:, i, 0:1], std[:, i:i + 1],
                                        ALU.subtract, ALU.mult).then_inc(norm_ready, 1)
            dve.wait_ge(c_in, 16)
            for c in range(6):
                dve.wait_ge(mod_done, c + 1)
                nc.vector.tensor_tensor(mod[:, c, :], PS[:, 4 + c % 2, :], bada[:, c * 512:(c + 1) * 512],
                                        ALU.add).then_inc(mod_ready, 1)
            dve.wait_ge(mod_ready, 6)
            nc.vector.tensor_copy(gate, mod[:, 4:6, :].rearrange("p a b -> p (a b)"))
            dve.wait_ge(col_done, 1)
            link(nc.vector.tensor_copy(modT, PS[:, 6, 0:16]))
            nc.vector.tensor_scalar(modT[:, 8:16], modT[:, 8:16], 1.0, None, ALU.add).then_inc(modT_ready, 1)

        @block.tensor
        def _(pe):
            pe.wait_ge(row_in, 16 * 10)
            nc.tensor.transpose(PS[:, 7, 0:128], rows[:, 0, :], ident)
            nc.tensor.transpose(PS[:, 7, 128:256], rows[:, 1, :], ident).then_inc(rows_tr, 1)
            pe.wait_ge(cbc_ready, 1)
            for c in range(6):
                pe.wait_ge(wada_in[c % 2], 16 * (c // 2 + 1))
                if c >= 2:
                    pe.wait_ge(mod_ready, c - 1)
                for k in range(KT):
                    last = nc.tensor.matmul(PS[:, 4 + c % 2, :], cbc[:, k, :], wada[:, c % 2, k, :],
                                            start=(k == 0), stop=(k == KT - 1))
                last.then_inc(mod_done, 1)
            pe.wait_ge(mod_ready, 4)
            for k in range(16):
                last = nc.tensor.matmul(PS[:, 6, k:k + 1], mod[0:1, k // 4, (k % 4) * P:(k % 4 + 1) * P],
                                        one[0:1, 0:1], start=True, stop=True)
            last.then_inc(col_done, 1)
            pe.wait_ge(norm_ready, NT)
            for n in range(16):
                k, h = n // 2, n % 2
                if n >= 4:
                    pe.wait_ge(hT_ready, n - 3)
                for i in range(4):
                    last = nc.tensor.transpose(PS[:, n % 4, i * P:(i + 1) * P], xr[:, 4 * h + i, k * P:(k + 1) * P], ident)
                last.then_inc(tr_done, 1)


ZV, X1T = FREE1, FREE1 + 4096
LF = X1T + 4096
HS = LF + 8192
FWORK = HS + 18 * 512
GHY = FWORK + 10240


class FilterNetwork:

    def __init__(self, K):
        self.K, nc, io = K, K.nc, K.io
        s = lambda n: K.sem("fn_" + n)
        self.small_in, self.mm, self.taken, self.arg, self.sin = s("small_in"), s("mm"), s("taken"), s("arg"), s("sin")
        self.posT, self.hA, self.kk, self.wf = K.at(LF, 2048), K.at(LF + 2048, 2048), K.at(LF + 4096, 2048), K.at(LF + 6144, 3, HD)
        self.mlpc, self.h3 = K.at(MLPC, 8), K.at(H3, 2048)

    def load(self, pool):
        io, put = self.K.io, self.small_in
        for n, name in enumerate(("filt_b1", "filt_b2", "filt_b3", "filt_freq")):
            pool.dma_start(self.mlpc[0:HD, n:n + 1], io[name].rearrange("o (p a) -> p (o a)", a=1)).then_inc(put, 16)
        pool.dma_start(self.posT[0:33, :], io["posT"]).then_inc(put, 16)
        pool.dma_start(self.wf[0:33, 0, :], io["filt_w1"][0]).then_inc(put, 16)
        pool.dma_start(self.wf[0:HD, 1, :], io["filt_w2"][0]).then_inc(put, 16)
        pool.dma_start(self.wf[0:HD, 2, :], io["filt_w3"][0]).then_inc(put, 16)

    def pe(self, pe, layer):
        nc, PS = self.K.nc, self.K.PS
        if layer == 0:
            pe.wait_ge(self.small_in, 16 * 8)
        else:
            pe.wait_ge(self.sin, layer)
        rows = 33 if layer == 0 else HD
        src = self.posT if layer == 0 else self.hA
        for n in range(4):
            job = 4 * layer + n
            if job >= 2:
                pe.wait_ge(self.taken, job - 1)
            nc.tensor.matmul(PS[0:HD, 4 + job % 2, :], self.wf[0:rows, layer, :], src[0:rows, n * 512:(n + 1) * 512],
                             start=True, stop=True).then_inc(self.mm, 1)

    def dve(self, dve, link, layer):
        nc, PS = self.K.nc, self.K.PS
        taken = Count(self.taken)
        taken.n = 4 * layer
        dve.wait_ge(self.small_in, 16 * 8)
        for n in range(4):
            job = 4 * layer + n
            dve.wait_ge(self.mm, job + 1)
            link(nc.vector.tensor_scalar(self.kk[0:HD, n * 512:(n + 1) * 512], PS[0:HD, 4 + job % 2, :],
                                         self.mlpc[0:HD, layer:layer + 1], self.mlpc[0:HD, 3:4], ALU.add, ALU.mult), taken)
        reduced_sine_argument(nc, link, self.hA[0:HD, :], self.kk[0:HD, :], self.posT[0:HD, :])
        nc.vector.memset(self.posT[0:1, 0:1], 0.0).then_inc(self.arg, 1)

    def act(self, act, layer):
        act.wait_ge(self.arg, layer + 1)
        dst = self.h3 if layer == 2 else self.hA
        self.K.nc.scalar.activation(dst[0:HD, :], self.hA[0:HD, :], ACT.Sin).then_inc(self.sin, 1)


class HyenaProjections:

    def __init__(self, K, name, first, x2=None, ghy=None):
        self.K, self.x2, self.ghy = K, x2, ghy
        self.tiles = list(range(first, first + 8))
        self.wt, self.pb, self.ub = K.at(HS, 4, KT, P), K.at(HS + 4096, 2, S + 2), K.at(HS + 4096 + 2 * (S + 2), 2, S)
        self.hT, self.cols1, self.ident = K.at(HT, KT, S), K.at(COLS1, N_COLS1), K.at(IDENT, P)
        self.rows_of = [K.at(ZV, 8, CH), K.at(X1T, 8, CH)]
        s = lambda n: K.sem(name + n)
        self.w_in = [s(f"w_in{b}") for b in range(4)]
        self.proj_done, self.p_ready, self.conv_done, self.tr_done, self.z_ready, self.border_ready = (
            s(n) for n in ("proj", "p_ready", "conv", "tr", "z", "border"))

    def load(self, sp, conv):
        w = self.K.io["w_in"][0].rearrange("(k p) n -> p k n", p=P)
        for n, t in enumerate(self.tiles):
            if n >= 4:
                sp.wait_ge(self.proj_done, n - 3)
            c0 = COL_HY + t * P
            sp.dma_start(self.wt[:, n % 4, :, :], w[:, :, c0:c0 + P]).then_inc(self.w_in[n % 4], 16)
            if n >= 3:
                for t in {3: range(0, 4), 4: range(4, 6), 5: range(6, 10), 6: range(10, 16)}.get(n, ()):
                    conv.load_decay(sp, t)

    def project(self, pe, n):
        nc, PS = self.K.nc, self.K.PS
        pe.wait_ge(self.w_in[n % 4], 16 * (n // 4 + 1))
        if n >= 2:
            pe.wait_ge(self.p_ready, n - 1)
        for h in range(2):
            for k in range(KT):
                last = nc.tensor.matmul(PS[:, 2 * (n % 2) + h, :], self.wt[:, n % 4, k, :], self.hT[:, k, h * 512:(h + 1) * 512],
                                        start=(k == 0), stop=(k == KT - 1))
        last.then_inc(self.proj_done, 1)

    def to_rows(self, pe, n):
        nc, PS = self.K.nc, self.K.PS
        if self.tiles[n] >= 8:
            return
        pe.wait_ge(self.conv_done, n + 1)
        if n >= 1:
            pe.wait_ge(self.z_ready, n)
        for i in range(NT):
            last = nc.tensor.transpose(PS[:, 6 + i // 4, (i % 4) * P:(i % 4 + 1) * P], self.ub[:, n % 2, i * P:(i + 1) * P], self.ident)
        last.then_inc(self.tr_done, 1)

    def take_projection(self, act, n):
        nc, PS, t = self.K.nc, self.K.PS, self.tiles[n]
        act.wait_ge(self.proj_done, n + 1)
        if n >= 2 and t < 12:
            act.wait_ge(self.conv_done, n - 1)
        bias = self.cols1[:, COL_HY // P + t:COL_HY // P + t + 1]
        for h in range(2):
            src = PS[:, 2 * (n % 2) + h, :]
            if t < 12:
                last = nc.scalar.activation(self.pb[:, n % 2, 1 + h * 512:1 + (h + 1) * 512], src, ACT.Identity, bias=bias)
            else:
                last = nc.scalar.activation(self.ghy[:, t - 12, h * 512:(h + 1) * 512], src, ACT.Silu, bias=bias)
        last.then_inc(self.p_ready, 1)

    def take_rows(self, act, n):
        nc, PS = self.K.nc, self.K.PS
        if self.tiles[n] >= 8:
            return
        act.wait_ge(self.tr_done, n + 1)
        dst = self.rows_of[self.tiles[n] // 4][:, :, (self.tiles[n] % 4) * P:(self.tiles[n] % 4 + 1) * P]
        for h in range(2):
            last = nc.scalar.copy(dst[:, 4 * h:4 * h + 4, :], PS[:, 6 + h, :].rearrange("p (i c) -> p i c", c=P))
        last.then_inc(self.z_ready, 1)

    def border(self, dve):
        nc = self.K.nc
        nc.vector.memset(self.pb[:, :, 0:1], 0.0)
        nc.vector.memset(self.pb[:, :, S + 1:S + 2], 0.0).then_inc(self.border_ready, 1)

    def convolve(self, dve, link, n):
        nc, t, pb = self.K.nc, self.tiles[n], self.pb
        if t >= 12:
            return
        dve.wait_ge(self.p_ready, n + 1)
        if n >= 2 and t < 8:
            dve.wait_ge(self.tr_done, n - 1)
        u = self.ub[:, n % 2, :] if t < 8 else self.x2[:, t - 8, :]
        tap = lambda j: self.cols1[:, 72 + 12 * j + t:73 + 12 * j + t]
        link(nc.vector.tensor_scalar(u, pb[:, n % 2, 1:S + 1], tap(1), self.cols1[:, 108 + t:109 + t], ALU.mult, ALU.add))
        link(nc.vector.scalar_tensor_tensor(u, pb[:, n % 2, 0:S], tap(0), u, ALU.mult, ALU.add))
        nc.vector.scalar_tensor_tensor(u, pb[:, n % 2, 2:S + 2], tap(2), u, ALU.mult, ALU.add).then_inc(self.conv_done, 1)


LEAVES = {"P": (4, 0, 2), "M": (4, 4, 2), "B": (4, 8, 2), "N": (2, 12, 1), "C": (2, 14, 2)}
NAMES = "PMBNC"


def leaf_inputs(name, neg, cyc):
    return {"P": [neg[0], neg[1], neg[4], neg[5]], "M": [neg[2], neg[3], neg[6], neg[7]],
            "B": cyc[0:4], "N": cyc[4:6], "C": cyc[6:8]}[name]


def spectrum_pair(H, name, q):
    kt, first, pairs = LEAVES[name]
    return H[:, first + q, :], H[:, first + pairs + q, :]


class LongConvolution:

    def __init__(self, K, order_no):
        self.K, self.order_no, io = K, order_no, K.io
        o = FWORK
        self.w4, self.dec, self.bias_row = K.at(o, 2, CH), K.at(o + 1024, 4, CH), K.at(o + 3072, CH)
        self.cyc2 = K.at(o, 8, CH)
        self.mat, self.tmp = K.at(o + 4096, 2, 2048), K.at(o + 8192, 4, CH)
        self.z, self.x1t, self.h3 = K.at(ZV, 8, CH), K.at(X1T, 8, CH), K.at(H3, 2048)
        self.neg, self.cyc, self.H = K.at(LF, 8, CH), K.at(LF + 4096, 8, CH), K.at(HS, 18, CH)
        self.rec = {"P": K.at(LF, 4, CH), "M": K.at(LF + 2048, 4, CH), "A": K.at(LF + 4096, 4, CH), "B": K.at(LF + 6144, 4, CH)}
        r = self.rec
        self.rec_of = {"P": r["P"], "M": r["M"], "B": r["B"], "N": r["A"][:, 0:2, :], "C": r["A"][:, 2:4, :]}
        s = lambda n: K.sem(f"lc{order_no}_" + n)
        self.w_in, self.dec_in, self.mat_in = s("w_in"), [s(f"dec_in{b}") for b in range(4)], [s("mat_in0"), s("mat_in1")]
        self.f_mm, self.f_ready, self.lf_ready, self.hs_mm, self.hs_ready, self.zl_ready, self.zs_mm, self.zs_ready, self.iv_mm, self.iv_ready = (
            s(n) for n in ("f_mm", "f_ready", "lf", "hs_mm", "hs", "zl", "zs_mm", "zs", "iv_mm", "iv"))
        self.matrices = [("fwd_" + n) for n in NAMES] * 2 + [("inv_" + n) for n in NAMES]
        self.jobs = 16 if order_no == 0 else 20

    def matrix(self, n):
        rows, cols = self.K.io[self.matrices[n]].shape
        return self.mat[:, n % 2, 0:rows // P * cols].rearrange("p (k c) -> p k c", c=cols)

    def used_after(self, stage, name):
        kt, first, pairs = LEAVES[name]
        if stage < 2:
            return first + 2 * pairs
        upto = NAMES[:NAMES.index(name) + 1]
        return 4 * len(upto) if self.order_no else sum(self.K.io["inv_" + m].shape[1] // P for m in upto)

    def load_filter(self, sp):
        io = self.K.io
        for d in range(2):
            c0 = self.order_no * 1024 + d * CH
            sp.dma_start(self.w4[0:HD, d, :], io["filt_w4"][0, :, c0:c0 + CH]).then_inc(self.w_in, 16)
        sp.dma_start(self.bias_row[0:1, :], io["filt_bias"][0, self.order_no:self.order_no + 1, :]).then_inc(self.w_in, 16)

    def load_decay(self, queue, t):
        if t >= 4:
            queue.wait_ge(self.f_ready, t - 3)
        queue.dma_start(self.dec[:, t % 4, :], self.K.io["decay"][t * P:(t + 1) * P, :]).then_inc(self.dec_in[t % 4], 16)

    def load_matrices(self, pool):
        for n, name in enumerate(self.matrices):
            if n >= 2:
                pool.wait_ge((self.hs_mm, self.zs_mm, self.iv_mm)[(n - 2) // 5], self.used_after((n - 2) // 5, NAMES[(n - 2) % 5]))
            pool.dma_start(self.matrix(n), self.K.io[name].rearrange("(k p) c -> p k c", p=P)).then_inc(self.mat_in[n % 2], 16)

    def filter_rows(self, pe, t0, t1):
        if t0 == 0:
            pe.wait_ge(self.w_in, 48)
        for t in range(t0, t1):
            if t >= 2:
                pe.wait_ge(self.f_ready, t - 1)
            self.K.nc.tensor.matmul(self.K.PS[:, 4 + t % 2, :], self.h3[0:HD, t * P:(t + 1) * P], self.w4[0:HD, t // 8, :],
                                    start=True, stop=True).then_inc(self.f_mm, 1)

    def forward(self, pe, n, name, neg_in, cyc_in, mm_sem, bank_free):
        kt, first, pairs = LEAVES[name]
        ins, m = leaf_inputs(name, [neg_in[:, i, :] for i in range(8)], [cyc_in[:, i, :] for i in range(8)]), self.matrix(n)
        pe.wait_ge(self.mat_in[n % 2], 16 * (n // 2 + 1))
        f = m.shape[2] // 2
        for q in range(pairs):
            for part in range(2):
                t = first + 2 * q + part
                bank_free(t)
                for k in range(kt):
                    last = self.K.nc.tensor.matmul(self.K.PS[:, t % 8, :], m[:, k, part * f + q * P:part * f + (q + 1) * P], ins[k],
                                                   start=(k == 0), stop=(k == kt - 1))
                last.then_inc(mm_sem, 1)

    def spectra(self, pe):
        def bank_free_h(t):
            if t >= 8:
                pe.wait_ge(self.hs_ready, t - 7)

        def bank_free_z(t):
            if t < 8:
                pe.wait_ge(self.hs_ready, 18)
            elif t % 2 == 0:
                pe.wait_ge(self.zs_ready, t // 2 - 3)

        pe.wait_ge(self.lf_ready, 1)
        for n, name in enumerate(NAMES):
            self.forward(pe, n, name, self.neg, self.cyc, self.hs_mm, bank_free_h)
        pe.wait_ge(self.zl_ready, 1)
        for n, name in enumerate(NAMES):
            self.forward(pe, 5 + n, name, self.z, self.cyc2, self.zs_mm, bank_free_z)

    def inverse(self, pe):
        nc, PS, H, job = self.K.nc, self.K.PS, self.H, 0
        for n, name in enumerate(NAMES):
            kt, first, pairs = LEAVES[name]
            m = self.matrix(10 + n)
            freq = 2 * pairs
            out_tiles = m.shape[2] // P
            pe.wait_ge(self.mat_in[(10 + n) % 2], 16 * ((10 + n) // 2 + 1))
            pe.wait_ge(self.zs_ready, 9)
            for i in range(out_tiles if self.order_no == 0 else 4):
                if job >= 8:
                    pe.wait_ge(self.iv_ready, job - 7)
                for k in range(freq):
                    if self.order_no == 0:
                        last = nc.tensor.matmul(PS[:, job % 8, :], m[:, k, i * P:(i + 1) * P], H[:, first + k, :],
                                                start=(k == 0), stop=(k == freq - 1))
                    else:
                        last = nc.tensor.matmul(PS[:, job % 8, 0:out_tiles * P], H[:, first + k, i * P:(i + 1) * P], m[:, k, :],
                                                start=(k == 0), stop=(k == freq - 1))
                last.then_inc(self.iv_mm, 1)
                job += 1

    def take_filter_spectra(self, act):
        t = 0
        for name in NAMES:
            for q in range(LEAVES[name][2]):
                for dst in spectrum_pair(self.H, name, q):
                    act.wait_ge(self.hs_mm, t + 1)
                    self.K.nc.scalar.copy(dst, self.K.PS[:, t % 8, :]).then_inc(self.hs_ready, 1)
                    t += 1

    def take_inverse(self, act):
        nc, PS, job = self.K.nc, self.K.PS, 0
        for name in NAMES:
            out_tiles = self.K.io["inv_" + name].shape[1] // P
            act.wait_ge(self.zs_ready, 9)
            for i in range(out_tiles if self.order_no == 0 else 4):
                act.wait_ge(self.iv_mm, job + 1)
                if self.order_no == 0:
                    nc.scalar.copy(self.rec_of[name][:, i, :], PS[:, job % 8, :]).then_inc(self.iv_ready, 1)
                else:
                    dst = self.rec_of[name][:, :, i * P:(i + 1) * P]
                    nc.scalar.copy(dst, PS[:, job % 8, 0:out_tiles * P].rearrange("p (a b) -> p a b", b=P)).then_inc(self.iv_ready, 1)
                job += 1

    def total_and_difference(self, link, a, b):
        nc = self.K.nc
        link(nc.vector.tensor_tensor(b, a, b, ALU.add))
        link(nc.vector.scalar_tensor_tensor(a, a, 2.0, b, ALU.mult, ALU.subtract))

    def split_negacyclic(self, link, v):
        nc = self.K.nc
        self.total_and_difference(link, v[:, 2:4, :], v[:, 6:8, :])
        for lo, hi in ((0, 2), (4, 6)):
            link(nc.vector.scalar_tensor_tensor(v[:, hi:hi + 2, :], v[:, hi:hi + 2, :], -R2, v[:, lo:lo + 2, :], ALU.mult, ALU.add))
            link(nc.vector.scalar_tensor_tensor(v[:, lo:lo + 2, :], v[:, lo:lo + 2, :], 2.0, v[:, hi:hi + 2, :], ALU.mult, ALU.subtract))

    def decay_rows(self, dve, t0, t1):
        for t in range(t0, t1):
            dve.wait_ge(self.f_mm, t + 1)
            dve.wait_ge(self.dec_in[t % 4], 16 * (t // 4 + 1))
            dst = (self.neg if t < 8 else self.cyc)[:, t % 8, :]
            self.K.nc.vector.tensor_tensor(dst, self.K.PS[:, 4 + t % 2, :], self.dec[:, t % 4, :], ALU.mult).then_inc(self.f_ready, 1)

    def filter_leaves(self, dve, link):
        nc, neg, cyc = self.K.nc, self.neg, self.cyc
        dve.wait_ge(self.f_ready, 16)
        link(nc.vector.tensor_tensor(neg[0:1, 0, :], neg[0:1, 0, :], self.bias_row[0:1, :], ALU.add))
        self.total_and_difference(link, neg[:, :, :], cyc[:, :, :])
        self.total_and_difference(link, cyc[:, 0:4, :], cyc[:, 4:8, :])
        self.total_and_difference(link, cyc[:, 4:6, :], cyc[:, 6:8, :])
        self.split_negacyclic(link, neg)
        nc.vector.memset(self.tmp[:, 0, 0:1], 0.0).then_inc(self.lf_ready, 1)

    def z_leaves(self, dve, link):
        nc, z, cyc = self.K.nc, self.z, self.cyc2
        link(nc.vector.tensor_tensor(cyc[:, 0:4, :], z[:, 0:4, :], z[:, 4:8, :], ALU.subtract))
        link(nc.vector.tensor_tensor(cyc[:, 4:8, :], z[:, 0:4, :], z[:, 4:8, :], ALU.add))
        self.total_and_difference(link, cyc[:, 4:6, :], cyc[:, 6:8, :])
        self.split_negacyclic(link, z)
        nc.vector.memset(self.tmp[:, 0, 0:1], 0.0).then_inc(self.zl_ready, 1)

    def multiply_spectra(self, dve, link):
        nc, PS, H, tmp, pair = self.K.nc, self.K.PS, self.H, self.tmp, 0
        dve.wait_ge(self.hs_ready, 18)
        for name in NAMES:
            kt, first, pairs = LEAVES[name]
            for q in range(pairs):
                t = first + 2 * q
                dve.wait_ge(self.zs_mm, t + 2)
                if pair:
                    dve.wait_ge(self.zs_ready, pair)
                else:
                    dve.wait_ge(self.zl_ready, 1)
                pair += 1
                hr, hi = spectrum_pair(H, name, q)
                zr, zi = PS[:, t % 8, :], PS[:, (t + 1) % 8, :]
                for dst, a, b in ((0, zr, hr), (1, zi, hi), (2, zr, hi)):
                    nc.vector.tensor_tensor(tmp[:, dst, :], a, b, ALU.mult)
                link(nc.vector.tensor_tensor(tmp[:, 3, :], zi, hr, ALU.mult))
                nc.vector.tensor_tensor(hr, tmp[:, 0, :], tmp[:, 1, :], ALU.subtract)
                nc.vector.tensor_tensor(hi, tmp[:, 2, :], tmp[:, 3, :], ALU.add).then_inc(self.zs_ready, 1)

    def recombine(self, dve, link):
        nc, y = self.K.nc, self.z
        Pm, Mm, Am, Bm = self.rec["P"], self.rec["M"], self.rec["A"], self.rec["B"]
        self.total_and_difference(link, Pm, Mm)
        self.total_and_difference(link, Pm[:, 0:2, :], Pm[:, 2:4, :])
        link(nc.vector.tensor_tensor(Am[:, 0:2, :], Am[:, 0:2, :], Am[:, 2:4, :], ALU.add))
        link(nc.vector.scalar_tensor_tensor(Am[:, 2:4, :], Am[:, 2:4, :], 2.0, Am[:, 0:2, :], ALU.mult, ALU.subtract))
        self.total_and_difference(link, Am, Bm)
        link(nc.vector.tensor_tensor(y[:, 0:2, :], Mm[:, 0:2, :], Bm[:, 0:2, :], ALU.add))
        link(nc.vector.scalar_tensor_tensor(y[:, 2:4, :], Pm[:, 2:4, :], R2, Bm[:, 2:4, :], ALU.mult, ALU.add))
        link(nc.vector.tensor_tensor(y[:, 4:6, :], Mm[:, 2:4, :], Am[:, 0:2, :], ALU.add))
        link(nc.vector.scalar_tensor_tensor(y[:, 6:8, :], Pm[:, 0:2, :], -R2, Am[:, 2:4, :], ALU.mult, ALU.add))


def hyena(K):
    nc = K.nc
    x2, ghy, yT = K.at(X1T, 4, S), K.at(GHY, 4, S), K.at(X1T, 4, S)
    with ExitStack() as ctx:
        order, yT_ready = K.sem("hyena_order"), K.sem("hyena_y")
        net = FilterNetwork(K)
        hy = [HyenaProjections(K, "hy0_", 0), HyenaProjections(K, "hy8_", 8, x2, ghy)]
        lc = [LongConvolution(K, 0), LongConvolution(K, 1)]
        rows_after = {3: (0, 6), 4: (6, 12), 5: (12, 16)}
        block = ctx.enter_context(nc.Block())

        @block.sync
        def _(sp):
            for o in range(2):
                if o == 1:
                    sp.wait_ge(lc[0].zs_mm, 18)
                lc[o].load_filter(sp)
                if o == 1:
                    sp.wait_ge(lc[0].iv_mm, lc[0].jobs)
                hy[o].load(sp, lc[o])

        @block.gpsimd
        def _(pool):
            net.load(pool)
            lc[0].load_matrices(pool)
            pool.wait_ge(lc[0].iv_mm, lc[0].jobs)
            lc[1].load_matrices(pool)

        @block.tensor
        def _(pe):
            for o in range(2):
                if o == 1:
                    pe.wait_ge(lc[0].iv_ready, lc[0].jobs)
                for n in range(8):
                    hy[o].project(pe, n)
                    if n >= 2:
                        hy[o].to_rows(pe, n - 2)
                    if o == 0 and n < 3:
                        net.pe(pe, n)
                    if n in rows_after:
                        if o == 0 and n == 3:
                            pe.wait_ge(net.sin, 3)
                            pe.wait_ge(net.taken, 12)
                        lc[o].filter_rows(pe, *rows_after[n])
                hy[o].to_rows(pe, 6)
                hy[o].to_rows(pe, 7)
                pe.wait_ge(hy[o].p_ready, 8)
                if o == 0:
                    pe.wait_ge(hy[o].z_ready, 8)
                lc[o].spectra(pe)
                lc[o].inverse(pe)

        @block.scalar
        def _(act):
            for o in range(2):
                act.wait_ge(hy[o].border_ready, 1)
                for n in range(8):
                    hy[o].take_projection(act, n)
                    if n >= 2:
                        hy[o].take_rows(act, n - 2)
                    if o == 0 and n < 3:
                        net.act(act, n)
                hy[o].take_rows(act, 6)
                hy[o].take_rows(act, 7)
                lc[o].take_filter_spectra(act)
                lc[o].take_inverse(act)

        @block.vector
        def _(dve):
            chain = Count(order)

            def link(ins, signal=chain):
                signal.by(ins)
                dve.wait_ge(signal.sem, signal.n)

            for o in range(2):
                if o == 1:
                    dve.wait_ge(lc[0].iv_ready, lc[0].jobs)
                hy[o].border(dve)
                if o == 1:
                    lc[0].recombine(dve, link)
                    link(nc.vector.tensor_tensor(lc[0].z, lc[0].z, lc[0].x1t, ALU.mult))
                for n in range(8):
                    hy[o].convolve(dve, link, n)
                    if o == 0 and n < 3:
                        net.dve(dve, link, n)
                    if n in rows_after:
                        lc[o].decay_rows(dve, *rows_after[n])
                    if n == 5:
                        lc[o].filter_leaves(dve, link)
                if o == 0:
                    dve.wait_ge(hy[0].z_ready, 8)
                lc[o].z_leaves(dve, link)
                lc[o].multiply_spectra(dve, link)
            dve.wait_ge(lc[1].iv_ready, lc[1].jobs)
            lc[1].recombine(dve, link)
            for c in range(4):
                yc = lc[1].z[:, :, c * P:(c + 1) * P]
                blocks = lambda a: a.rearrange("p (a b) -> p a b", b=P)
                link(nc.vector.tensor_tensor(blocks(yT[:, c, :]), yc, blocks(x2[:, c, :]), ALU.mult))
                link(nc.vector.tensor_tensor(yT[:, c, :], yT[:, c, :], ghy[:, c, :], ALU.mult))


HT_HI = 42368
YATT, YHY = ZV, X1T
SLOPES = [2.0 ** (-(h + 1)) for h in range(8)]
TILES = 10
UNITS = 32


def unit_kind(u):
    return u < 16, (u % 16) // 2, u % 2


def first_key(i):
    return min(max(P * i - 64, 0), S - 256)


V_TILES = ([(0, 0, 1), (0, 128, 1)] + [(0, 64 + P * m, 1) for m in range(7)] + [(0, 768, 1), (0, 896, 1)]
           + [(1, c + 512 * half, 4) for c in range(4) for half in range(2)] + [(2, r, 8) for r in range(8)])
V_GROUPS = [list(range(g, min(g + 4, len(V_TILES)))) for g in range(0, len(V_TILES), 4)]


def unit_blocks(u):
    strided, i, _ = unit_kind(u)
    if strided:
        return [V_TILES.index((1, i % 4, 4)), V_TILES.index((1, i % 4 + 512, 4)), V_TILES.index((2, i, 8))]
    return [V_TILES.index((0, first_key(i), 1)), V_TILES.index((0, first_key(i) + P, 1))]


def dilated_attention(K):
    nc, io, PS = K.nc, K.io, K.PS
    o = YATT
    w_slots = K.at(o, 2, KT * P)
    w_parts = [(K.part(f"da_w{j}_hi", o + (2 + j) * KT * P, KT * P), K.part(f"da_w{j}_rest", o + j * KT * P, KT * P)) for j in range(2)]
    o += 4 * KT * P
    vrows = K.at(o, 27, P); o += 27 * P
    assert YATT + 4096 <= YHY
    qk = K.at(o, 2, 6, S); o += 12 * S
    vT = K.at(o, 3, S); o += 3 * S
    gat = K.at(o, 2, S); o += 2 * S
    bias = K.at(o, 2, 1536); o += 3072
    st_b = K.at(o, 8, 2, 66); o += 1056
    outs = K.at(o, NT, P); o += NT * P
    sb = [K.at(o, 384)]; o += 384
    assert o <= HT_HI
    o = HT_HI + KT * S
    sb += [K.at(o, 384), K.at(o + 384, 384)]; o += 768
    back = K.at(o, 8, 2, 66); o += 1056
    o = H3
    pt = K.at(o, 2, 384); o += 768
    st_a = K.at(o, 8, 2, 66); o += 1056
    nm = K.at(o, 4); o += 4
    mx = K.at(o, 16); o += 16
    ex = K.at(o, 2, 16); o += 32
    den = K.at(o, 16); o += 16
    assert o <= FREE1
    hT, cols1, ident = K.at(HT, KT, S), K.at(COLS1, N_COLS1), K.at(IDENT, P)
    K.h_parts = [(K.part(f"h{c}_hi", HT_HI + 2 * S * c, 2, S), K.part(f"h{c}_rest", HT + 2 * S * c, 2, S)) for c in range(KT // 2)]
    K.branches = nc.dram_tensor("branches", (2, P, 4 * S), fp32, kind="Internal").ap()
    w = io["w_in"][0].rearrange("(k p) n -> p k n", p=P)
    scratch = nc.dram_tensor("strided_sums", (S, 132), fp32, kind="Internal").ap()
    pairs = 4
    halves = 2 * TILES

    def tile_column(T):
        j, t = T // TILES, T % TILES
        return (36 + j) if t == 9 else (t // 3) * 12 + (t % 3) * 4 + j

    def dest(T):
        j, t = T // TILES, T % TILES
        return gat[:, j % 2, :] if t == 9 else (vT[:, t - 6, :] if t >= 6 else qk[:, j % 2, t, :])

    def projections(j):
        after = [[] for _ in range(UNITS + 1)]
        if j + 1 < pairs:
            for n in range(halves):
                after[min(2 * n, UNITS) if n < 16 else UNITS].append((j + 1) * halves + n)
        return after

    def bank_of_t(j, n):
        g = j * 41 + n
        return g, 2 + g % 2

    with ExitStack() as ctx:
        s = lambda n: K.sem("da_" + n)
        h_hi, h_rest, w_hi, w_rest, yhy_out, y_out = s("h_hi"), s("h_rest"), s("w_hi"), s("w_rest"), s("yhy_out"), s("y_out")
        w_in, dist_in = [s(f"w_in{b}") for b in range(2)], s("dist_in")
        proj_mm, proj_ready, order = s("proj_mm"), s("proj_ready"), s("order")
        t_done, t_taken, bias_ready = s("t_done"), s("t_taken"), s("bias")
        s_done, s_taken, nm_ready, exp_done, pv_done, o_ready = s("s_done"), s("s_taken"), s("nm"), s("exp"), s("pv"), s("o")
        sums_out, sums_in, comb_d, comb_e, comb_done, y_ready = s("sums_out"), s("sums_in"), s("comb_d"), s("comb_e"), s("comb"), s("y")
        block = ctx.enter_context(nc.Block())

        @block.sync
        def _(sp):
            def load(T):
                if T >= 2:
                    sp.wait_ge(proj_mm, 2 * (T - 1))
                c0 = tile_column(T) * P
                sp.dma_start(w_slots[:, T % 2, :].rearrange("p (k n) -> p k n", n=P), w[:, :, c0:c0 + P]).then_inc(w_in[T % 2], 16)

            load(0)
            load(1)
            sp.dma_start(K.branches[1], K.at(YHY, 4 * S)).then_inc(yhy_out, 16)
            for h in range(2):
                sp.dma_start(bias[:, h, :], io["dist"]).then_inc(dist_in, 16)
            for T in range(2, TILES * pairs):
                load(T)
            sp.wait_ge(yhy_out, 16)

        @block.gpsimd
        def _(pool):
            def rest(T):
                pool.wait_ge(w_hi, T + 1)
                hi, lo = w_parts[T % 2]
                nc.gpsimd.tensor_tensor(lo, w_slots[:, T % 2, :], hi.bitcast(fp32), ALU.subtract).then_inc(w_rest, 1)

            def output(j):
                pool.wait_ge(y_ready, j + 1)
                pool.dma_start(K.branches[0][:, j * S:(j + 1) * S], gat[:, j % 2, :]).then_inc(y_out, 16)

            for T in range(TILES):
                rest(T)
            for j in range(pairs):
                more = [TILES * (j + 1) + t for t in range(TILES)] if j + 1 < pairs else []
                for T in more[:4]:
                    rest(T)
                if j >= 1:
                    output(j - 1)
                for T in more[4:6]:
                    rest(T)
                pool.wait_ge(o_ready, UNITS * j + 16)
                pool.dma_start(scratch.rearrange("(n r) c -> n r c", r=8), st_b.rearrange("p r h c -> p r (h c)")).then_inc(sums_out, 16)
                pool.wait_ge(sums_out, 16 * (j + 1))
                if j >= 1:
                    pool.wait_ge(comb_done, j)
                pool.dma_start(back.rearrange("p r h c -> p r (h c)"), scratch.rearrange("(i p) c -> p i c", p=P)).then_inc(sums_in, 16)
                for T in more[6:]:
                    rest(T)
            output(pairs - 1)
            pool.wait_ge(y_out, 16 * pairs)

        @block.tensor
        def _(pe):
            def project(n):
                T, h = n // 2, n % 2
                pe.wait_ge(w_rest, T + 1)
                if n >= 2:
                    pe.wait_ge(proj_ready, n - 1)
                for k in range(KT):
                    if T == 0 and k % 2 == 0:
                        pe.wait_ge(h_rest, 4 * h + k // 2 + 1)
                    last = split_product(nc, PS[:, 6 + h, :], tuple(v[:, k * P:(k + 1) * P] for v in w_parts[T % 2]),
                                         tuple(v[:, k % 2, h * 512:(h + 1) * 512] for v in K.h_parts[k // 2]), k == 0, k == KT - 1)
                last.then_inc(proj_mm, 1)

            def transposes(j, n, sources):
                g, b = bank_of_t(j, n)
                if g >= 2:
                    pe.wait_ge(t_taken, g - 1)
                for i, src in enumerate(sources):
                    last = nc.tensor.transpose(PS[:, b, i * P:(i + 1) * P], src, ident)
                last.then_inc(t_done, 1)

            def scores(j, u):
                U = UNITS * j + u
                strided, i, h = unit_kind(u)
                if U >= 2:
                    pe.wait_ge(s_taken, U - 1)
                head = slice(64 * h, 64 * h + 64)
                q = lambda g: qk[head, j % 2, g, :]
                k = lambda g: qk[head, j % 2, 3 + g, :]
                b = PS[:, U % 2, :]
                if strided:
                    nc.tensor.matmul(b[:, 0:256], q(1)[:, i:S:8], k(1)[:, i % 4:S:4], start=True, stop=True)
                    last = nc.tensor.matmul(b[:, 256:384], q(2)[:, i:S:8], k(2)[:, i:S:8], start=True, stop=True)
                else:
                    k0 = first_key(i)
                    last = nc.tensor.matmul(b[:, 0:256], q(0)[:, i * P:(i + 1) * P], k(0)[:, k0:k0 + 256], start=True, stop=True)
                last.then_inc(s_done, 1)

            def prob_transposes(j, u):
                U = UNITS * j + u
                pe.wait_ge(exp_done, U + 1)
                transposes(j, 7 + u, [sb[U % 3][:, b * P:(b + 1) * P] for b in range(len(unit_blocks(u)))])

            def values(j, u):
                U = UNITS * j + u
                _, _, h = unit_kind(u)
                pe.wait_ge(t_taken, bank_of_t(j, 7 + u)[0] + 1)
                if U >= 2:
                    pe.wait_ge(o_ready, U - 1)
                blocks = unit_blocks(u)
                for b, v in enumerate(blocks):
                    last = nc.tensor.matmul(PS[:, 4 + U % 2, 0:HD], pt[:, U % 2, b * P:(b + 1) * P], vrows[:, v, h * HD:(h + 1) * HD],
                                            start=(b == 0), stop=(b == len(blocks) - 1))
                last.then_inc(pv_done, 1)

            for n in range(halves):
                project(n)
            for j in range(pairs):
                pe.wait_ge(proj_ready, halves * (j + 1))
                for g, tiles in enumerate(V_GROUPS):
                    transposes(j, g, [vT[:, V_TILES[v][0], V_TILES[v][1]:V_TILES[v][1] + P * V_TILES[v][2] - V_TILES[v][2] + 1:V_TILES[v][2]] for v in tiles])
                extra = projections(j)
                for u in range(UNITS + 2):
                    if u < UNITS:
                        scores(j, u)
                        for n in extra[u]:
                            project(n)
                    if 1 <= u <= UNITS:
                        prob_transposes(j, u - 1)
                    if u >= 2:
                        values(j, u - 2)
                for n in extra[UNITS]:
                    project(n)
                pe.wait_ge(comb_done, j + 1)
                for g in range(2):
                    transposes(j, 39 + g, [outs[:, i, :] for i in range(4 * g, 4 * g + 4)])

        @block.scalar
        def _(act):
            def round_weights(T):
                act.wait_ge(w_in[T % 2], 16 * (T // 2 + 1))
                nc.scalar.copy(w_parts[T % 2][0], w_slots[:, T % 2, :]).then_inc(w_hi, 1)

            def take_projection(n):
                T, h = n // 2, n % 2
                t = T % TILES
                if h == 0 and T >= 1 and T + 1 < TILES * pairs:
                    round_weights(T + 1)
                act.wait_ge(proj_mm, n + 1)
                if t == 9 and T // TILES >= 2:
                    act.wait_ge(y_out, 16 * (T // TILES - 1))
                c = tile_column(T)
                nc.scalar.activation(dest(T)[:, h * 512:(h + 1) * 512], PS[:, 6 + h, :], ACT.Silu if t == 9 else ACT.Identity,
                                     bias=cols1[:, c:c + 1]).then_inc(proj_ready, 1)

            def stats_of(u):
                strided, i, h = unit_kind(u)
                return (st_b if strided else st_a)[:, i, h, :]

            def exponentials(j, u):
                U = UNITS * j + u
                n = 384 if unit_kind(u)[0] else 256
                act.wait_ge(nm_ready, U + 1)
                nc.scalar.activation(sb[U % 3][:, 0:n], sb[U % 3][:, 0:n], ACT.Exp, bias=nm[:, U % 4:U % 4 + 1], scale=0.125,
                                     accum_out=stats_of(u)[:, 64:65]).then_inc(exp_done, 1)

            def take_output(j, u):
                U = UNITS * j + u
                act.wait_ge(pv_done, U + 1)
                nc.scalar.copy(stats_of(u)[:, 0:HD], PS[:, 4 + U % 2, 0:HD]).then_inc(o_ready, 1)

            round_weights(0)
            for h in range(2):
                for c in range(4):
                    half = slice(h * 512, (h + 1) * 512)
                    nc.scalar.copy(K.h_parts[c][0][:, :, half], hT[:, 2 * c:2 * c + 2, half]).then_inc(h_hi, 1)
                if h == 0:
                    round_weights(1)
            act.wait_ge(yhy_out, 16)
            for n in range(halves):
                take_projection(n)
            for j in range(pairs):
                if j >= 1:
                    act.wait_ge(sums_out, 16 * j)
                    act.wait_ge(comb_done, j)
                extra = projections(j)
                for u in range(UNITS + 2):
                    if u < UNITS:
                        exponentials(j, u)
                        for n in extra[u]:
                            take_projection(n)
                    if u >= 2:
                        take_output(j, u - 2)
                act.wait_ge(comb_d, j + 1)
                nc.scalar.activation(ex, ex, ACT.Exp, scale=0.125).then_inc(comb_e, 1)
                for n in extra[UNITS]:
                    take_projection(n)

        @block.vector
        def _(dve):
            chain = Count(order)
            done = Count(comb_done)
            diff = Count(comb_d)

            def link(ins, signal=chain):
                signal.by(ins)
                dve.wait_ge(signal.sem, signal.n)

            def take_scores(j, u):
                U = UNITS * j + u
                strided, i, h = unit_kind(u)
                n = 384 if strided else 256
                col = 768 + 384 * (i // 4) if strided else 256 * (0 if i == 0 else 2 if i == NT - 1 else 1)
                st = (st_b if strided else st_a)[:, i, h, :]
                dve.wait_ge(s_done, U + 1)
                if U >= 3:
                    dve.wait_ge(t_done, bank_of_t((U - 3) // UNITS, 7 + (U - 3) % UNITS)[0] + 1)
                nc.vector.tensor_tensor_reduce(out=sb[U % 3][:, 0:n], in0=PS[:, U % 2, 0:n], in1=bias[:, h, col:col + n],
                                               scale=1.0, scalar=-3e38, op0=ALU.add, op1=ALU.max, accum_out=st[:, 65:66]).then_inc(s_taken, 1)
                dve.wait_ge(s_taken, U + 1)
                nc.vector.tensor_scalar(nm[:, U % 4:U % 4 + 1], st[:, 65:66], -0.125, None, ALU.mult).then_inc(nm_ready, 1)

            def take_transposes(j, n, dst, wait=None):
                g, b = bank_of_t(j, n)
                dve.wait_ge(t_done, g + 1)
                cols = dst.shape[1] * (dst.shape[2] if len(dst.shape) == 3 else 1)
                src = PS[:, b, 0:cols]
                if len(dst.shape) == 3:
                    src = src.rearrange("p (a b) -> p a b", a=dst.shape[1])
                return src

            for n in range(8):
                c, half = n % 4, slice(n // 4 * 512, (n // 4 + 1) * 512)
                hi, lo = K.h_parts[c]
                dve.wait_ge(h_hi, n + 1)
                nc.vector.tensor_tensor(lo[:, :, half], hT[:, 2 * c:2 * c + 2, half], hi[:, :, half].bitcast(fp32), ALU.subtract).then_inc(h_rest, 1)
            for j in range(pairs):
                if j == 0:
                    dve.wait_ge(dist_in, 32)
                    dve.wait_ge(yhy_out, 16)
                else:
                    dve.wait_ge(s_taken, UNITS * j)
                for h in range(2):
                    link(nc.vector.tensor_scalar(bias[:, h, :], bias[:, h, :], -8.0 * SLOPES[h] if j == 0 else SLOPES[2] / SLOPES[0], None, ALU.mult))
                for g, tiles in enumerate(V_GROUPS):
                    dst = vrows[:, tiles[0]:tiles[-1] + 1, :]
                    nc.vector.tensor_copy(dst, take_transposes(j, g, dst)).then_inc(t_taken, 1)
                if j >= 1:
                    dve.wait_ge(sums_out, 16 * j)
                for u in range(UNITS + 1):
                    if u < UNITS:
                        take_scores(j, u)
                    if u >= 1:
                        U = UNITS * j + u - 1
                        if U >= 2:
                            dve.wait_ge(pv_done, U - 1)
                        n = 384 if unit_kind(u - 1)[0] else 256
                        dst = pt[:, U % 2, 0:n]
                        nc.vector.tensor_copy(dst, take_transposes(j, 6 + u, dst)).then_inc(t_taken, 1)
                dve.wait_ge(o_ready, UNITS * (j + 1))
                dve.wait_ge(sums_in, 16 * (j + 1))
                pick = lambda st, c: st[:, :, :, c:c + 1].rearrange("p r h c -> p (r h) c")[:, :, 0]
                link(nc.vector.tensor_tensor(mx, pick(st_a, 65), pick(back, 65), ALU.max))
                link(nc.vector.tensor_tensor(ex[:, 0, :], pick(st_a, 65), mx, ALU.subtract))
                link(nc.vector.tensor_tensor(ex[:, 1, :], pick(back, 65), mx, ALU.subtract), diff)
                dve.wait_ge(comb_e, j + 1)
                link(nc.vector.tensor_tensor(mx, pick(st_a, 64), ex[:, 0, :], ALU.mult))
                link(nc.vector.tensor_tensor(den, pick(back, 64), ex[:, 1, :], ALU.mult))
                link(nc.vector.tensor_tensor(den, den, mx, ALU.add))
                link(nc.vector.reciprocal(den, den))
                for n in range(2):
                    link(nc.vector.tensor_tensor(ex[:, n, :], ex[:, n, :], den, ALU.mult))
                for n, st in enumerate((st_a, back)):
                    v = st[:, :, :, 0:HD].rearrange("p r h c -> p (r h) c")
                    link(nc.vector.tensor_tensor(v, v, ex[:, n, :].unsqueeze(2).to_broadcast([P, 16, HD]), ALU.mult))
                    if n == 1:
                        link(nc.vector.tensor_tensor(outs.rearrange("p r (h c) -> p (r h) c", h=2), v,
                                                     st_a[:, :, :, 0:HD].rearrange("p r h c -> p (r h) c"), ALU.add), done)
                for g in range(2):
                    dst = gat[:, j % 2, g * 512:(g + 1) * 512]
                    ins = nc.vector.tensor_tensor(dst, take_transposes(j, 39 + g, dst), dst, ALU.mult)
                    ins.then_inc(t_taken, 1)
                dve.wait_ge(t_taken, bank_of_t(j, 40)[0] + 1)
                nc.vector.memset(mx[:, 0:1], 0.0).then_inc(y_ready, 1)


MWT = LF
MERGED = 34176
WOUT_A, WOUT_B = MERGED + 8192, MERGED - 4096


def merge_branches(K):
    nc, io, PS = K.nc, K.io, K.PS
    SLOT = KT * P + 4 * P
    Y_HI = [MWT + 4 * SLOT + 4 * S, MWT + 4 * SLOT]
    W_HI = MWT + 2 * SLOT
    Y = [YATT, YHY]
    assert MERGED + 8192 <= HT_HI and Y_HI[0] + 4096 <= MERGED and WOUT_B == Y_HI[0] and YHY + 4096 <= MWT
    cols1, merged, sg = K.at(COLS1, N_COLS1), K.at(MERGED, KT, S), K.at(H3, 4, 512)
    y_parts = [[(K.part(f"mg_y{a}{c}_hi", Y_HI[a] + 2 * S * c, 2, S), K.part(f"mg_y{a}{c}_rest", Y[a] + 2 * S * c, 2, S))
                for c in range(2)] for a in range(2)]
    w_parts = [(K.part(f"mg_w{j}_hi", W_HI + SLOT * j, SLOT), K.part(f"mg_w{j}_rest", MWT + SLOT * j, SLOT)) for j in range(2)]
    w_slots = K.at(MWT, 2, SLOT)
    w = io["w_in"][0].rearrange("(k p) n -> p k n", p=P)
    wy = [io[name][0].rearrange("(k p) n -> p k n", p=P) for name in ("w_proj_attn", "w_proj_hyena")]
    wout = io["w_out"][0].rearrange("(k p) n -> p k n", p=P)
    units = 2 * KT

    start = [("w", 0), ("w", 1)] + [("y", a, h, c) for a in range(2) for h in range(2) for c in range(2)]
    items = start + [("w", u) for u in range(2, units)]

    def views(item):
        if item[0] == "w":
            j = item[1] % 2
            return w_slots[:, j, :], *w_parts[j]
        _, a, h, c = item
        source, parts = K.at(Y[a] + 2 * S * c, 2, S), y_parts[a][c]
        return tuple(v[:, :, h * 512:(h + 1) * 512] for v in (source, *parts))

    with ExitStack() as ctx:
        s = lambda n: K.sem("mg_" + n)
        w_in, hi_ready, rest_ready, wout_in = [s("w_in0"), s("w_in1")], s("hi"), s("rest"), s("wout_in")
        y_in = [s("y_in0"), s("y_in1")]
        r_mm, y_mm, sig_ready, merged_ready, order = s("r_mm"), s("y_mm"), s("sig"), s("merged"), s("order")
        block = ctx.enter_context(nc.Block())

        @block.sync
        def _(sp):
            for u in range(units):
                k, a = u % KT, u // KT
                if u >= 2:
                    sp.wait_ge(r_mm, 2 * (u - 1))
                    sp.wait_ge(y_mm, 2 * (u - 1))
                c0 = COL_R + a * D + k * P
                sp.dma_start(w_slots[:, u % 2, 0:KT * P].rearrange("p (c n) -> p c n", n=P), w[:, :, c0:c0 + P]).then_inc(w_in[u % 2], 16)
                sp.dma_start(w_slots[:, u % 2, KT * P:SLOT].rearrange("p (c n) -> p c n", n=P), wy[a][:, :, k * P:(k + 1) * P]).then_inc(w_in[u % 2], 16)
                if u == KT + 2:
                    sp.dma_start(K.at(WOUT_B, 4, D), wout[:, 4:8, :]).then_inc(wout_in, 16)
            sp.wait_ge(wout_in, 16)

        @block.gpsimd
        def _(pool):
            for a in range(2):
                pool.dma_start(K.at(Y[a], 4 * S), K.branches[a]).then_inc(y_in[a], 16)

        @block.tensor
        def _(pe):
            for n in range(2 * units):
                u, h = n // 2, n % 2
                a, b = u // KT, 2 * (n % 4)
                half = slice(h * 512, (h + 1) * 512)
                cols = lambda c: tuple(v[:, c * P:(c + 1) * P] for v in w_parts[u % 2])
                if n >= 4:
                    pe.wait_ge(merged_ready, n - 3)
                if h == 0:
                    pe.wait_ge(rest_ready, items.index(("w", u)) + 1)
                for c in range(KT):
                    last = split_product(nc, PS[:, b, :], cols(c), tuple(v[:, c % 2, half] for v in K.h_parts[c // 2]), c == 0, c == KT - 1)
                last.then_inc(r_mm, 1)
                if u % KT == 0:
                    pe.wait_ge(rest_ready, items.index(("y", a, h, 1)) + 1)
                for c in range(4):
                    last = split_product(nc, PS[:, b + 1, :], cols(KT + c), tuple(v[:, c % 2, half] for v in y_parts[a][c // 2]), c == 0, c == 3)
                last.then_inc(y_mm, 1)

        @block.scalar
        def _(act):
            def round_part(item):
                if item[0] == "w":
                    act.wait_ge(w_in[item[1] % 2], 32 * (item[1] // 2 + 1))
                else:
                    act.wait_ge(y_in[item[1]], 16)
                operand, hi, _ = views(item)
                nc.scalar.copy(hi, operand).then_inc(hi_ready, 1)

            for item in start:
                round_part(item)
            for n in range(2 * units):
                u = n // 2
                act.wait_ge(r_mm, n + 1)
                if n >= 4:
                    act.wait_ge(merged_ready, n - 3)
                col = COL_R // P + u
                nc.scalar.activation(sg[:, n % 4, :], PS[:, 2 * (n % 4), :], ACT.Sigmoid, bias=cols1[:, col:col + 1]).then_inc(sig_ready, 1)
                if n % 2 == 0 and 2 <= u + 1 < units and u >= 1:
                    round_part(("w", u + 1))

        @block.vector
        def _(dve):
            chain = Count(order)

            def link(ins, signal=chain):
                signal.by(ins)
                dve.wait_ge(signal.sem, signal.n)

            def rest(item):
                dve.wait_ge(hi_ready, items.index(item) + 1)
                operand, hi, lo = views(item)
                nc.vector.tensor_tensor(lo, operand, hi.bitcast(fp32), ALU.subtract).then_inc(rest_ready, 1)

            for item in start:
                rest(item)
            for n in range(2 * units):
                u, h = n // 2, n % 2
                k, a, b = u % KT, u // KT, 2 * (n % 4)
                out, gate = merged[:, k, h * 512:(h + 1) * 512], sg[:, n % 4, :]
                dve.wait_ge(sig_ready, n + 1)
                dve.wait_ge(y_mm, n + 1)
                if a == 0:
                    nc.vector.tensor_tensor(out, PS[:, b + 1, :], gate, ALU.mult).then_inc(merged_ready, 1)
                else:
                    link(nc.vector.tensor_tensor(gate, PS[:, b + 1, :], gate, ALU.mult))
                    dve.wait_ge(merged_ready, n - 2 * KT + 1)
                    nc.vector.tensor_tensor(out, out, gate, ALU.add).then_inc(merged_ready, 1)
                if h == 0 and u >= 1 and u + 1 < units:
                    rest(("w", u + 1))


VECS = 1408 + 64
X2T = 11648
X2R = X2T + 8192
LATW = X2R
LAT = X2R + KT * 448
LATS = LAT + NT * 448


class RowNorm:

    def __init__(self, nc, dve, link, stat, var_signal, std_sem):
        self.nc, self.dve, self.link, self.stat, self.var, self.std = nc, dve, link, stat, var_signal, std_sem

    def __call__(self, row, gamma, beta, final=None):
        nc, st = self.nc, self.stat
        self.link(nc.vector.bn_stats(st[:, 0:6], row[:, 0:512]))
        self.link(nc.vector.bn_stats(st[:, 6:12], row[:, 512:1024]))
        self.link(nc.vector.bn_aggr(st[:, 12:14], st[:, 0:12]))
        self.link(nc.vector.tensor_scalar(st[:, 14:15], st[:, 13:14], 1e-5, None, ALU.add), self.var)
        self.dve.wait_ge(self.std, self.var.n)
        self.link(nc.vector.reciprocal(st[:, 15:16], st[:, 15:16]))
        self.link(nc.vector.tensor_scalar(row, row, st[:, 12:13], st[:, 15:16], ALU.subtract, ALU.mult))
        self.link(nc.vector.tensor_tensor(row, row, gamma, ALU.mult))
        self.link(nc.vector.tensor_tensor(row, row, beta, ALU.add), *([final] if final else []))


def first_output(K):
    nc, io, PS = K.nc, K.io, K.PS
    vec = K.at(VECS, 5, D)
    xin = K.at(VECS + 5 * D, 2, D)
    work = K.at(VECS + 7 * D, 2, D)
    stat = K.at(28032, 16)
    gate, merged, ident = K.at(GATE, D), K.at(MERGED, KT, S), K.at(IDENT, P)
    wout = [K.at(WOUT_A, 4, D), K.at(WOUT_B, 4, D)]
    x2r, x2T = K.at(X2R, NT, D), K.at(X2T, KT, S)
    x_class = io["x"][0].rearrange("(n r) d -> n r d", r=8)
    with ExitStack() as ctx:
        s = lambda n: K.sem("fo_" + n)
        x_in, vec_in, mm, t_read, x_used, order = [s("x_in0"), s("x_in1")], s("vec_in"), s("mm"), s("t_read"), s("x_used"), s("order")
        var, std, row_ready, tr, tr_taken, gated = s("var"), s("std"), s("row"), s("tr"), s("tr_taken"), s("gated")
        wout_in = [s(f"wout_in{k}") for k in range(4)]
        block = ctx.enter_context(nc.Block())

        @block.gpsimd
        def _(pool):
            for r in range(NT):
                pool.wait_ge(t_read, r + 1)
                nc.gpsimd.tensor_tensor(work[:, r % 2, :], work[:, r % 2, :], gate, ALU.mult).then_inc(gated, 1)

        @block.sync
        def _(sp):
            for k in range(4):
                sp.dma_start(wout[0][:, k, :], io["w_out"][0][k * P:(k + 1) * P, :]).then_inc(wout_in[k], 16)
            for n, v in enumerate((io["b_out"][0], io["ln_g"][0], io["ln_b"][0], io["ln_emb_g_2"], io["ln_emb_b_2"])):
                sp.dma_start(vec[:, n, :], bcast_rows(v)).then_inc(vec_in, 16)
            for r in range(NT):
                if r >= 2:
                    sp.wait_ge(x_used, r - 1)
                sp.dma_start(xin[:, r % 2, :], x_class[:, r, :]).then_inc(x_in[r % 2], 16)

        @block.tensor
        def _(pe):
            def out_rows(r):
                if r >= 2:
                    pe.wait_ge(t_read, r - 1)
                for i, k in enumerate([4, 5, 6, 7, 0, 1, 2, 3]):
                    if r == 0 and k < 4:
                        pe.wait_ge(wout_in[k], 16)
                    for h in range(2):
                        last = nc.tensor.matmul(PS[:, 2 * (r % 2) + h, :], merged[:, k, r:S:8], wout[k // 4][:, k % 4, h * 512:(h + 1) * 512],
                                                start=(i == 0), stop=(i == KT - 1))
                last.then_inc(mm, 1)

            def to_columns(r):
                pe.wait_ge(row_ready, r + 1)
                for g in range(2):
                    n = 2 * r + g
                    if n >= 4:
                        pe.wait_ge(tr_taken, n - 3)
                    for i in range(4):
                        k = 4 * g + i
                        last = nc.tensor.transpose(PS[:, 4 + n % 4, i * P:(i + 1) * P], x2r[:, r, k * P:(k + 1) * P], ident)
                    last.then_inc(tr, 1)

            for r in range(NT):
                out_rows(r)
                if r >= 1:
                    to_columns(r - 1)
            to_columns(NT - 1)

        @block.scalar
        def _(act):
            def take_columns(r):
                for g in range(2):
                    n = 2 * r + g
                    act.wait_ge(tr, n + 1)
                    nc.scalar.copy(x2T[:, 4 * g:4 * g + 4, r:S:8], PS[:, 4 + n % 4, :].rearrange("p (a b) -> p a b", b=P)).then_inc(tr_taken, 1)

            for r in range(NT):
                for n in range(2 * r, 2 * r + 2):
                    act.wait_ge(var, n + 1)
                    nc.scalar.activation(stat[:, 15:16], stat[:, 14:15], ACT.Sqrt).then_inc(std, 1)
                if r >= 1:
                    take_columns(r - 1)
            take_columns(NT - 1)

        @block.vector
        def _(dve):
            chain = Count(order)

            def link(ins, signal=chain):
                signal.by(ins)
                dve.wait_ge(signal.sem, signal.n)

            norm = RowNorm(nc, dve, link, stat, Count(var), std)
            rows, used, read = Count(row_ready), Count(x_used), Count(t_read)
            dve.wait_ge(vec_in, 80)
            for r in range(NT):
                dve.wait_ge(mm, r + 1)
                src = PS[:, 2 * (r % 2):2 * (r % 2) + 2, :].rearrange("p a b -> p (a b)")
                link(nc.vector.tensor_tensor(work[:, r % 2, :], src, vec[:, 0, :], ALU.add), read)
                dve.wait_ge(gated, r + 1)
                dve.wait_ge(x_in[r % 2], 16 * (r // 2 + 1))
                row = x2r[:, r, :]
                link(nc.vector.scalar_tensor_tensor(row, xin[:, r % 2, :], ALPHA, work[:, r % 2, :], ALU.mult, ALU.add), used)
                norm(row, vec[:, 1, :], vec[:, 2, :])
                norm(row, vec[:, 3, :], vec[:, 4, :], rows)


XS = VECS
QTAP = XS + 4096
S5S = QTAP + 4608
S5T = 28032
S5W, S5M, S5U, S5G, S5TMP = S5T + 4096, S5T + 8192, S5T + 12288, S5T + 16384, S5T + 20480
S5B = S5TMP + 2048
TC = 8
NCH = S // TC


def s5_states(K):
    nc, io, PS = K.nc, K.io, K.PS
    ident, cols2, x2T = K.at(IDENT, P), K.at(COLS2, 64), K.at(X2T, KT, S)
    xs = K.at(XS, 32, TC, 16)
    yg = K.at(S5T, TC, CH)
    QR, QN = K.at(QTAP, 16, 9, 16), K.at(QTAP + 2304, 16, 9, 16)
    Tc, Ts = K.at(S5T, 16, NCH), K.at(S5T + 2048, 16, NCH)
    W = K.at(S5W, 16, 2, P)
    M, U = K.at(S5M, 2, 16, P), K.at(S5U, 2, 16, P)
    WTr, WTi = K.at(S5M, 16, 8, 16), K.at(S5M + 2048, 16, 8, 16)
    wxs, Ksb = K.at(S5G, KT, CH), K.at(S5G, 2, 16, P)
    G = [K.at(S5G, 16, NCH), K.at(S5G + 2048, 16, NCH)]
    tmp = K.at(S5TMP, 4, 4, NCH)
    braw = K.at(S5TMP, 2, 16, 16)
    craw = K.at(S5W, 2, 4, P)
    kB, C = K.at(S5B, 2, 16, 16), K.at(S5B + 512, 2, 16, 16)
    pw, rev = K.at(S5B + 1024, 2, 9, 16), K.at(S5B + 1312, 2, 8, 16)
    o = S5S
    dskip = K.at(o, CH); o += CH
    ldt = K.at(o, 32); o += 32
    names = ("dt", "arg", "magarg", "kk", "sn", "cs", "mag", "rho", "den", "nr", "kre", "kim", "ta", "tb", "abre", "abim", "s8", "c8", "arg2", "argc")
    v = {}
    for n in names:
        v[n] = K.at(o, 16); o += 16
    args = K.at(o, 4, 16); o += 64
    trig = K.at(o, 4, 16); o += 64
    assert o <= X2T
    are, aim = cols2[:, 0:16], cols2[:, 16:32]
    wlat, lat, squares, ss = K.at(LATW, KT, 448), K.at(LAT, NT, 448), K.at(LATS + 16, 384), K.at(LATS, NT, 2)
    K.x2_rows = nc.dram_tensor("x2_rows", (P, NT * D), fp32, kind="Internal").ap()
    over_c = lambda a: a.unsqueeze(2).to_broadcast([P, 16, 16])
    with ExitStack() as ctx:
        s = lambda n: K.sem("s5_" + n)
        rows_out, lat_in, lat_mm, lat_ready = s("rows_out"), s("lat_in"), s("lat_mm"), s("lat")
        wxs_in, dt_in, b_in, c_in, ds_in = s("wxs_in"), s("dt_in"), s("b_in"), s("c_in"), s("ds_in")
        order, aorder = s("order"), s("aorder")
        c_tr, c_ready, xs_mm, xs_ready, u_tr, u_ready = s("c_tr"), s("c_ready"), s("xs_mm"), s("xs_ready"), s("u_tr"), s("u_ready")
        dt_ready, arg_ready, trig_ready = s("dt"), s("arg"), s("trig")
        wt_ready, w_tr, w_ready, kb_ready, k_mm, k_ready, m_clear, toeplitz = s("wt"), s("w_tr"), s("w"), s("kb"), s("k_mm"), s("k"), s("m_clear"), s("toeplitz")
        v_mm, v_read, h_ready, y_mm, y_ready, gelu_done = s("v_mm"), s("v_read"), s("h"), s("y_mm"), s("y"), s("gelu")
        block = ctx.enter_context(nc.Block())

        @block.sync
        def _(sp):
            sp.dma_start(ldt, bcast_rows(io["log_dt_2"][0])).then_inc(dt_in, 16)
            for n, name in enumerate(("b_re_2", "b_im_2")):
                sp.dma_start(braw[:, n, :, :], io[name][0].rearrange("(j g) p c -> (g p) j c", g=2)).then_inc(b_in, 16)
            for n, name in enumerate(("c_re_2", "c_im_2")):
                rows = io[name][0].rearrange("(q g) c p -> (g c) q p", q=4)
                for dup in range(2):
                    sp.dma_start(craw[:, n, :, dup * 64:dup * 64 + 64], rows).then_inc(c_in, 16)
            sp.dma_start(wxs, io["w_in_2"][0, :, 0:CH].rearrange("(k p) n -> p k n", p=P)).then_inc(wxs_in, 16)
            sp.dma_start(dskip, bcast_rows(io["d_skip_2"][0])).then_inc(ds_in, 16)
            sp.wait_ge(wxs_in, 16)
            sp.dma_start(K.x2_rows, K.at(X2R, NT * D)).then_inc(rows_out, 16)
            sp.wait_ge(rows_out, 16)
            sp.dma_start(wlat, io["w_in_2"][0, :, 2 * CH:2 * CH + 448].rearrange("(k p) n -> p k n", p=P)).then_inc(lat_in, 16)
            sp.wait_ge(k_ready, 8)
            sp.wait_ge(m_clear, 1)
            for t in range(TC):
                sp.dma_start(M[16 * t:16 * t + 16, :, :, 16 * t:P], Ksb[0:16, :, :, 0:P - 16 * t]).then_inc(toeplitz, 16)

        @block.gpsimd
        def _(pool):
            pool.wait_ge(w_tr, 8)
            nc.gpsimd.memset(K.at(S5M, 4096), 0.0).then_inc(m_clear, 1)

        @block.tensor
        def _(pe):
            pe.wait_ge(c_in, 64)
            for n in range(2):
                for q in range(4):
                    last = nc.tensor.transpose(PS[:, 6 + n, q * P:(q + 1) * P], craw[:, n, q, :], ident)
            last.then_inc(c_tr, 1)
            pe.wait_ge(wxs_in, 16)
            for t in range(TC):
                if t >= 6:
                    pe.wait_ge(xs_ready, t - 5)
                for k in range(KT):
                    last = nc.tensor.matmul(PS[:, t % 6, :], x2T[:, k, t:S:TC], wxs[:, k, :], start=(k == 0), stop=(k == KT - 1))
                last.then_inc(xs_mm, 1)
            pe.wait_ge(xs_ready, TC)
            pe.wait_ge(c_ready, 1)
            for n in range(8):
                q, g2 = n // 2, n % 2
                for i in range(4):
                    g = 2 * (4 * q + i) + g2
                    last = nc.tensor.transpose(PS[:, n, i * P:(i + 1) * P], xs[:, g, :, :], ident)
                last.then_inc(u_tr, 1)
            pe.wait_ge(wt_ready, 1)
            for n in range(8):
                pe.wait_ge(u_ready, n + 1)
                q, ri = n // 2, n % 2
                for i in range(4):
                    last = nc.tensor.transpose(PS[:, n, i * P:(i + 1) * P], (WTr, WTi)[ri][:, 4 * q + i, :, :], ident)
                last.then_inc(w_tr, 1)
            pe.wait_ge(kb_ready, 1)
            for n in range(8):
                pe.wait_ge(w_ready, n + 1)
                q, g2 = n // 2, n % 2
                half = slice(64 * g2, 64 * g2 + 64)
                for i in range(4):
                    j = 4 * q + i
                    nc.tensor.matmul(PS[0:16, n, i * P:(i + 1) * P], kB[half, 0, j, :], QR[half, j, 0:8, :], start=True, stop=False)
                    last = nc.tensor.matmul(PS[0:16, n, i * P:(i + 1) * P], kB[half, 1, j, :], QN[half, j, 0:8, :], start=False, stop=True)
                last.then_inc(k_mm, 1)
            for n in range(8):
                pe.wait_ge(k_ready, n + 1)
                q, ri = n // 2, n % 2
                for i in range(4):
                    j = 4 * q + i
                    for g2 in range(2):
                        half = slice(64 * g2, 64 * g2 + 64)
                        last = nc.tensor.matmul(PS[half, n, i * P:(i + 1) * P], W[:, j, ri, half], U[:, g2, j, :], start=True, stop=True)
                last.then_inc(v_mm, 1)
            pe.wait_ge(lat_in, 16)
            pe.wait_ge(v_read, 1)
            for i in range(NT):
                if i >= 2:
                    pe.wait_ge(lat_ready, i - 1)
                for k in range(KT):
                    last = nc.tensor.matmul(PS[:, i % 2, 0:448], x2T[:, k, i * P:(i + 1) * P], wlat[:, k, :], start=(k == 0), stop=(k == KT - 1))
                last.then_inc(lat_mm, 1)
            pe.wait_ge(lat_ready, NT)
            pe.wait_ge(toeplitz, 16 * TC)
            for n in range(8):
                q, g2 = n // 2, n % 2
                pe.wait_ge(v_read, 4)
                pe.wait_ge(h_ready, q + 1)
                half = slice(64 * g2, 64 * g2 + 64)
                for i in range(4):
                    j = 4 * q + i
                    out = PS[:, n, i * P:(i + 1) * P]
                    nc.tensor.matmul(out, U[:, g2, j, :], M[:, g2, j, :], start=True, stop=False)
                    nc.tensor.matmul(out, G[0][half, j, :], QR[half, j, 1:9, :], start=False, stop=False)
                    last = nc.tensor.matmul(out, G[1][half, j, :], QN[half, j, 1:9, :], start=False, stop=True)
                last.then_inc(y_mm, 1)

        @block.scalar
        def _(act):
            act.wait_ge(dt_ready, 1)
            nc.scalar.activation(v["dt"], v["dt"], ACT.Exp).then_inc(aorder, 1)
            act.wait_ge(arg_ready, 1)
            nc.scalar.activation(v["mag"], v["magarg"], ACT.Exp)
            nc.scalar.activation(v["rho"], v["magarg"], ACT.Exp, scale=float(TC))
            nc.scalar.activation(trig, args, ACT.Sin).then_inc(trig_ready, 1)
            for t in range(TC):
                act.wait_ge(xs_mm, t + 1)
                nc.scalar.copy(xs[:, :, t, :], PS[:, t % 6, :].rearrange("p (g c) -> p g c", c=16)).then_inc(xs_ready, 1)
            act.wait_ge(c_tr, 1)
            for n in range(8):
                act.wait_ge(u_tr, n + 1)
                nc.scalar.copy(U[:, n % 2, 4 * (n // 2):4 * (n // 2) + 4, :], PS[:, n, :].rearrange("p (a b) -> p a b", b=P)).then_inc(u_ready, 1)
            for n in range(8):
                act.wait_ge(w_tr, n + 1)
                nc.scalar.copy(W[:, 4 * (n // 2):4 * (n // 2) + 4, n % 2, :], PS[:, n, :].rearrange("p (a b) -> p a b", b=P)).then_inc(w_ready, 1)
            for n in range(8):
                act.wait_ge(k_mm, n + 1)
                nc.scalar.copy(Ksb[0:16, n % 2, 4 * (n // 2):4 * (n // 2) + 4, :], PS[0:16, n, :].rearrange("p (a b) -> p a b", b=P)).then_inc(k_ready, 1)
            for i in range(NT):
                act.wait_ge(lat_mm, i + 1)
                if i >= 1:
                    act.wait_ge(lat_ready, i)
                nc.scalar.activation(squares[:, 0:256], PS[:, i % 2, 0:256], ACT.Square, accum_out=ss[:, i, 0:1])
                nc.scalar.activation(squares[:, 256:384], PS[:, i % 2, 256:384], ACT.Square, accum_out=ss[:, i, 1:2])
                nc.scalar.copy(lat[:, i, :], PS[:, i % 2, 0:448]).then_inc(lat_ready, 1)
            for q in range(4):
                act.wait_ge(y_ready, 2 * q + 2)
                nc.scalar.activation(yg[:, :, q * P:(q + 1) * P].rearrange("p t (g c) -> p g t c", c=16), xs[:, 8 * q:8 * q + 8, :, :],
                                     ACT.Gelu_apprx_tanh).then_inc(gelu_done, 1)

        @block.vector
        def _(dve):
            chain = Count(order)

            def link(ins, signal=chain):
                signal.by(ins)
                dve.wait_ge(signal.sem, signal.n)

            def tt(out, a, b, op, signal=chain):
                link(nc.vector.tensor_tensor(out, a, b, op), signal)

            dve.wait_ge(dt_in, 16)
            nc.vector.tensor_copy(v["dt"][0:64, :], ldt[0:64, 0:32:2])
            link(nc.vector.tensor_copy(v["dt"][64:128, :], ldt[64:128, 1:32:2]), Count(dt_ready))
            dve.wait_ge(aorder, 1)
            tt(v["magarg"], v["dt"], are, ALU.mult)
            tt(v["arg"], v["dt"], aim, ALU.mult)
            link(nc.vector.tensor_scalar(v["arg2"], v["arg"], float(TC), None, ALU.mult))
            for n, (src, quarter) in enumerate(((v["arg"], 0.0), (v["arg"], 0.25), (v["arg2"], 0.0), (v["arg2"], 0.25))):
                reduced_sine_argument(nc, link, args[:, n, :], src, v["kk"], quarter)
            link(nc.vector.memset(v["ta"], 0.0), Count(arg_ready))
            dve.wait_ge(trig_ready, 1)
            sn, cs = trig[:, 0, :], trig[:, 1, :]
            tt(v["abre"], v["mag"], cs, ALU.mult)
            tt(v["abim"], v["mag"], sn, ALU.mult)
            tt(v["den"], are, are, ALU.mult)
            tt(v["ta"], aim, aim, ALU.mult)
            tt(v["den"], v["den"], v["ta"], ALU.add)
            link(nc.vector.reciprocal(v["den"], v["den"]))
            link(nc.vector.tensor_scalar(v["nr"], v["abre"], 1.0, None, ALU.subtract))
            tt(v["ta"], v["nr"], are, ALU.mult)
            tt(v["tb"], v["abim"], aim, ALU.mult)
            tt(v["kre"], v["ta"], v["tb"], ALU.add)
            tt(v["kre"], v["kre"], v["den"], ALU.mult)
            tt(v["ta"], v["abim"], are, ALU.mult)
            tt(v["tb"], v["nr"], aim, ALU.mult)
            tt(v["kim"], v["ta"], v["tb"], ALU.subtract)
            tt(v["kim"], v["kim"], v["den"], ALU.mult)

            def complex_product(out_r, out_i, ar, ai, br, bi, t, negate_imaginary=False, signal=chain):
                tt(out_r, ar, br, ALU.mult)
                tt(t, ai, bi, ALU.mult)
                tt(out_r, out_r, t, ALU.subtract)
                tt(out_i, ar, bi, ALU.mult)
                tt(t, ai, br, ALU.mult)
                if negate_imaginary:
                    link(nc.vector.scalar_tensor_tensor(out_i, out_i, -1.0, t, ALU.mult, ALU.subtract), signal)
                else:
                    tt(out_i, out_i, t, ALU.add, signal)

            small = K.at(S5TMP + 512, 16, 16)
            dve.wait_ge(b_in, 32)
            complex_product(kB[:, 0, :, :], kB[:, 1, :, :], braw[:, 0, :, :], braw[:, 1, :, :], over_c(v["kre"]), over_c(v["kim"]), small)
            link(nc.vector.memset(pw[:, 0, 0, :], 1.0))
            link(nc.vector.memset(pw[:, 1, 0, :], 0.0))
            link(nc.vector.tensor_copy(pw[:, 0, 1, :], v["abre"]))
            link(nc.vector.tensor_copy(pw[:, 1, 1, :], v["abim"]))
            n = 1
            while n < TC:
                last_power = lambda ri: pw[:, ri, n:n + 1, :].to_broadcast([P, n, 16])
                complex_product(pw[:, 0, n + 1:2 * n + 1, :], pw[:, 1, n + 1:2 * n + 1, :], pw[:, 0, 1:n + 1, :], pw[:, 1, 1:n + 1, :],
                                last_power(0), last_power(1), small[:, 0:n, :])
                n *= 2
            for ri in range(2):
                for t in range(TC):
                    chain.by(nc.vector.tensor_copy(rev[:, ri, t, :], pw[:, ri, TC - 1 - t, :]))
            dve.wait_ge(order, chain.n)
            by_jsc = lambda a: a.rearrange("p m j -> p j m").unsqueeze(3).to_broadcast([P, 16, 8, 16])
            over_s = lambda a: a.unsqueeze(2).to_broadcast([P, 16, 8, 16])
            whole = K.at(S5TMP, 16, 8, 16)
            complex_product(WTr, WTi, over_s(kB[:, 0, :, :]), over_s(kB[:, 1, :, :]), by_jsc(rev[:, 0, :, :]), by_jsc(rev[:, 1, :, :]), whole,
                            signal=Count(wt_ready))
            dve.wait_ge(c_tr, 1)
            for ri in range(2):
                src = PS[:, 6 + ri, :].rearrange("p (j g c) -> p j g c", g=2, c=16)
                chain.by(nc.vector.tensor_copy(C[0:64, ri, :, :], src[0:64, :, 0, :]))
                last = nc.vector.tensor_copy(C[64:128, ri, :, :], src[64:128, :, 1, :])
                if ri == 1:
                    link(last, Count(c_ready))
            for j0 in (0, 8):
                js = slice(j0, j0 + 8)
                over_m = lambda a: a.unsqueeze(2).to_broadcast([P, 8, 9, 16])
                by_jmc = lambda a: a.rearrange("p m j -> p j m")[:, js, :].unsqueeze(3).to_broadcast([P, 8, 9, 16])
                complex_product(QR[:, js, :, :], QN[:, js, :, :], over_m(C[:, 0, js, :]), over_m(C[:, 1, js, :]),
                                by_jmc(pw[:, 0, :, :]), by_jmc(pw[:, 1, :, :]), K.at(S5TMP, 8, 9, 16), negate_imaginary=True,
                                signal=chain if j0 == 0 else Count(kb_ready))
            link(nc.vector.tensor_copy(Ts[:, :, 0], trig[:, 2, :]))
            link(nc.vector.tensor_copy(Tc[:, :, 0], trig[:, 3, :]))
            n = 1
            while n < NCH:
                last_power = lambda a: a[:, :, n - 1:n].to_broadcast([P, 16, n])
                complex_product(Tc[:, :, n:2 * n], Ts[:, :, n:2 * n], Tc[:, :, 0:n], Ts[:, :, 0:n], last_power(Tc), last_power(Ts),
                                K.at(S5TMP, 16, n))
                n *= 2
            dve.wait_ge(u_tr, 8)
            dve.wait_ge(ds_in, 16)
            link(nc.vector.tensor_tensor(xs, xs, dskip.rearrange("p (g c) -> p g c", c=16).unsqueeze(2).to_broadcast([P, 32, TC, 16]), ALU.mult))
            dve.wait_ge(toeplitz, 16 * TC)
            for q in range(4):
                js = slice(4 * q, 4 * q + 4)
                dve.wait_ge(v_mm, 2 * q + 2)
                vr, vi = (PS[:, 2 * q + ri, :].rearrange("p (a b) -> p a b", b=NCH) for ri in range(2))
                c, sn_ = Tc[:, js, :], Ts[:, js, :]
                for n, (a, b) in enumerate(((vr, c), (vi, sn_), (vi, c), (vr, sn_))):
                    ins = nc.vector.tensor_tensor(tmp[:, n, :, :], a, b, ALU.mult)
                    if n < 3:
                        chain.by(ins)
                    else:
                        ins.then_inc(v_read, 1)
                dve.wait_ge(v_read, q + 1)
                tt(tmp[:, 0, :, :], tmp[:, 0, :, :], tmp[:, 1, :, :], ALU.add)
                tt(tmp[:, 2, :, :], tmp[:, 2, :, :], tmp[:, 3, :, :], ALU.subtract)
                for ri in range(2):
                    for i in range(4):
                        j = 4 * q + i
                        chain.by(nc.vector.tensor_tensor_scan(G[ri][:, j, :], v["rho"][:, j:j + 1].to_broadcast([P, NCH]), tmp[:, 2 * ri, i, :], 0.0,
                                                              ALU.mult, ALU.add))
                dve.wait_ge(order, chain.n)
                gr, gi = G[0][:, js, 0:NCH - 1], G[1][:, js, 0:NCH - 1]
                c, sn_ = Tc[:, js, 0:NCH - 1], Ts[:, js, 0:NCH - 1]
                for n, (a, b) in enumerate(((gr, c), (gi, sn_), (gi, c), (gr, sn_))):
                    chain.by(nc.vector.tensor_tensor(tmp[:, n, :, 0:NCH - 1], a, b, ALU.mult))
                dve.wait_ge(order, chain.n)
                chain.by(nc.vector.tensor_tensor(G[0][:, js, 1:NCH], tmp[:, 0, :, 0:NCH - 1], tmp[:, 1, :, 0:NCH - 1], ALU.subtract))
                chain.by(nc.vector.tensor_tensor(G[1][:, js, 1:NCH], tmp[:, 2, :, 0:NCH - 1], tmp[:, 3, :, 0:NCH - 1], ALU.add))
                chain.by(nc.vector.memset(G[0][:, js, 0:1], 0.0))
                nc.vector.memset(G[1][:, js, 0:1], 0.0).then_inc(h_ready, 1)
                dve.wait_ge(h_ready, q + 1)
            for n in range(8):
                q, g2 = n // 2, n % 2
                dve.wait_ge(y_mm, n + 1)
                for i in range(4):
                    g = 2 * (4 * q + i) + g2
                    dst = xs[:, g, :, :]
                    src = PS[:, n, i * P:(i + 1) * P].rearrange("p (t c) -> p t c", c=16)
                    last = nc.vector.tensor_tensor(dst, dst, src, ALU.add)
                last.then_inc(y_ready, 1)


CQT, CKVT, KRT, YMT = VECS, VECS + 2048, VECS + 3072, VECS + 4096
ROPE = VECS + 8192
YG, YGT, YST, GMT, SECW = 28032, 32128, 36224, 40320, 44416
RMS_EPS = 1e-6


def project_second(K):
    nc, io, PS = K.nc, K.io, K.PS
    ident, cols2, x2T = K.at(IDENT, P), K.at(COLS2, 64), K.at(X2T, KT, S)
    cqT, ckvT, krT = K.at(CQT, 2, S), K.at(CKVT, S), K.at(KRT, S)
    lat = K.at(LAT, NT, 448)
    cos, sin = K.at(ROPE, NT, 32), K.at(ROPE + 256, NT, 32)
    kr2 = K.at(ROPE + 512, NT, P)
    o = ROPE + 1536
    ss = K.at(LATS, NT, 2)
    rinv, posr, posf, pcol = K.at(o + 16, NT, 2), K.at(o + 32, P), K.at(o + 160, P), K.at(o + 288, NT)
    invf = K.at(o + 296, 32)
    assert o + 328 <= X2T
    yg, ygT, ysT, gmT = K.at(YG, TC, CH), K.at(YGT, 4, S), K.at(YST, 4, S), K.at(GMT, 4, S)
    sg = K.at(YG, 2, 512)
    ang, kk = K.at(YG + 1024, NT, 32), K.at(YG + 1280, NT, 32)
    red, t1, t2 = K.at(YG + 1792, NT, 32), K.at(YG + 2048, NT, 32), K.at(YG + 2304, NT, 32)
    w_slots, wglu = K.at(SECW, 2, KT * P), K.at(SECW + 2 * KT * P, 4, CH)
    o = SECW + 2 * KT * P + 4 * CH
    w_parts = [(K.part(f"p2_w{j}_hi", o + j * KT * P, KT * P), K.part(f"p2_w{j}_rest", SECW + j * KT * P, KT * P)) for j in range(2)]
    o += 2 * KT * P
    assert LATW + 3 * S <= LAT and YG + 2560 + S <= YGT
    places = [LATW, LATW + S, LATW + 2 * S, YMT, YMT + S, YMT + 2 * S, o, YG + 2560]
    x_parts = [(K.part(f"p2_x{k}_hi", place, S), K.part(f"p2_x{k}_rest", X2T + k * S, S)) for k, place in enumerate(places)]
    w = io["w_in_2"][0].rearrange("(k p) n -> p k n", p=P)
    col_of = lambda T: CH + T * P if T < 4 else 2 * CH + 448 + (T - 4) * P
    with ExitStack() as ctx:
        s = lambda n: K.sem("p2_" + n)
        glu_in, w_in, small_in, order = s("glu_in"), [s("w_in0"), s("w_in1")], s("small_in"), s("order")
        y_tr, y_taken, proj_mm, proj_ready, pos_ready, pos_tr = (s(n) for n in ("y_tr", "y_taken", "proj_mm", "proj", "posf", "pos_tr"))
        glu_mm, glu_sig, ys_ready, pos_taken, arg_ready, trig_ready, ms_ready, rms_ready = (s(n) for n in ("glu_mm", "glu_sig", "ys", "pos_taken", "arg", "trig", "ms", "rms"))
        rows_ready, l_tr, l_taken, sig_used = s("rows"), s("l_tr"), s("l_taken"), s("sig_used")
        x_hi, x_rest, w_hi, w_rest = s("x_hi"), s("x_rest"), s("w_hi"), s("w_rest")
        block = ctx.enter_context(nc.Block())

        @block.sync
        def _(sp):
            sp.dma_start(posr[0:NT, :].bitcast(i32), io["positions_2"].rearrange("o (i p) -> (o i) p", p=P)).then_inc(small_in, 16)
            sp.dma_start(invf, bcast_rows(io["inv_freq"])).then_inc(small_in, 16)
            for T in range(8):
                if T >= 2:
                    sp.wait_ge(proj_mm, 2 * (T - 1))
                sp.dma_start(w_slots[:, T % 2, :].rearrange("p (k n) -> p k n", n=P), w[:, :, col_of(T):col_of(T) + P]).then_inc(w_in[T % 2], 16)
                if T == 1:
                    sp.dma_start(wglu, io["w_glu_2"][0].rearrange("(k p) n -> p k n", p=P)).then_inc(glu_in, 16)

        @block.gpsimd
        def _(pool):
            for T in range(8):
                pool.wait_ge(w_hi, T + 1)
                hi, lo = w_parts[T % 2]
                nc.gpsimd.tensor_tensor(lo, w_slots[:, T % 2, :], hi.bitcast(fp32), ALU.subtract).then_inc(w_rest, 1)

        @block.tensor
        def _(pe):
            for n in range(8):
                c, h = n // 2, n % 2
                for i in range(4):
                    last = nc.tensor.transpose(PS[:, n, i * P:(i + 1) * P], yg[:, 4 * h + i, c * P:(c + 1) * P], ident)
                last.then_inc(y_tr, 1)
            pe.wait_ge(pos_ready, 1)
            pe.wait_ge(y_taken, 8)
            nc.tensor.transpose(PS[:, 7, 0:NT], posf[0:NT, :], ident[0:NT, 0:NT]).then_inc(pos_tr, 1)
            def project(n):
                T, h = n // 2, n % 2
                pe.wait_ge(w_rest, T + 1)
                if n >= 2:
                    pe.wait_ge(proj_ready, n - 1)
                for k in range(KT):
                    if n == 0:
                        pe.wait_ge(x_rest, k + 1)
                    last = split_product(nc, PS[:, 4 + h, :], tuple(v[:, k * P:(k + 1) * P] for v in w_parts[T % 2]),
                                         tuple(v[:, h * 512:(h + 1) * 512] for v in x_parts[k]), k == 0, k == KT - 1)
                last.then_inc(proj_mm, 1)

            for n in range(8):
                project(n)
            pe.wait_ge(glu_in, 16)
            pe.wait_ge(pos_taken, 1)
            for n in range(8):
                c, h = n // 2, n % 2
                if n >= 2:
                    pe.wait_ge(glu_sig, n - 1)
                for k in range(4):
                    last = nc.tensor.matmul(PS[:, 6 + h, :], wglu[:, k, c * P:(c + 1) * P], ygT[:, k, h * 512:(h + 1) * 512], start=(k == 0), stop=(k == 3))
                last.then_inc(glu_mm, 1)
                project(8 + n)
            pe.wait_ge(rows_ready, 1)
            for n in range(8):
                c, h = n // 2, n % 2
                if n >= 4:
                    pe.wait_ge(l_taken, n - 3)
                for i in range(4):
                    src = lat[:, 4 * h + i, c * P:(c + 1) * P] if c < 3 else kr2[:, 4 * h + i, :]
                    last = nc.tensor.transpose(PS[:, n % 4, i * P:(i + 1) * P], src, ident)
                last.then_inc(l_tr, 1)

        @block.scalar
        def _(act):
            for n in range(8):
                c, h = n // 2, n % 2
                act.wait_ge(y_tr, n + 1)
                dst = ygT[:, c, :].rearrange("p (n t) -> p t n", t=TC)[:, 4 * h:4 * h + 4, :]
                nc.scalar.copy(dst, PS[:, n, :].rearrange("p (a b) -> p a b", b=P)).then_inc(y_taken, 1)
            def round_weights(T):
                act.wait_ge(w_in[T % 2], 16 * (T // 2 + 1))
                nc.scalar.copy(w_parts[T % 2][0], w_slots[:, T % 2, :]).then_inc(w_hi, 1)

            round_weights(0)
            for k in range(KT):
                nc.scalar.copy(x_parts[k][0], x2T[:, k, :]).then_inc(x_hi, 1)
            round_weights(1)

            def take_projection(n):
                T, h = n // 2, n % 2
                if h == 0 and 1 <= T < 7:
                    round_weights(T + 1)
                act.wait_ge(proj_mm, n + 1)
                dst = (ysT if T < 4 else gmT)[:, T % 4, h * 512:(h + 1) * 512]
                nc.scalar.activation(dst, PS[:, 4 + h, :], ACT.Silu).then_inc(proj_ready, 1)

            for n in range(8):
                take_projection(n)
            act.wait_ge(arg_ready, 1)
            nc.scalar.activation(sin, red, ACT.Sin).then_inc(trig_ready, 1)
            act.wait_ge(arg_ready, 2)
            nc.scalar.activation(cos, red, ACT.Sin).then_inc(trig_ready, 1)
            act.wait_ge(ms_ready, 1)
            nc.scalar.activation(rinv, rinv, ACT.Sqrt).then_inc(rms_ready, 1)
            for n in range(8):
                c, h = n // 2, n % 2
                act.wait_ge(glu_mm, n + 1)
                if n >= 2:
                    act.wait_ge(ys_ready, n - 1)
                nc.scalar.activation(sg[:, n % 2, :], PS[:, 6 + h, :], ACT.Sigmoid, bias=cols2[:, 32 + c:33 + c]).then_inc(glu_sig, 1)
                take_projection(8 + n)
            for n in range(8):
                c, h = n // 2, n % 2
                act.wait_ge(l_tr, n + 1)
                dst = (cqT[:, c, :] if c < 2 else ckvT if c == 2 else krT)[:, h * 512:(h + 1) * 512]
                scale = cols2[:, 36 + c:37 + c] if c < 3 else 1.0
                nc.scalar.activation(dst, PS[:, n % 4, :], ACT.Copy, scale=scale).then_inc(l_taken, 1)

        @block.vector
        def _(dve):
            chain = Count(order)

            def link(ins, signal=chain):
                signal.by(ins)
                dve.wait_ge(signal.sem, signal.n)

            def tt(out, a, b, op, signal=chain):
                link(nc.vector.tensor_tensor(out, a, b, op), signal)

            args = Count(arg_ready)
            dve.wait_ge(small_in, 32)
            link(nc.vector.tensor_copy(posf[0:NT, :], posr[0:NT, :].bitcast(i32)), Count(pos_ready))
            dve.wait_ge(pos_tr, 1)
            link(nc.vector.tensor_copy(pcol, PS[:, 7, 0:NT]), Count(pos_taken))
            dve.wait_ge(y_tr, 8)
            for k in range(KT):
                hi, lo = x_parts[k]
                dve.wait_ge(x_hi, k + 1)
                nc.vector.tensor_tensor(lo, x2T[:, k, :], hi.bitcast(fp32), ALU.subtract).then_inc(x_rest, 1)
            tt(ang, pcol.unsqueeze(2).to_broadcast([P, NT, 32]), invf.unsqueeze(1).to_broadcast([P, NT, 32]), ALU.mult)
            reduced_sine_argument(nc, link, red, ang, kk)
            link(nc.vector.memset(t1[:, 0, 0:1], 0.0), args)
            dve.wait_ge(trig_ready, 1)
            reduced_sine_argument(nc, link, red, ang, kk, 0.25)
            link(nc.vector.memset(t1[:, 0, 0:1], 0.0), args)
            dve.wait_ge(trig_ready, 2)
            for n, width in enumerate((256, 128)):
                link(nc.vector.tensor_scalar(rinv[:, :, n], ss[:, :, n], 1 / width, RMS_EPS, ALU.mult, ALU.add), chain if n == 0 else Count(ms_ready))
            k1, k2 = lat[:, :, 384:416], lat[:, :, 416:448]
            for out, a, b, op in ((0, cos, sin, ALU.subtract), (32, sin, cos, ALU.add)):
                tt(t1, k1, a, ALU.mult)
                tt(t2, k2, b, ALU.mult)
                tt(kr2[:, :, out:out + 32], t1, t2, op)
            link(nc.vector.tensor_copy(kr2[:, :, 64:128], kr2[:, :, 0:64]))
            dve.wait_ge(rms_ready, 1)
            link(nc.vector.reciprocal(rinv, rinv))
            for n, (a, b) in enumerate(((0, 256), (256, 384))):
                tt(lat[:, :, a:b], lat[:, :, a:b], rinv[:, :, n:n + 1].to_broadcast([P, NT, b - a]), ALU.mult,
                   chain if n == 0 else Count(rows_ready))
            for n in range(8):
                c, h = n // 2, n % 2
                dve.wait_ge(proj_ready, n + 1)
                d, y = ysT[:, c, h * 512:(h + 1) * 512], ygT[:, c, h * 512:(h + 1) * 512]
                tt(d, d, y, ALU.mult)
                dve.wait_ge(glu_sig, n + 1)
                nc.vector.tensor_tensor(d, d, sg[:, n % 2, :], ALU.mult).then_inc(ys_ready, 1)


MLA_HEADS, ROPE_D = 4, 64
QK_SCALE = 192 ** -0.5


def latent_attention(K):
    nc, io, PS = K.nc, K.io, K.PS
    ident = K.at(IDENT, P)
    cqT, ckvT, krT, ymT, gmT = K.at(CQT, 2, S), K.at(CKVT, S), K.at(KRT, S), K.at(YMT, 4, S), K.at(GMT, 4, S)
    cos, sin = K.at(ROPE, NT, 32), K.at(ROPE + 256, NT, 32)
    knT, qnT = K.at(X2T, 4, S), K.at(X2T + 4096, 4, S)
    vr = K.at(YG, NT, CH)
    wuq, wukv = K.at(YG + 4096, 2, 4, 192), K.at(YG + 4096 + 1536, 4, 256)
    causal = K.at(YG + 4096 + 2560, S)
    qrT = K.at(SECW, 2, S)
    sb, pt = K.at(SECW + 2048, 2, S), K.at(SECW + 4096, 2, S)
    orow = K.at(SECW + 6144, NT, P)
    rope_rows = K.at(SECW + 2048, NT, 4, 64)
    t1, t2 = K.at(SECW + 4096, 4, 32), K.at(SECW + 4096 + P, 4, 32)
    o = SECW + 7168
    mx, nm, l, rl = K.at(o, 32), K.at(o + 32, 32), K.at(o + 64, 32), K.at(o + 96, 32)
    units = [(h, i) for h in range(MLA_HEADS) for i in range(NT)]
    t_jobs, first_job, out_job = [], {}, {}
    for step in range(len(units) + 2):
        if 1 <= step <= len(units):
            h, i = units[step - 1]
            first_job[step - 1] = len(t_jobs)
            t_jobs += [("p", step - 1, b0, min(b0 + 4, i + 1)) for b0 in range(0, i + 1, 4)]
        if step >= 2 and units[step - 2][1] == NT - 1:
            h = units[step - 2][0]
            out_job[h] = len(t_jobs)
            t_jobs += [("o", h, 0, 4), ("o", h, 4, 8)]
    after_unit = lambda u: first_job[u] + (units[u][1] + 4) // 4
    with ExitStack() as ctx:
        s = lambda n: K.sem("ml_" + n)
        wout_in = s("wout_in")
        w_in, causal_in, order = s("w_in"), s("causal_in"), s("order")
        up_mm, up_ready, r_mm, r_ready, rt, rt_ready = s("up_mm"), s("up"), s("r_mm"), s("r"), s("rt"), s("rt_ready")
        s_done, s_taken, nm_ready, exp_done, t_done, t_taken, pv_done, o_ready, rl_ready = (s(n) for n in ("s", "s_taken", "nm", "exp", "t", "t_taken", "pv", "o", "rl"))
        block = ctx.enter_context(nc.Block())

        @block.sync
        def _(sp):
            sp.dma_start(wuq, io["w_uq_2"][0].rearrange("(k p) (h n) -> p k h n", p=P, h=4)).then_inc(w_in, 16)
            sp.dma_start(wukv, io["w_ukv_2"][0].rearrange("p (h n) -> p h n", h=4)).then_inc(w_in, 16)
            sp.dma_start(causal, io["causal"]).then_inc(causal_in, 16)
            sp.dma_start(K.at(X2R, KT, D), io["w_out_2"][0].rearrange("(k p) n -> p k n", p=P)).then_inc(wout_in, 16)
            sp.wait_ge(wout_in, 16)

        @block.tensor
        def _(pe):
            pe.wait_ge(w_in, 32)
            for i in range(NT):
                if i >= 4:
                    pe.wait_ge(r_ready, i - 3)
                for c in range(2):
                    last = nc.tensor.matmul(PS[:, 4 + i % 4, 0:256], cqT[:, c, i * P:(i + 1) * P], wuq[:, c, :, 128:192], start=(c == 0), stop=(c == 1))
                last.then_inc(r_mm, 1)
            for n in range(24):
                kind, a, h = n // 8, (n % 8) // 2, n % 2
                if n >= 4:
                    pe.wait_ge(up_ready, n - 3)
                out = PS[:, n % 4, :]
                if kind == 0:
                    for c in range(2):
                        last = nc.tensor.matmul(out, wuq[:, c, a, 0:128], cqT[:, c, h * 512:(h + 1) * 512], start=(c == 0), stop=(c == 1))
                elif kind == 1:
                    last = nc.tensor.matmul(out, wukv[:, a, 0:128], ckvT[:, h * 512:(h + 1) * 512], start=True, stop=True)
                else:
                    last = nc.tensor.matmul(out, ckvT[:, (n % 8) * P:(n % 8 + 1) * P], wukv[:, :, 128:256], start=True, stop=True)
                last.then_inc(up_mm, 1)
            pe.wait_ge(r_ready, NT)
            for n in range(4):
                pair, h = n // 2, n % 2
                for i in range(4):
                    last = nc.tensor.transpose(PS[:, 4 + n, i * P:(i + 1) * P], rope_rows[:, 4 * h + i, 2 * pair:2 * pair + 2, :], ident)
                last.then_inc(rt, 1)
            pe.wait_ge(up_ready, 24)
            pe.wait_ge(rt_ready, 4)

            def scores(u):
                h, i = units[u]
                if u >= 2:
                    pe.wait_ge(s_taken, u - 1)
                half = slice(64 * (h % 2), 64 * (h % 2) + 64)
                n = (i + 1) * P
                for c in range(0, n, 512):
                    e = min(n, c + 512)
                    out = PS[:, 2 * (u % 2) + c // 512, 0:e - c]
                    nc.tensor.matmul(out, qnT[:, h, i * P:(i + 1) * P], knT[:, h, c:e], start=True, stop=False)
                    last = nc.tensor.matmul(out, qrT[half, h // 2, i * P:(i + 1) * P], krT[half, c:e], start=False, stop=True)
                last.then_inc(s_done, 1)

            def transposes(g):
                kind, which, b0, b1 = t_jobs[g]
                if g >= 2:
                    pe.wait_ge(t_taken, g - 1)
                for b in range(b0, b1):
                    src = sb[:, which % 2, b * P:(b + 1) * P] if kind == "p" else orow[:, b, :]
                    last = nc.tensor.transpose(PS[:, 4 + g % 2, (b - b0) * P:(b - b0 + 1) * P], src, ident)
                last.then_inc(t_done, 1)

            for step in range(len(units) + 2):
                if step < len(units):
                    scores(step)
                if 1 <= step <= len(units):
                    u = step - 1
                    pe.wait_ge(exp_done, u + 1)
                    for g in range(first_job[u], after_unit(u)):
                        transposes(g)
                if step >= 2:
                    u = step - 2
                    h, i = units[u]
                    pe.wait_ge(t_taken, after_unit(u))
                    if u >= 2:
                        pe.wait_ge(o_ready, u - 1)
                    for b in range(i + 1):
                        last = nc.tensor.matmul(PS[:, 6 + u % 2, 0:P], pt[:, u % 2, b * P:(b + 1) * P], vr[:, b, h * P:(h + 1) * P],
                                                start=(b == 0), stop=(b == i))
                    last.then_inc(pv_done, 1)
                    if i == NT - 1:
                        pe.wait_ge(o_ready, u + 1)
                        for g in range(out_job[h], out_job[h] + 2):
                            transposes(g)

        @block.scalar
        def _(act):
            for n in range(24):
                kind, a, h = n // 8, (n % 8) // 2, n % 2
                act.wait_ge(up_mm, n + 1)
                dst = vr[:, n % 8, :] if kind == 2 else (qnT, knT)[kind][:, a, h * 512:(h + 1) * 512]
                nc.scalar.copy(dst, PS[:, n % 4, :]).then_inc(up_ready, 1)
            for step in range(len(units) + 2):
                if step < len(units):
                    h, i = units[step]
                    n = (i + 1) * P
                    act.wait_ge(nm_ready, step + 1)
                    nc.scalar.activation(sb[:, step % 2, 0:n], sb[:, step % 2, 0:n], ACT.Exp, bias=nm[:, step:step + 1], scale=QK_SCALE,
                                         accum_out=l[:, step:step + 1]).then_inc(exp_done, 1)
                if step >= 2:
                    u = step - 2
                    h, i = units[u]
                    act.wait_ge(pv_done, u + 1)
                    act.wait_ge(rl_ready, u + 1)
                    if h >= 1:
                        act.wait_ge(t_done, out_job[h - 1] + 2)
                    nc.scalar.activation(orow[:, i, :], PS[:, 6 + u % 2, 0:P], ACT.Copy, scale=rl[:, u:u + 1]).then_inc(o_ready, 1)

        @block.vector
        def _(dve):
            chain = Count(order)

            def link(ins, signal=chain):
                signal.by(ins)
                dve.wait_ge(signal.sem, signal.n)

            for i in range(NT):
                dve.wait_ge(r_mm, i + 1)
                x = PS[:, 4 + i % 4, 0:256].rearrange("p (h e) -> p h e", h=4)
                c, sn = (a[:, i, :].unsqueeze(1).to_broadcast([P, 4, 32]) for a in (cos, sin))
                for out, a, b, op in ((0, c, sn, ALU.subtract), (32, sn, c, ALU.add)):
                    link(nc.vector.tensor_tensor(t1, x[:, :, 0:32], a, ALU.mult))
                    link(nc.vector.tensor_tensor(t2, x[:, :, 32:64], b, ALU.mult))
                    ins = nc.vector.tensor_tensor(rope_rows[:, i, :, out:out + 32], t1, t2, op)
                    if out:
                        ins.then_inc(r_ready, 1)
                        dve.wait_ge(r_ready, i + 1)
                    else:
                        link(ins)
            for n in range(4):
                dve.wait_ge(rt, n + 1)
                nc.vector.tensor_copy(qrT[:, n // 2, (n % 2) * 512:(n % 2 + 1) * 512], PS[:, 4 + n, :]).then_inc(rt_ready, 1)
            dve.wait_ge(causal_in, 16)

            def take(g, dst, gate=None):
                dve.wait_ge(t_done, g + 1)
                src = PS[:, 4 + g % 2, 0:dst.shape[1]]
                if gate is None:
                    nc.vector.tensor_copy(dst, src).then_inc(t_taken, 1)
                else:
                    nc.vector.tensor_tensor(dst, src, gate, ALU.mult).then_inc(t_taken, 1)

            for step in range(len(units) + 2):
                if step < len(units):
                    h, i = units[step]
                    n = (i + 1) * P
                    dve.wait_ge(s_done, step + 1)
                    if step >= 2:
                        dve.wait_ge(t_done, after_unit(step - 2))
                    src = PS[:, 2 * (step % 2):2 * (step % 2) + 2, :].rearrange("p a b -> p (a b)")[:, 0:n]
                    nc.vector.tensor_tensor_reduce(out=sb[:, step % 2, 0:n], in0=src, in1=causal[:, S - n:S], scale=1.0, scalar=-3e38,
                                                   op0=ALU.add, op1=ALU.max, accum_out=mx[:, step:step + 1]).then_inc(s_taken, 1)
                    dve.wait_ge(s_taken, step + 1)
                    nc.vector.tensor_scalar(nm[:, step:step + 1], mx[:, step:step + 1], -QK_SCALE, None, ALU.mult).then_inc(nm_ready, 1)
                if 1 <= step <= len(units):
                    u = step - 1
                    if u >= 2:
                        dve.wait_ge(pv_done, u - 1)
                    for g in range(first_job[u], after_unit(u)):
                        _, _, b0, b1 = t_jobs[g]
                        take(g, pt[:, u % 2, b0 * P:b1 * P])
                    dve.wait_ge(exp_done, u + 1)
                    nc.vector.reciprocal(rl[:, u:u + 1], l[:, u:u + 1]).then_inc(rl_ready, 1)
                if step >= 2 and units[step - 2][1] == NT - 1:
                    h = units[step - 2][0]
                    for n, g in enumerate(range(out_job[h], out_job[h] + 2)):
                        take(g, ymT[:, h, n * 512:(n + 1) * 512], gmT[:, h, n * 512:(n + 1) * 512])


def second_output(K):
    nc, io, PS = K.nc, K.io, K.PS
    ident = K.at(IDENT, P)
    x2r = K.at(X2T, NT, D)
    sources = [YST, YST + 2 * S, YMT, YMT + 2 * S]
    raw = [(K.at(place, 2, S), K.at(X2R + 2 * D * i, 2, D)) for i, place in enumerate(sources)]
    y_parts = [(K.part(f"so_y{i}_hi", GMT + 2 * S * i, 2, S), K.part(f"so_y{i}_rest", place, 2, S)) for i, place in enumerate(sources)]
    o_parts = [(K.part(f"so_o{i}_hi", YG + 2 * D * i, 2, D), K.part(f"so_o{i}_rest", X2R + 2 * D * i, 2, D)) for i in range(4)]
    o = GMT + 4 * 2 * S
    places = [o + D * i for i in range(3)] + [VECS + D * i for i in range(4)] + [ROPE]
    assert o + 3 * D <= ARENA and VECS + 4 * D <= YMT and YST + 4 * S <= GMT
    wpg = [K.at(place, D) for place in places]
    g_parts = [(K.part(f"so_g{k}_hi", YG + D * k, D), K.part(f"so_g{k}_rest", place, D)) for k, place in enumerate(places)]
    stat = K.at(ROPE + D, 16)
    prow, pT, wpp, vec = K.at(X2R, NT, 256), K.at(X2R + 2048, 2, NT, P), K.at(X2R + 4096, 2, D), K.at(X2R + 6144, 2, D)
    u_parts = [(K.part(f"so_u{j}_hi", YST + 2 * D * j, D), K.part(f"so_u{j}_rest", YST + 2 * D * j + D, D)) for j in range(2)]
    sg = K.at(GMT, 2, D)
    out_class = io["out"][0].rearrange("(n r) d -> n r d", r=8)
    flat = lambda banks: banks.rearrange("p a b -> p (a b)")
    with ExitStack() as ctx:
        s = lambda n: K.sem("so_" + n)
        wpp_in, p_in, vec_in, order, hi_ready, rest_ready, g_hi, g_rest = (s(n) for n in ("wpp_in", "p_in", "vec_in", "order", "hi", "rest", "g_hi", "g_rest"))
        p_tr, p_taken, mix, u_ready, ut, u_hi, u_rest, pg, pp, sig, pp_used, var, std, row_ready = (s(n) for n in (
            "p_tr", "p_taken", "mix", "u", "ut", "u_hi", "u_rest", "pg", "pp", "sig", "pp_used", "var", "std", "row"))
        row_in, wpg_in = [s(f"row_in{r}") for r in range(NT)], [s(f"wpg_in{k}") for k in range(KT)]
        block = ctx.enter_context(nc.Block())

        @block.gpsimd
        def _(pool):
            for r in range(NT):
                pool.dma_start(x2r[:, r, :], K.x2_rows[:, r * D:(r + 1) * D]).then_inc(row_in[r], 16)

        @block.sync
        def _(sp):
            for k in range(KT):
                sp.dma_start(wpg[k], io["w_pg_2"][0, k * P:(k + 1) * P, :]).then_inc(wpg_in[k], 16)
            sp.wait_ge(mix, NT)
            sp.dma_start(prow, io["p_2"][0, 0].rearrange("(n r) e -> n r e", r=8)).then_inc(p_in, 16)
            sp.dma_start(wpp, io["w_pp_2"][0].rearrange("(k p) n -> p k n", p=P)).then_inc(wpp_in, 16)
            for n, name in enumerate(("ln_g_2", "ln_b_2")):
                sp.dma_start(vec[:, n, :], bcast_rows(io[name][0])).then_inc(vec_in, 16)
            for r in range(NT):
                sp.wait_ge(row_ready, r + 1)
                sp.dma_start(out_class[:, r, :], x2r[:, r, :]).then_inc(K.out_done, 16)
            sp.wait_ge(K.out_done, 16 * NT)

        @block.tensor
        def _(pe):
            def mixed(r, k, h):
                return split_product(nc, PS[:, 2 * (r % 4) + h, :], tuple(v[:, k % 2, r:S:8] for v in y_parts[k // 2]),
                                     tuple(v[:, k % 2, h * 512:(h + 1) * 512] for v in o_parts[k // 2]), k == 0, k == KT - 1)

            for k in range(KT):
                if k % 2 == 0:
                    pe.wait_ge(rest_ready, 2 * (k // 2) + 2)
                for r in range(4):
                    for h in range(2):
                        last = mixed(r, k, h)
                    if k == KT - 1:
                        last.then_inc(mix, 1)
            for r in range(4, NT):
                pe.wait_ge(u_ready, r - 3)
                for h in range(2):
                    for k in range(KT):
                        last = mixed(r, k, h)
                last.then_inc(mix, 1)

            def to_columns(r):
                pe.wait_ge(u_ready, 8 if r < 2 else r + 1)
                if r >= 2:
                    pe.wait_ge(u_rest, r - 1)
                for k in range(KT):
                    last = nc.tensor.transpose(PS[:, 2 * (r % 2) + k // 4, k % 4 * P:(k % 4 + 1) * P], x2r[:, r, k * P:(k + 1) * P], ident)
                last.then_inc(ut, 1)

            to_columns(0)
            to_columns(1)
            for r in range(NT):
                if 1 <= r < NT - 1:
                    to_columns(r + 1)
                pe.wait_ge(u_rest, r + 1)
                if r >= 1:
                    pe.wait_ge(sig, r)
                for k in range(KT):
                    if r == 0:
                        pe.wait_ge(g_rest, k + 1)
                    for h in range(2):
                        last = split_product(nc, PS[:, 4 + h, :], tuple(v[:, k * P:(k + 1) * P] for v in u_parts[r % 2]),
                                             tuple(v[:, h * 512:(h + 1) * 512] for v in g_parts[k]), k == 0, k == KT - 1)
                last.then_inc(pg, 1)
                if r == 0:
                    pe.wait_ge(p_in, 16)
                    for n in range(4):
                        k, h = n // 2, n % 2
                        if n >= 2:
                            pe.wait_ge(p_taken, n - 1)
                        for i in range(4):
                            last = nc.tensor.transpose(PS[:, 6 + h, i * P:(i + 1) * P], prow[:, 4 * h + i, k * P:(k + 1) * P], ident)
                        last.then_inc(p_tr, 1)
                    pe.wait_ge(wpp_in, 16)
                    pe.wait_ge(p_taken, 4)
                else:
                    pe.wait_ge(pp_used, r)
                for h in range(2):
                    for k in range(2):
                        last = nc.tensor.matmul(PS[:, 6 + h, :], pT[:, k, r, :], wpp[:, k, h * 512:(h + 1) * 512], start=(k == 0), stop=(k == 1))
                last.then_inc(pp, 1)

        @block.scalar
        def _(act):
            for i in range(4):
                nc.scalar.copy(y_parts[i][0], raw[i][0]).then_inc(hi_ready, 1)
                nc.scalar.copy(o_parts[i][0], raw[i][1]).then_inc(hi_ready, 1)

            def round_columns(r):
                act.wait_ge(ut, r + 1)
                nc.scalar.copy(u_parts[r % 2][0], flat(PS[:, 2 * (r % 2):2 * (r % 2) + 2, :])).then_inc(u_hi, 1)

            act.wait_ge(mix, NT)
            for k in range(KT):
                if k == 1:
                    round_columns(0)
                act.wait_ge(wpg_in[k], 16)
                nc.scalar.copy(g_parts[k][0], wpg[k]).then_inc(g_hi, 1)
            round_columns(1)
            for n in range(4):
                act.wait_ge(p_tr, n + 1)
                nc.scalar.copy(pT[:, n // 2, 4 * (n % 2):4 * (n % 2) + 4, :], PS[:, 6 + n % 2, :].rearrange("p (a b) -> p a b", b=P)).then_inc(p_taken, 1)
            for r in range(NT):
                act.wait_ge(pg, r + 1)
                if r >= 2:
                    act.wait_ge(pp_used, r - 1)
                nc.scalar.activation(sg[:, r % 2, :], flat(PS[:, 4:6, :]), ACT.Sigmoid).then_inc(sig, 1)
                if r + 2 < NT:
                    round_columns(r + 2)
                act.wait_ge(var, r + 1)
                nc.scalar.activation(stat[:, 15:16], stat[:, 14:15], ACT.Sqrt).then_inc(std, 1)

        @block.vector
        def _(dve):
            chain = Count(order)

            def link(ins, signal=chain):
                signal.by(ins)
                dve.wait_ge(signal.sem, signal.n)

            norm = RowNorm(nc, dve, link, stat, Count(var), std)
            u, used, rows = Count(u_ready), Count(pp_used), Count(row_ready)

            for i in range(4):
                for j, (hi, lo) in enumerate((y_parts[i], o_parts[i])):
                    dve.wait_ge(hi_ready, 2 * i + j + 1)
                    nc.vector.tensor_tensor(lo, raw[i][j], hi.bitcast(fp32), ALU.subtract).then_inc(rest_ready, 1)
            for r in range(NT):
                dve.wait_ge(row_in[r], 16)
                dve.wait_ge(mix, r + 1)
                link(nc.vector.scalar_tensor_tensor(x2r[:, r, :], x2r[:, r, :], ALPHA, flat(PS[:, 2 * (r % 4):2 * (r % 4) + 2, :]), ALU.mult, ALU.add), u)

            def rest_of_columns(r):
                hi, lo = u_parts[r % 2]
                dve.wait_ge(u_hi, r + 1)
                nc.vector.tensor_tensor(lo, flat(PS[:, 2 * (r % 2):2 * (r % 2) + 2, :]), hi.bitcast(fp32), ALU.subtract).then_inc(u_rest, 1)

            for k in range(KT):
                if k == 1:
                    rest_of_columns(0)
                hi, lo = g_parts[k]
                dve.wait_ge(g_hi, k + 1)
                nc.vector.tensor_tensor(lo, wpg[k], hi.bitcast(fp32), ALU.subtract).then_inc(g_rest, 1)
            rest_of_columns(1)
            dve.wait_ge(vec_in, 32)
            for r in range(NT):
                dve.wait_ge(sig, r + 1)
                dve.wait_ge(pp, r + 1)
                link(nc.vector.tensor_tensor(sg[:, r % 2, :], flat(PS[:, 6:8, :]), sg[:, r % 2, :], ALU.mult), used)
                link(nc.vector.tensor_tensor(x2r[:, r, :], x2r[:, r, :], sg[:, r % 2, :], ALU.add))
                if r + 2 < NT:
                    rest_of_columns(r + 2)
                norm(x2r[:, r, :], vec[:, 0, :], vec[:, 1, :], rows)


def hybrid_kernel(nc, io):
    K = Kernel(nc, io)
    with K.ctx:
        steps = [lambda: prepare(K),
                 lambda: hyena(K),
                 lambda: dilated_attention(K),
                 lambda: merge_branches(K),
                 lambda: first_output(K),
                 lambda: s5_states(K),
                 lambda: project_second(K),
                 lambda: latent_attention(K),
                 lambda: second_output(K)]
        for step in steps:
            step()
            K.end_phase()


INPUTS = ["x", "c", "w_ada", "b_ada", "w_in", "b_in", "conv_w", "conv_b", "filt_w1", "filt_b1", "filt_w2", "filt_b2",
          "filt_w3", "filt_b3", "filt_w4", "filt_freq", "filt_bias", "w_proj_attn", "w_proj_hyena", "w_out", "b_out",
          "ln_g", "ln_b", "p_2", "positions_2", "ln_emb_g_2", "ln_emb_b_2", "w_in_2", "a_re_2", "a_im_2", "log_dt_2",
          "b_re_2", "b_im_2", "c_re_2", "c_im_2", "d_skip_2", "w_glu_2", "b_glu_2", "q_norm_g_2", "w_uq_2",
          "kv_norm_g_2", "w_ukv_2", "w_out_2", "w_pg_2", "w_pp_2", "ln_g_2", "ln_b_2"]


def kernel(**inputs):
    import concourse.bacc as bacc
    from concourse.bass_utils import run_bass_kernel_spmd as run

    nc = bacc.Bacc("TRN2", target_bir_lowering=False, num_devices=1)
    arrays, io = {}, {}
    for name, value in [(n, inputs[n]) for n in INPUTS] + list(shape_constants().items()):
        a = np.ascontiguousarray(value)
        arrays[f"in_{name}"] = a
        io[name] = nc.dram_tensor(f"in_{name}", a.shape, mybir.dt.from_np(a.dtype), kind="ExternalInput").ap()
    io["out"] = nc.dram_tensor("out_x", (1, S, D), fp32, kind="ExternalOutput").ap()
    hybrid_kernel(nc, io)
    r = run(nc, [arrays], core_ids=[0])
    return r.results[0]["out_x"]
```
